# Optimizing a Trainium2 kernel written in Bass

```python
import jax, jax.numpy as jnp
from jax import lax
import numpy as np

D_MODEL = 1024
BATCH = 1
SEQ = 512
DEPTH = 1

CTX_LEN = 256
GRID_W = 64
N_MOD = 6
NORM_EPS = 1e-6

ML_HEADS = 4
ML_DQK = 64
ML_DV = 128
ML_QK = ML_HEADS * ML_DQK
ML_V = ML_HEADS * ML_DV
ML_CHUNK = 64
GATE_CAP = 15.0
ML_COLS = 2 * ML_QK + 2 * ML_V + 4 * ML_HEADS

RW_HEADS = 8
RW_N = 64
RW_W = RW_HEADS * RW_N
RW_DECAY_LORA = 64
RW_A_LORA = 64
RW_GATE_LORA = 128
RW_GN_EPS = 6.4e-4
RW_COLS = 3 * RW_W + 2 * RW_DECAY_LORA + 2 * RW_A_LORA + RW_GATE_LORA

IN_COLS = ML_COLS + RW_COLS + 2 * D_MODEL

N_EXPERTS = 16
N_GROUPS = 4
EXPERTS_PER_GROUP = N_EXPERTS // N_GROUPS
GROUP_SCORE_TOPK = 2
TOP_K = 2
D_EXPERT = 512

kernel_name = "bidir_mlstm_rwkv7_gated_moe_dit"

def _split(u, sizes):
    idx = [int(i) for i in np.cumsum(sizes)[:-1]]
    return jnp.split(u, idx, axis=-1)

def _rmsnorm(u, g):
    uf = u.astype(jnp.float32)
    y = uf * lax.rsqrt(jnp.mean(uf * uf, axis=-1, keepdims=True) + NORM_EPS)
    return (y * g.astype(jnp.float32)).astype(u.dtype)

def _prev(u):
    return jnp.pad(u[:, :-1], ((0, 0), (1, 0), (0, 0)))

def _next(u):
    return jnp.pad(u[:, 1:], ((0, 0), (0, 1), (0, 0)))

def _grid_conv(u, taps, bias):
    bsz, t, ch = u.shape
    rows = t // GRID_W
    img = u.reshape(bsz, rows, GRID_W, ch)
    out = lax.conv_general_dilated(img, taps[:, :, None, :].astype(u.dtype), (1, 1), "SAME",
                                   dimension_numbers=("NHWC", "HWIO", "NHWC"), feature_group_count=ch)
    return out.reshape(bsz, t, ch) + bias

def _line_conv(u, taps, bias):
    row = taps[1]
    return row[0] * _prev(u) + row[1] * u + row[2] * _next(u) + bias

def _mlstm_zero_state(bsz):
    f32 = jnp.float32
    return (jnp.zeros((bsz, ML_HEADS, ML_DQK, ML_DV), f32), jnp.zeros((bsz, ML_HEADS, ML_DQK), f32),
            jnp.zeros((bsz, ML_HEADS), f32))

def _mlstm_state_update(state, k, v, ig, b):
    C, n, m = state
    g_end = b[..., -1:] - b + ig
    m_new = jnp.maximum(b[..., -1] + m, jnp.max(g_end, axis=-1))
    wk = jnp.exp(g_end - m_new[..., None])
    carry = jnp.exp(b[..., -1] + m - m_new)
    C_new = carry[..., None, None] * C + jnp.einsum("bhsd,bhse->bhde", k * wk[..., None], v)
    n_new = carry[..., None] * n + jnp.einsum("bhs,bhsd->bhd", wk, k)
    return (C_new, n_new, m_new)

def _mlstm_segment(state, q, k, v, ig, lf):
    C, n, m = state
    L = q.shape[2]
    b = jnp.cumsum(lf, axis=-1)
    logw = b[..., :, None] - b[..., None, :] + ig[..., None, :]
    logw = jnp.where(jnp.tril(jnp.ones((L, L), dtype=bool)), logw, -jnp.inf)
    inter = b + m[..., None]
    m_t = jnp.maximum(inter, jnp.max(logw, axis=-1))
    s = jnp.einsum("bhtd,bhsd->bhts", q, k) * jnp.exp(logw - m_t[..., None])
    w_inter = jnp.exp(inter - m_t)
    num = w_inter[..., None] * jnp.einsum("bhtd,bhde->bhte", q, C) + jnp.einsum("bhts,bhse->bhte", s, v)
    den = w_inter * jnp.einsum("bhtd,bhd->bht", q, n) + jnp.sum(s, axis=-1)
    h = num / jnp.maximum(jnp.abs(den), jnp.exp(-m_t))[..., None]
    return _mlstm_state_update(state, k, v, ig, b), h

def _mlstm_run(q, k, v, ig, lf, state, reverse):
    if reverse:
        q, k, v, ig, lf = (jnp.flip(a, axis=2) for a in (q, k, v, ig, lf))
    bsz, nh, t, _ = q.shape
    nc = t // ML_CHUNK

    def chunks(a):
        return jnp.moveaxis(a.reshape(bsz, nh, nc, ML_CHUNK, *a.shape[3:]), 2, 0)

    state, hs = lax.scan(lambda st, xs: _mlstm_segment(st, *xs), state,
                         tuple(chunks(a) for a in (q, k, v, ig, lf)))
    h = jnp.moveaxis(hs, 0, 2).reshape(bsz, nh, t, ML_DV)
    if reverse:
        h = jnp.flip(h, axis=2)
    return state, h

def _mlstm_final_state(k, v, ig, lf, state, reverse):
    if reverse:
        k, v, ig, lf = (jnp.flip(a, axis=2) for a in (k, v, ig, lf))
    return _mlstm_state_update(state, k, v, ig, jnp.cumsum(lf, axis=-1))

def _mlstm_inputs(p, conv, gate_b):
    f32 = jnp.float32
    qk, v, o, gates = _split(p, [2 * ML_QK, ML_V, ML_V, 4 * ML_HEADS])
    q, k = _split(conv(qk), [ML_QK, ML_QK])
    bsz, t, _ = p.shape

    def heads(a, d):
        return jnp.transpose(a.reshape(bsz, t, ML_HEADS, d), (0, 2, 1, 3)).astype(f32)

    q = heads(q, ML_DQK)
    k = heads(k, ML_DQK) * (ML_DQK ** -0.5)
    v = heads(v, ML_DV)
    pre = gates.reshape(bsz, t, 2, 2, ML_HEADS).astype(f32) + gate_b.astype(f32)
    pre = GATE_CAP * jnp.tanh(pre / GATE_CAP)
    pre = jnp.transpose(pre, (2, 3, 0, 4, 1))
    return q, k, v, o, pre[0], jax.nn.log_sigmoid(pre[1])

def _mlstm_readout(h, o, norm_g):
    h = h * lax.rsqrt(jnp.mean(h * h, axis=-1, keepdims=True) + NORM_EPS)
    bsz, nh, t, dv = h.shape
    h = jnp.transpose(h, (0, 2, 1, 3)).reshape(bsz, t, nh * dv)
    return (h * norm_g * jax.nn.sigmoid(o.astype(jnp.float32))).astype(o.dtype)

def _rwkv_inputs(p, mu, w_up, w0, a_up, a0, k_k, k_a):
    f32 = jnp.float32
    p = p + mu * (0.5 * (_prev(p) + _next(p)) - p)
    r, k, v, wd, ad, gd = _split(p, [RW_W, RW_W, RW_W, 2 * RW_DECAY_LORA, 2 * RW_A_LORA, RW_GATE_LORA])
    bsz, t, _ = p.shape
    wd = wd.reshape(bsz, t, 2, RW_DECAY_LORA)
    ad = ad.reshape(bsz, t, 2, RW_A_LORA)
    lw = (w0 + jnp.einsum("btdr,drc->btdc", jnp.tanh(wd), w_up)).astype(f32)
    decay = jnp.exp(-jnp.exp(-jax.nn.softplus(-lw) - 0.5))
    a = jax.nn.sigmoid((a0 + jnp.einsum("btdr,drc->btdc", ad, a_up)).astype(f32))

    def heads(u):
        return u.reshape(*u.shape[:-1], RW_HEADS, RW_N)

    kf = k.astype(f32)
    kk = heads(kf * k_k)
    kk = kk * lax.rsqrt(jnp.sum(kk * kk, axis=-1, keepdims=True) + 1e-12)
    kd = kf[:, :, None, :] * (1.0 + (a - 1.0) * k_a)
    return heads(r.astype(f32)), heads(kd), heads(v.astype(f32)), heads(decay), kk, heads(a), gd

def _rwkv7_update(S, k, v, w, kk, a):
    sa = jnp.einsum("bhij,bhj->bhi", S, kk)
    return S * w[:, :, None, :] - sa[..., None] * (kk * a)[:, :, None, :] + v[..., None] * k[:, :, None, :]

def _rwkv7_run(r, k, v, w, kk, a, state, reverse):
    xs = tuple(jnp.moveaxis(u, 1, 0) for u in (r, k, v, w, kk, a))

    def step(S, inp):
        r_t, k_t, v_t, w_t, kk_t, a_t = inp
        S = _rwkv7_update(S, k_t, v_t, w_t, kk_t, a_t)
        return S, jnp.einsum("bhij,bhj->bhi", S, r_t)

    state, ys = lax.scan(step, state, xs, reverse=reverse)
    return state, jnp.moveaxis(ys, 0, 1)

def _rwkv7_final_state(k, v, w, kk, a, state, reverse):
    xs = tuple(jnp.moveaxis(u, 1, 0) for u in (k, v, w, kk, a))
    state, _ = lax.scan(lambda S, inp: (_rwkv7_update(S, *inp), None), state, xs, reverse=reverse)
    return state

def _rwkv_readout(y, r, kd, v, gd, r_k, ln_w, ln_b, g_up):
    bsz, t = y.shape[:2]
    mu = jnp.mean(y, axis=-1, keepdims=True)
    var = jnp.mean(jnp.square(y - mu), axis=-1, keepdims=True)
    yn = ((y - mu) * lax.rsqrt(var + RW_GN_EPS)).reshape(bsz, t, RW_W) * ln_w + ln_b
    bonus = jnp.sum(r[:, :, None] * kd * r_k, axis=(2, 4))[..., None] * v
    g = jax.nn.sigmoid(gd) @ g_up
    return ((yn + bonus.reshape(bsz, t, RW_W)) * g).astype(g.dtype)

def _merge(ha, hb, gates, p_a, p_b, w_out):
    ga, gb = _split(gates, [D_MODEL, D_MODEL])
    return (jax.nn.sigmoid(ga) * (ha @ p_a) + jax.nn.sigmoid(gb) * (hb @ p_b)) @ w_out

def _hybrid_mixer(h_lat, h_ctx, w_in, conv_k, conv_b, gate_b, ml_norm_g, rw_mu, rw_w_up, rw_w0, rw_a_up,
                  rw_a0, rw_g_up, rw_k_k, rw_k_a, rw_r_k, rw_ln_w, rw_ln_b, p_a, p_b, w_out, need_ctx):
    bsz = h_lat.shape[0]
    ml_l, rw_l, gt_l = _split(h_lat @ w_in, [ML_COLS, RW_COLS, 2 * D_MODEL])
    ml_c, rw_c, gt_c = _split(h_ctx @ w_in, [ML_COLS, RW_COLS, 2 * D_MODEL])

    ql, kl, vl, ol, igl, lfl = _mlstm_inputs(ml_l, lambda u: _grid_conv(u, conv_k, conv_b), gate_b)
    qc, kc, vc, oc, igc, lfc = _mlstm_inputs(ml_c, lambda u: _line_conv(u, conv_k, conv_b), gate_b)
    zero = _mlstm_zero_state(bsz)
    if need_ctx:
        mst_f, mhc_f = _mlstm_run(qc, kc, vc, igc[0], lfc[0], zero, False)
        mst_b, mhc_b = _mlstm_run(qc, kc, vc, igc[1], lfc[1], zero, True)
    else:
        mst_f = _mlstm_final_state(kc, vc, igc[0], lfc[0], zero, False)
        mst_b = _mlstm_final_state(kc, vc, igc[1], lfc[1], zero, True)
    _, mhl_f = _mlstm_run(ql, kl, vl, igl[0], lfl[0], mst_f, False)
    _, mhl_b = _mlstm_run(ql, kl, vl, igl[1], lfl[1], mst_b, True)
    a_lat = _mlstm_readout(mhl_f + mhl_b, ol, ml_norm_g)

    rw_par = (rw_mu, rw_w_up, rw_w0, rw_a_up, rw_a0, rw_k_k, rw_k_a)
    rl, kdl, vvl, wl, kkl, al, gdl = _rwkv_inputs(rw_l, *rw_par)
    rc, kdc, vvc, wc, kkc, ac, gdc = _rwkv_inputs(rw_c, *rw_par)
    s0 = jnp.zeros((bsz, RW_HEADS, RW_N, RW_N), jnp.float32)
    if need_ctx:
        rst_f, ryc_f = _rwkv7_run(rc, kdc[:, :, 0], vvc, wc[:, :, 0], kkc, ac[:, :, 0], s0, False)
        rst_b, ryc_b = _rwkv7_run(rc, kdc[:, :, 1], vvc, wc[:, :, 1], kkc, ac[:, :, 1], s0, True)
    else:
        rst_f = _rwkv7_final_state(kdc[:, :, 0], vvc, wc[:, :, 0], kkc, ac[:, :, 0], s0, False)
        rst_b = _rwkv7_final_state(kdc[:, :, 1], vvc, wc[:, :, 1], kkc, ac[:, :, 1], s0, True)
    _, ryl_f = _rwkv7_run(rl, kdl[:, :, 0], vvl, wl[:, :, 0], kkl, al[:, :, 0], rst_f, False)
    _, ryl_b = _rwkv7_run(rl, kdl[:, :, 1], vvl, wl[:, :, 1], kkl, al[:, :, 1], rst_b, True)
    b_lat = _rwkv_readout(ryl_f + ryl_b, rl, kdl, vvl, gdl, rw_r_k, rw_ln_w, rw_ln_b, rw_g_up)

    out_lat = _merge(a_lat, b_lat, gt_l, p_a, p_b, w_out)
    out_ctx = None
    if need_ctx:
        a_ctx = _mlstm_readout(mhc_f + mhc_b, oc, ml_norm_g)
        b_ctx = _rwkv_readout(ryc_f + ryc_b, rc, kdc, vvc, gdc, rw_r_k, rw_ln_w, rw_ln_b, rw_g_up)
        out_ctx = _merge(a_ctx, b_ctx, gt_c, p_a, p_b, w_out)
    return out_lat, out_ctx

def _moe(h, router_w, router_b, w_gate, w_up, w_down):
    bsz, t, d = h.shape
    hf = h.reshape(bsz * t, d)
    scores = jax.nn.sigmoid((hf @ router_w).astype(jnp.float32))
    sel = scores + router_b.astype(jnp.float32)
    grp = sel.reshape(-1, N_GROUPS, EXPERTS_PER_GROUP)
    group_score = jnp.sum(lax.top_k(grp, GROUP_SCORE_TOPK)[0], axis=-1)
    best = jnp.argmax(group_score, axis=-1)
    in_group = (jnp.arange(N_EXPERTS) // EXPERTS_PER_GROUP)[None, :] == best[:, None]
    _, idx = lax.top_k(jnp.where(in_group, sel, -jnp.inf), TOP_K)
    wsel = jnp.take_along_axis(scores, idx, axis=-1)
    wsel = wsel / jnp.sum(wsel, axis=-1, keepdims=True)
    comb = jnp.sum(jax.nn.one_hot(idx, N_EXPERTS, dtype=jnp.float32) * wsel[..., None], axis=1).astype(h.dtype)
    y = jnp.zeros_like(hf)
    for e in range(N_EXPERTS):
        hid = jax.nn.silu(hf @ w_gate[e]) * (hf @ w_up[e])
        y = y + (comb[:, e:e + 1] * hid) @ w_down[e]
    return y.reshape(bsz, t, d)

def setup_inputs(seed: int = 0) -> dict:
    key = jax.random.key(seed)
    ks = list(jax.random.split(key, 40))
    f32 = jnp.float32
    L = DEPTH

    def nrm(i, shape, scale):
        return scale * jax.random.normal(ks[i], shape, f32)

    def gain(i, shape):
        return 1.0 + nrm(i, shape, 0.02)

    i_bias = nrm(12, (L, 1, 2, ML_HEADS), 0.1)
    f_bias = jax.random.uniform(ks[13], (L, 1, 2, ML_HEADS), f32, 3.0, 6.0)
    centre = jnp.zeros((3, 3, 1), f32).at[1, 1, 0].set(1.0)
    return {
        "x": nrm(0, (BATCH, SEQ, D_MODEL), 1.0),
        "c": nrm(1, (BATCH, D_MODEL), 1.0),
        "ctx": nrm(2, (BATCH, CTX_LEN, D_MODEL), 1.0),
        "c_ctx": nrm(3, (D_MODEL,), 1.0),
        "w_ada": nrm(4, (L, D_MODEL, N_MOD * D_MODEL), 0.5 * D_MODEL ** -0.5),
        "b_ada": nrm(5, (L, N_MOD * D_MODEL), 0.02),
        "norm1_g": gain(6, (L, D_MODEL)),
        "norm2_g": gain(7, (L, D_MODEL)),
        "w_in": nrm(8, (L, D_MODEL, IN_COLS), D_MODEL ** -0.5),
        "ml_conv_k": centre + nrm(9, (L, 3, 3, 2 * ML_QK), 0.1),
        "ml_conv_b": nrm(10, (L, 2 * ML_QK), 0.02),
        "ml_gate_b": jnp.concatenate([i_bias, f_bias], axis=1),
        "ml_norm_g": gain(11, (L, ML_V)),
        "rw_mu": jax.random.uniform(ks[14], (L, RW_COLS), f32, 0.0, 1.0),
        "rw_w_up": nrm(15, (L, 2, RW_DECAY_LORA, RW_W), 0.5 * RW_DECAY_LORA ** -0.5),
        "rw_w0": jax.random.uniform(ks[16], (L, 2, RW_W), f32, -6.0, -1.0),
        "rw_a_up": nrm(17, (L, 2, RW_A_LORA, RW_W), 0.5 * RW_A_LORA ** -0.5),
        "rw_a0": nrm(18, (L, 2, RW_W), 0.1),
        "rw_g_up": nrm(19, (L, RW_GATE_LORA, RW_W), RW_GATE_LORA ** -0.5),
        "rw_k_k": 0.85 + nrm(20, (L, RW_W), 0.02),
        "rw_k_a": gain(21, (L, RW_W)),
        "rw_r_k": nrm(22, (L, RW_HEADS, RW_N), 0.1),
        "rw_ln_w": gain(23, (L, RW_W)),
        "rw_ln_b": nrm(24, (L, RW_W), 0.02),
        "merge_pa": nrm(25, (L, ML_V, D_MODEL), ML_V ** -0.5),
        "merge_pb": nrm(26, (L, RW_W, D_MODEL), RW_W ** -0.5),
        "w_out": nrm(27, (L, D_MODEL, D_MODEL), D_MODEL ** -0.5),
        "router_w": nrm(28, (D_MODEL, N_EXPERTS), D_MODEL ** -0.5),
        "router_b": nrm(29, (N_EXPERTS,), 0.01),
        "exp_w_gate": nrm(30, (L, N_EXPERTS, D_MODEL, D_EXPERT), D_MODEL ** -0.5),
        "exp_w_up": nrm(31, (L, N_EXPERTS, D_MODEL, D_EXPERT), D_MODEL ** -0.5),
        "exp_w_down": nrm(32, (L, N_EXPERTS, D_EXPERT, D_MODEL), D_EXPERT ** -0.5),
        "final_g": gain(33, (D_MODEL,)),
    }

def reference(x, c, ctx, c_ctx, w_ada, b_ada, norm1_g, norm2_g, w_in, ml_conv_k, ml_conv_b, ml_gate_b,
              ml_norm_g, rw_mu, rw_w_up, rw_w0, rw_a_up, rw_a0, rw_g_up, rw_k_k, rw_k_a, rw_r_k, rw_ln_w,
              rw_ln_b, merge_pa, merge_pb, w_out, router_w, router_b, exp_w_gate, exp_w_up, exp_w_down,
              final_g):
    f32 = jnp.float32
    s_lat = jax.nn.silu(c.astype(f32))
    s_ctx = jax.nn.silu(c_ctx.astype(f32))
    x_lat, x_ctx = x, ctx
    for l in range(DEPTH):
        last = l == DEPTH - 1
        sh1, sc1, g1, sh2, sc2, g2 = _split((s_lat @ w_ada[l] + b_ada[l]).astype(x.dtype)[:, None, :],
                                            [D_MODEL] * N_MOD)
        csh1, csc1, cg1, csh2, csc2, cg2 = _split((s_ctx @ w_ada[l] + b_ada[l]).astype(x.dtype),
                                                  [D_MODEL] * N_MOD)
        h_lat = _rmsnorm(x_lat, norm1_g[l]) * (1 + sc1) + sh1
        h_ctx = _rmsnorm(x_ctx, norm1_g[l]) * (1 + csc1) + csh1
        mix_lat, mix_ctx = _hybrid_mixer(
            h_lat, h_ctx, w_in[l], ml_conv_k[l], ml_conv_b[l], ml_gate_b[l], ml_norm_g[l], rw_mu[l],
            rw_w_up[l], rw_w0[l], rw_a_up[l], rw_a0[l], rw_g_up[l], rw_k_k[l], rw_k_a[l], rw_r_k[l],
            rw_ln_w[l], rw_ln_b[l], merge_pa[l], merge_pb[l], w_out[l], not last)
        moe_w = (router_w, router_b, exp_w_gate[l], exp_w_up[l], exp_w_down[l])
        x_lat = x_lat + g1 * mix_lat
        x_lat = x_lat + g2 * _moe(_rmsnorm(x_lat, norm2_g[l]) * (1 + sc2) + sh2, *moe_w)
        if not last:
            x_ctx = x_ctx + cg1 * mix_ctx
            x_ctx = x_ctx + cg2 * _moe(_rmsnorm(x_ctx, norm2_g[l]) * (1 + csc2) + csh2, *moe_w)
    return _rmsnorm(x_lat, final_g)


_drawn_inputs = setup_inputs


def setup_inputs(seed=0):
    import zlib

    import numpy as np

    out = dict(_drawn_inputs(seed))
    spreads = {}
    factors = {'norm1_g': 2.89,
     'ml_conv_b': 3.667,
     'ml_norm_g': 38.805,
     'rw_w_up': 5.248,
     'rw_a0': 8.0,
     'rw_k_k': 42.6,
     'rw_k_a': 5.122,
     'rw_ln_w': 39.656,
     'rw_ln_b': 51.858,
     'final_g': 8.258,
     'norm2_g': 5.938,
     'router_b': 4.34}
    for name, (base, spread) in spreads.items():
        noise = np.random.default_rng([zlib.crc32(name.encode()), seed]).standard_normal(out[name].shape)
        drawn = base * np.exp(spread * noise) if base else spread * noise
        out[name] = __import__('jax').numpy.asarray(drawn.astype(out[name].dtype))
    for name, factor in factors.items():
        out[name] = (out[name] * factor).astype(out[name].dtype)
    return out
```

```python
import numpy as np
import concourse.bass as bass
from concourse import mybir
from contextlib import ExitStack

F32 = mybir.dt.float32
I32 = mybir.dt.int32
ALU = mybir.AluOpType
ACT = mybir.ActivationFunctionType
AX = mybir.AxisListType

P = 128
D = 1024
DB = D // P
SEQ, CTX = 512, 256
T = SEQ + CTX
TT = T // P
TL = SEQ // P
GRID_W = 64
GRID_H = SEQ // GRID_W
ML_H, DQK, DV = 4, 64, 128
RW_H, RN = 8, 64
RW_W = RW_H * RN
C = 64
NC = T // C
NCL = SEQ // C
COL_Q, COL_K, COL_V, COL_O, COL_G, COL_RW = 0, 256, 512, 1024, 1536, 1552
NRW = 15
COL_GT = COL_RW + NRW * P
NE, DE = 16, 512
EB = DE // P
EPS = 1e-6
GN_EPS = 6.4e-4
KAPPA = float(np.exp(-0.5))


class Chain:

    def __init__(self, eng, sem):
        self.eng, self.sem, self.n = eng, sem, 0

    def __call__(self, ins):
        self.n += 1
        ins.then_inc(self.sem, 1)
        self.eng.wait_ge(self.sem, self.n)


class Core:
    pass


def bc(ap, n):
    return ap.unsqueeze(2).to_broadcast([ap.shape[0], ap.shape[1], n])



def rounds(eng, n):
    yield 0
    with eng.Fori(1, n) as i:
        yield i


def wait(eng, sem, value):
    if not (isinstance(value, int) and value == 0):
        eng.wait_ge(sem, value)


def phase(nc, k, program, give_back=True):
    sems = []

    def sem(name):
        sems.append(nc.alloc_semaphore(name=name))
        return sems[-1]
    k.sem = sem
    program(nc, k)
    if give_back:
        nc.clear_and_free_semaphores(sems)
        nc.all_engine_barrier()




def constants(nc, k):
    with nc.Block() as block:
        made = k.sem("const_made")

        @block.gpsimd
        def _(pool):
            pool.memset(k.ident[:, :], 0.0).then_inc(made, 1)
            pool.memset(k.ones[:, :], 1.0).then_inc(made, 1)
            pool.wait_ge(made, 2)
            pool.affine_select(out=k.ident[:, :], in_=k.ident[:, :], compare_op=ALU.not_equal, fill=1.0,
                               base=0, pattern=[[-1, P]], channel_multiplier=1).then_inc(made, 1)
            pool.wait_ge(made, 3)


def modulate(nc, k):
    ctx = ExitStack()
    with ctx:
        def sb(name, shape):
            return ctx.enter_context(nc.sbuf_tensor(name, shape, F32))
        x_rows = sb("x_rows", [P, TT, D])
        xT = sb("xT", [P, DB, T])
        wada = [sb(f"wada{s}", [P, DB, 512]) for s in range(2)]
        sT = sb("sT", [P, DB, 2])
        sT_t = sb("sT_t", [P, DB, 2])
        b_ada = sb("b_ada_sb", [P, 48])
        g1n = sb("g1n", [P, DB])
        scale1 = sb("scale1", [P, 2, DB])
        rstd = sb("rstd", [P, T])
        rms = sb("rms", [P, T])
        ps = k.ps
        x_in, small_in, silu_t, silu = k.sem("x_in"), k.sem("small_in"), k.sem("silu_t"), k.sem("silu")
        ada_in = [k.sem(f"ada_in{s}") for s in range(2)]
        ada_used = [k.sem(f"ada_used{s}") for s in range(2)]
        x_turned, x_kept, sq_done, ss_done = k.sem("x_turned"), k.sem("x_kept"), k.sem("sq_done"), k.sem("ss_done")
        ms_done, rms_done, norm_done = k.sem("ms_done"), k.sem("rms_done"), k.sem("norm_done")
        xt_out, h_done, dch = k.sem("xt_out"), k.sem("h_done"), k.sem("mod_dve")
        sq = x_rows[:, :, :].rearrange("p a b -> p (a b)").rearrange("p (k t) -> p k t", k=DB)
        block = ctx.enter_context(nc.Block())
        ada_v = k.w["w_ada"][0].rearrange("(k p) n -> p k n", p=P)
        ADA = 12

        @block.sync
        def _(sp):
            with nc.allow_non_contiguous_dma(reason="vectors over partitions"):
                sp.dma_start(sT_t[:, :, 0], k.w["c"][0].rearrange("(k p) -> p k", p=P)).then_inc(small_in, 16)
                sp.dma_start(sT_t[:, :, 1], k.w["c_ctx"].rearrange("(k p) -> p k", p=P)).then_inc(small_in, 16)
                sp.dma_start(b_ada[:, :], k.w["b_ada"][0].rearrange("(k p) -> p k", p=P)).then_inc(small_in, 16)
                sp.dma_start(g1n[:, :], k.w["norm1_g"][0].rearrange("(k p) -> p k", p=P)).then_inc(small_in, 16)
            sp.dma_start(x_rows[:, 0:TL, :], k.w["x"][0].rearrange("(t p) d -> p t d", p=P)).then_inc(x_in, 16)
            sp.dma_start(x_rows[:, TL:TT, :], k.w["ctx"][0].rearrange("(t p) d -> p t d", p=P)).then_inc(x_in, 16)
            for i in rounds(sp, ADA // 2):
                for s in range(2):
                    wait(sp, ada_used[s], i)
                    sp.dma_start(wada[s][:, :, :], ada_v[:, :, bass.ds((2 * i + s) * 512, 512)]).then_inc(ada_in[s], 16)
            sp.wait_ge(x_kept, TT * 2)
            sp.dma_start(k.xT_d.rearrange("(k p) t -> p k t", p=P), xT[:, :, 0:SEQ]).then_inc(xt_out, 16)
            sp.wait_ge(xt_out, 16)

        @block.tensor
        def _(pe):
            pe.wait_ge(x_in, 32)
            for t in range(TT):
                for g in range(2):
                    n = 2 * t + g
                    if n >= 4:
                        pe.wait_ge(x_kept, n - 3)
                    for j in range(4):
                        mm = pe.transpose(ps[:, n % 4, j * P:(j + 1) * P],
                                          x_rows[:, t, (4 * g + j) * P:(4 * g + j + 1) * P], k.ident[:, :])
                    mm.then_inc(x_turned, 1)
            pe.wait_ge(silu, 1)
            for i in rounds(pe, ADA // 2):
                for s in range(2):
                    pe.wait_ge(ada_in[s], 16 * i + 16)
                    for m in range(4):
                        for kb in range(DB):
                            mm = pe.matmul(ps[:, 7, bass.ds((2 * i + s) * 8 + 2 * m, 2)],
                                           wada[s][:, kb, m * P:(m + 1) * P], sT[:, kb, :],
                                           start=(kb == 0), stop=(kb == DB - 1))
                    mm.then_inc(ada_used[s], 1)
            pe.wait_ge(sq_done, 1)
            for lo, n, b in ((0, SEQ, 4), (SEQ, CTX, 5)):
                for kb in range(DB):
                    mm = pe.matmul(ps[:, b, 0:n], k.ones[:, :], sq[:, kb, lo:lo + n],
                                   start=(kb == 0), stop=(kb == DB - 1))
            mm.then_inc(ss_done, 1)

        @block.scalar
        def _(act):
            act.wait_ge(small_in, 64)
            act.activation(sT[:, :, :], sT_t[:, :, :], ACT.Tanh, scale=0.5).then_inc(silu_t, 1)
            for n in range(2 * TT):
                t, g = n // 2, n % 2
                act.wait_ge(x_turned, n + 1)
                act.activation(xT[:, 4 * g:4 * g + 4, t * P:(t + 1) * P],
                               ps[:, n % 4, :].rearrange("p (j t) -> p j t", j=4), ACT.Copy).then_inc(x_kept, 1)
            act.wait_ge(x_kept, 2 * TT)
            act.activation(sq, xT[:, :, :], ACT.Square).then_inc(sq_done, 1)
            act.wait_ge(ms_done, 1)
            act.activation(rms[:, :], rms[:, :], ACT.Sqrt).then_inc(rms_done, 1)
            for kb in range(DB):
                act.wait_ge(norm_done, kb + 1)
                act.activation(k.hT[:, kb, 0:SEQ], k.hT[:, kb, 0:SEQ], ACT.Identity,
                               bias=k.mod[:, 0, kb:kb + 1]).then_inc(h_done, 1)
                act.activation(k.hT[:, kb, SEQ:T], k.hT[:, kb, SEQ:T], ACT.Identity,
                               bias=k.mod[:, 1, kb:kb + 1]).then_inc(h_done, 1)
            act.wait_ge(h_done, 2 * DB)

        @block.vector
        def _(dve):
            link = Chain(dve, dch)
            dve.wait_ge(silu_t, 1)
            link(dve.tensor_scalar(sT[:, :, :], sT[:, :, :], 0.5, 0.5, ALU.mult, ALU.add))
            dve.tensor_tensor(sT[:, :, :], sT[:, :, :], sT_t[:, :, :], ALU.mult).then_inc(silu, 1)
            dve.wait_ge(ss_done, 1)
            dve.tensor_scalar(rms[:, 0:SEQ], ps[:, 4, :], 1.0 / D, EPS, ALU.mult, ALU.add)
            dve.tensor_scalar(rms[:, SEQ:T], ps[:, 5, 0:CTX], 1.0 / D, EPS, ALU.mult, ALU.add).then_inc(ms_done, 1)
            for s in range(2):
                dve.wait_ge(ada_used[s], ADA // 2)
            for w in range(2):
                link(dve.tensor_tensor(k.mod[:, w, :], ps[:, 7, 0:96].rearrange("p (m w) -> p m w", w=2)[:, :, w],
                                       b_ada[:, :], ALU.add))
                link(dve.tensor_scalar(scale1[:, w, :], k.mod[:, w, DB:2 * DB], 1.0, None, ALU.add))
                link(dve.tensor_tensor(scale1[:, w, :], scale1[:, w, :], g1n[:, :], ALU.mult))
            dve.wait_ge(rms_done, 1)
            link(dve.reciprocal(rstd[:, :], rms[:, :]))
            for kb in range(DB):
                dve.scalar_tensor_tensor(k.hT[:, kb, 0:SEQ], xT[:, kb, 0:SEQ], scale1[:, 0, kb:kb + 1],
                                         rstd[:, 0:SEQ], ALU.mult, ALU.mult)
                dve.scalar_tensor_tensor(k.hT[:, kb, SEQ:T], xT[:, kb, SEQ:T], scale1[:, 1, kb:kb + 1],
                                         rstd[:, SEQ:T], ALU.mult, ALU.mult).then_inc(norm_done, 1)


def project(nc, k):
    ctx = ExitStack()
    with ctx:
        def sb(name, shape):
            return ctx.enter_context(nc.sbuf_tensor(name, shape, F32))
        w = [sb(f"w_slot{s}", [P, DB, P]) for s in range(2)]
        wv = [sb(f"wv{s}", [P, DB, 512]) for s in range(2)]
        wg = sb("wg", [P, DB, 16])
        raw = [sb(f"raw{s}", [P, T + 4]) for s in range(2)]
        own = [sb(f"own{s}", [P, T]) for s in range(2)]
        nb = sb("nb", [P, T])
        res = [sb(f"res{s}", [P, T]) for s in range(2)]
        mu = sb("mu", [P, NRW])
        mu1 = sb("mu1", [P, NRW])
        muh = sb("muh", [P, NRW])
        ps = k.ps
        w_in_s = [k.sem(f"w_in{s}") for s in range(2)]
        wv_in, wg_in, mu_in, mu_done = k.sem("wv_in"), k.sem("wg_in"), k.sem("mu_in"), k.sem("mu_done")
        rows_done, rows_kept, nbs = k.sem("rows_done"), k.sem("rows_kept"), k.sem("neighbours_added")
        mm_done, ps_kept, shifted, stored, gate_done = (
            [k.sem(f"{what}{s}") for s in range(2)] for what in ("mm_done", "ps_kept", "shifted", "stored", "gate_done"))
        block = ctx.enter_context(nc.Block())
        w_v = k.w["w_in"][0].rearrange("(k p) n -> p k n", p=P)
        QK, NGT = 4, 16
        RW_LOOP = (NRW - 1) // 2
        N_RW = [(NRW + 1) // 2, NRW // 2]
        GATE_N = [QK // 2 + N_RW[0], QK // 2 + N_RW[1]]
        GATE_SLOTS = (NRW % 2, 1 - NRW % 2)

        @block.sync
        def _(sp):
            def load(s, n, col, first=False):
                if not first:
                    sp.wait_ge(mm_done[s], n)
                sp.dma_start(w[s][:, :, :], w_v[:, :, bass.ds(col, P)]).then_inc(w_in_s[s], 16)
            with nc.allow_non_contiguous_dma(reason="a vector over partitions"):
                sp.dma_start(mu[:, :], k.w["rw_mu"][0].rearrange("(b p) -> p b", p=P)).then_inc(mu_in, 16)
            for u in range(QK):
                load(u % 2, u // 2, COL_Q + u * P, first=u < 2)
            for i in rounds(sp, RW_LOOP):
                for s in range(2):
                    load(s, QK // 2 + i, COL_RW + (2 * i + s) * P)
            load(0, QK // 2 + RW_LOOP, COL_RW + (NRW - 1) * P)
            for i in rounds(sp, NGT // 2):
                for j, s in enumerate(GATE_SLOTS):
                    load(s, GATE_N[s] + i, COL_GT + (2 * i + j) * P)
            sp.dma_start(wv[0][:, :, :], w_v[:, :, COL_V:COL_V + 512]).then_inc(wv_in, 16)
            sp.dma_start(wv[1][:, :, :], w_v[:, :, COL_O:COL_O + 512]).then_inc(wv_in, 16)
            sp.dma_start(wg[:, :, :], w_v[:, :, COL_G:COL_G + 16]).then_inc(wg_in, 16)

        @block.tensor
        def _(pe):
            def cols(s, n, n_ctx, first=False):
                pe.wait_ge(w_in_s[s], n * 16 + 16)
                if not first:
                    pe.wait_ge(ps_kept[s], n)
                for lo, m, b in ((0, SEQ, 2 * s), (SEQ, n_ctx, 2 * s + 1)):
                    for kb in range(DB if m else 0):
                        mm = pe.matmul(ps[:, b, 0:m], w[s][:, kb, :], k.hT[:, kb, lo:lo + m],
                                       start=(kb == 0), stop=(kb == DB - 1))
                mm.then_inc(mm_done[s], 1)
            for u in range(QK):
                cols(u % 2, u // 2, CTX, first=u < 2)
            for i in rounds(pe, RW_LOOP):
                for s in range(2):
                    cols(s, QK // 2 + i, CTX)
            cols(0, QK // 2 + RW_LOOP, CTX)
            for i in rounds(pe, NGT // 2):
                for s in GATE_SLOTS:
                    cols(s, GATE_N[s] + i, 0)
            pe.wait_ge(wv_in, 32)
            n = 0
            for j, tiles in ((0, TT), (1, TL)):
                for t in range(tiles):
                    if n >= 2:
                        pe.wait_ge(rows_kept, n - 1)
                    for kb in range(DB):
                        mm = pe.matmul(ps[:, 4 + n % 2, :], k.hT[:, kb, t * P:(t + 1) * P], wv[j][:, kb, :],
                                       start=(kb == 0), stop=(kb == DB - 1))
                    mm.then_inc(rows_done, 1)
                    n += 1
            pe.wait_ge(wg_in, 16)
            for t in range(TT):
                for kb in range(DB):
                    mm = pe.matmul(ps[:, 6, 16 * t:16 * t + 16], k.hT[:, kb, t * P:(t + 1) * P], wg[:, kb, :],
                                   start=(kb == 0), stop=(kb == DB - 1))
            mm.then_inc(rows_done, 1)

        @block.scalar
        def _(act):
            for u in range(QK):
                s = u % 2
                act.wait_ge(mm_done[s], u // 2 + 1)
                act.activation(k.qkT[:, u, 0:SEQ], ps[:, 2 * s, :], ACT.Copy)
                act.activation(k.qkT[:, u, SEQ:T], ps[:, 2 * s + 1, 0:CTX], ACT.Copy).then_inc(ps_kept[s], 1)
            act.wait_ge(mu_done, 3)

            def keep(s, m, i):
                act.wait_ge(mm_done[s], QK // 2 + m + 1)
                wait(act, shifted[s], m)
                a, b = ps[:, 2 * s, :], ps[:, 2 * s + 1, 0:CTX]
                act.activation(raw[s][:, 1:SEQ + 1], a, ACT.Copy)
                act.activation(raw[s][:, SEQ + 3:T + 3], b, ACT.Copy)
                act.activation(own[s][:, 0:SEQ], a, ACT.Copy, scale=mu1[:, bass.ds(i, 1)])
                act.activation(own[s][:, SEQ:T], b, ACT.Copy, scale=mu1[:, bass.ds(i, 1)]).then_inc(ps_kept[s], 1)
            for i in rounds(act, RW_LOOP):
                for s in range(2):
                    keep(s, i, 2 * i + s)
            keep(0, RW_LOOP, NRW - 1)
            for s in range(2):
                act.wait_ge(shifted[s], N_RW[s])
            for i in rounds(act, NGT // 2):
                for s in GATE_SLOTS:
                    act.wait_ge(mm_done[s], GATE_N[s] + i + 1)
                    wait(act, gate_done[s], i)
                    act.activation(own[s][:, 0:SEQ], ps[:, 2 * s, :], ACT.Tanh, scale=0.5).then_inc(ps_kept[s], 1)
            n = 0
            for j, tiles in ((0, TT), (1, TL)):
                for t in range(tiles):
                    act.wait_ge(rows_done, n + 1)
                    if j:
                        ins = act.activation(k.o_ml[:, t, :], ps[:, 4 + n % 2, :], ACT.Tanh, scale=0.5)
                    else:
                        ins = act.activation(k.v_ml[:, t, :, 0:DV], ps[:, 4 + n % 2, :].rearrange("p (h v) -> p h v", v=DV),
                                             ACT.Copy)
                    ins.then_inc(rows_kept, 1)
                    n += 1
            act.wait_ge(rows_done, n + 1)
            act.activation(k.g_ml[:, :, :], ps[:, 6, 0:16 * TT].rearrange("p (t g) -> p t g", t=TT),
                           ACT.Copy).then_inc(rows_kept, 1)
            act.wait_ge(rows_kept, n + 1)

        @block.vector
        def _(dve):
            for s in range(2):
                dve.memset(raw[s][:, :], 0.0)
            dve.wait_ge(mu_in, 16)
            dve.tensor_scalar(mu1[:, :], mu[:, :], -1.0, 1.0, ALU.mult, ALU.add).then_inc(mu_done, 1)
            dve.tensor_scalar(muh[:, :], mu[:, :], 0.5, None, ALU.mult).then_inc(mu_done, 1)
            dve.wait_ge(mu_done, 2)
            dve.memset(nb[:, 0:1], 0.0).then_inc(mu_done, 1)
            dve.wait_ge(mu_done, 3)

            def shift(s, m, i):
                r = raw[s]
                dve.wait_ge(ps_kept[s], QK // 2 + m + 1)
                dve.tensor_tensor(nb[:, 0:SEQ], r[:, 0:SEQ], r[:, 2:SEQ + 2], ALU.add)
                dve.tensor_tensor(nb[:, SEQ:T], r[:, SEQ + 2:T + 2], r[:, SEQ + 4:T + 4], ALU.add).then_inc(nbs, 1)
                dve.wait_ge(nbs, i + 1)
                wait(dve, stored[s], 16 * m)
                dve.scalar_tensor_tensor(res[s][:, :], nb[:, :], muh[:, bass.ds(i, 1)], own[s][:, :],
                                         ALU.mult, ALU.add).then_inc(shifted[s], 1)
                dve.wait_ge(shifted[s], m + 1)
            for i in rounds(dve, RW_LOOP):
                for s in range(2):
                    shift(s, i, 2 * i + s)
            shift(0, RW_LOOP, NRW - 1)
            for i in rounds(dve, NGT // 2):
                for s in GATE_SLOTS:
                    dve.wait_ge(ps_kept[s], GATE_N[s] + i + 1)
                    dve.wait_ge(stored[s], 16 * N_RW[s] + 16 * i)
                    dve.tensor_scalar(res[s][:, 0:SEQ], own[s][:, 0:SEQ], 0.5, 0.5, ALU.mult, ALU.add)\
                       .then_inc(gate_done[s], 1)
            dve.wait_ge(rows_kept, TT + TL)
            dve.tensor_scalar(k.o_ml[:, :, :], k.o_ml[:, :, :], 0.5, 0.5, ALU.mult, ALU.add).then_inc(mu_done, 1)
            dve.wait_ge(mu_done, 4)

        @block.gpsimd
        def _(pool):
            def store(s, m, i):
                pool.wait_ge(shifted[s], m + 1)
                pool.dma_start(k.rw_d[bass.ds(i, 1)].rearrange("a p t -> p (a t)"), res[s][:, :]).then_inc(stored[s], 16)
            for i in rounds(pool, RW_LOOP):
                for s in range(2):
                    store(s, i, 2 * i + s)
            store(0, RW_LOOP, NRW - 1)
            for i in rounds(pool, NGT // 2):
                for j, s in enumerate(GATE_SLOTS):
                    pool.wait_ge(gate_done[s], i + 1)
                    pool.dma_start(k.gt_d[bass.ds(2 * i + j, 1)].rearrange("a p t -> p (a t)"), res[s][:, 0:SEQ])\
                        .then_inc(stored[s], 16)
            for s in range(2):
                pool.wait_ge(stored[s], 16 * (N_RW[s] + NGT // 2))


def masks(nc, k):
    with nc.Block() as block:
        made = k.sem("mask_made")

        @block.gpsimd
        def _(pool):
            n = 0
            for value, mask in ((1.0, k.upto), (1.0, k.onward), (0.0, k.neg_upto), (0.0, k.neg_onward)):
                pool.memset(mask[:, :], value).then_inc(made, 1)
                n += 1
            pool.wait_ge(made, n)
            for fill, sign, mask in ((0.0, 1, k.upto), (0.0, -1, k.onward), (LOG_ZERO, 1, k.neg_upto), (LOG_ZERO, -1, k.neg_onward)):
                pool.affine_select(out=mask[:, :], in_=mask[:, :], compare_op=ALU.is_ge, fill=fill, base=0,
                                   pattern=[[sign, P]], channel_multiplier=-sign).then_inc(made, 1)
                n += 1
            pool.wait_ge(made, n)


LOG_ZERO = -1e6
GATE_CAP = 15.0
VW = DV + 1


def mlstm(nc, k):
    ctx = ExitStack()
    with ctx:
        def sb(name, shape):
            return ctx.enter_context(nc.sbuf_tensor(name, shape, F32))
        PADW, PADH = GRID_W + 2, GRID_H + 2
        pad = [sb(f"pad{s}", [P, PADH, PADW]) for s in range(2)]
        line = [sb(f"line{s}", [P, CTX + 2]) for s in range(2)]
        taps, conv_b = sb("taps", [P, 4, 9]), sb("conv_bias", [P, 4])
        gate_b = sb("gate_bias", [P, 16])
        norm_g = sb("ml_norm", [P, 4])
        conv = sb("conv", [P, 4, T])
        kN = sb("k_rows", [P, TT, 256])
        kw = sb("k_weighted", [P, 2, TT, 256])
        pre = sb("pre", [P, TT, 16])
        lf = sb("lf", [P, TT, 8])
        dec = sb("dec", [P, TT, 16])
        ib, eb, wk, carry = sb("ib", [P, TT, 8]), sb("eb", [P, TT, 8]), sb("wk", [P, TT, 8]), sb("carry", [P, TT, 8])
        carry2 = sb("carry2", [P, TT, 2, 2])
        Cs = sb("C_states", [P, 2, TT - 1, 2, VW])
        E = [sb(f"E{s}", [P, 4, P]) for s in range(2)]
        Wt = [sb(f"Wt{s}", [P, 4, P]) for s in range(2)]
        tmp = [sb(f"tmp{s}", [P, 4, VW]) for s in range(2)]
        den, den2 = sb("den", [P, 4]), sb("den2", [P, 4])
        hs = sb("h_sum", [P, TL, 4, DV])
        hq = sb("h_sq", [P, TL, 4, DV])
        ms = sb("h_ms", [P, TL, 4])
        aT = sb("aT", [P, 4, SEQ])
        ps = k.ps
        small_in, pads, conv_done, dch = k.sem("ml_small"), k.sem("pads"), k.sem("conv_done"), k.sem("ml_dve")
        pre_t, pre_done, soft, lf_done, cum_done = k.sem("pre_t"), k.sem("pre_done"), k.sem("soft"), k.sem("lf_done"), k.sem("cum_done")
        k_turned, k_kept, dec_done, exps_done = k.sem("k_turned"), k.sem("k_kept"), k.sem("dec_done"), k.sem("exps_done")
        kw_done, upd_ready, state_done, c2_done = k.sem("kw_done"), k.sem("upd_ready"), k.sem("state_done"), k.sem("c2_done")
        s_ready, e_ready, inter_ready, intra_ready = k.sem("s_ready"), k.sem("e_ready"), k.sem("inter_ready"), k.sem("intra_ready")
        exp_done, inter_kept, w_done, intra_used = k.sem("exp_done"), k.sem("inter_kept"), k.sem("w_done"), k.sem("intra_used")
        h_done, sq_done, ms_done, rms_done = k.sem("mh_done"), k.sem("msq_done"), k.sem("mms_done"), k.sem("mrms_done")
        hn_done, gated, a_turned, a_kept, a_out = k.sem("hn_done"), k.sem("gated"), k.sem("a_turned"), k.sem("a_kept"), k.sem("a_out")
        raw_in = k.sem("raw_in")
        zeros, zero_out = sb("zero_rows", [P, D]), k.sem("zero_rows_out")
        order = [[4, 5, 0, 1, 2, 3], [5, 4, 3, 2, 1, 0]]
        block = ctx.enter_context(nc.Block())

        @block.sync
        def _(sp):
            with nc.allow_non_contiguous_dma(reason="vectors over partitions"):
                for blk in range(4):
                    sp.dma_start(taps[:, blk, :], k.w["ml_conv_k"][0].rearrange("a b (k p) -> k p (a b)", p=P)[blk])\
                        .then_inc(small_in, 16)
                sp.dma_start(conv_b[:, :], k.w["ml_conv_b"][0].rearrange("(k p) -> p k", p=P)).then_inc(small_in, 16)
                sp.dma_start(norm_g[:, :], k.w["ml_norm_g"][0].rearrange("(k p) -> p k", p=P)).then_inc(small_in, 16)
            sp.dma_start(gate_b[:, :], k.w["ml_gate_b"].rearrange("l a b h -> l (a b h)").to_broadcast([P, 16]))\
                .then_inc(small_in, 16)
            sp.wait_ge(pads, 6)
            for blk in range(FEWEST, BLOCKS):
                sp.dma_start(k.ys_d[blk * P:(blk + 1) * P, :], zeros[:, :]).then_inc(zero_out, 16)
            sp.wait_ge(zero_out, 16 * (BLOCKS - FEWEST))
            sp.wait_ge(a_kept, TL * 4)
            sp.dma_start(k.aT_d.rearrange("b p t -> p b t"), aT[:, :, :]).then_inc(a_out, 16)
            sp.wait_ge(a_out, 16)

        @block.gpsimd
        def _(pool):
            for s in range(2):
                pool.memset(pad[s][:, :, :], 0.0).then_inc(pads, 1)
                pool.memset(line[s][:, :], 0.0).then_inc(pads, 1)
            pool.memset(k.v_ml[:, :, :, DV:VW], 1.0).then_inc(pads, 1)
            pool.memset(zeros[:, :], 0.0).then_inc(pads, 1)
            pool.wait_ge(small_in, 16 * 7)
            pool.tensor_tensor(pre[:, :, :], k.g_ml[:, :, :], gate_b[:, :].unsqueeze(1).to_broadcast([P, TT, 16]),
                               ALU.add).then_inc(pre_done, 1)
            pool.wait_ge(k_kept, 3)
            pool.wait_ge(exps_done, 3)
            for i in range(TT - 1):
                for d in range(2):
                    t = order[d][i]
                    pool.tensor_tensor(kw[:, d, t, :].rearrange("p (h j) -> p h j", h=4),
                                       kN[:, t, :].rearrange("p (h j) -> p h j", h=4),
                                       bc(wk[:, t, 4 * d:4 * d + 4], DQK), ALU.mult).then_inc(kw_done, 1)
            for t in range(TL):
                pool.wait_ge(h_done, 2 * t + 2)
                pool.tensor_tensor(hq[:, t, :, :], hs[:, t, :, :], hs[:, t, :, :], ALU.mult).then_inc(sq_done, 1)
            for t in range(TL):
                pool.wait_ge(hn_done, t + 1)
                pool.tensor_tensor(hs[:, t, :, :].rearrange("p h v -> p (h v)"),
                                   hs[:, t, :, :].rearrange("p h v -> p (h v)"), k.o_ml[:, t, :],
                                   ALU.mult).then_inc(gated, 1)

        @block.tensor
        def _(pe):
            pe.wait_ge(lf_done, 1)
            for t in range(TT):
                for lhs, lo, n, at in ((k.upto, 0, 4, 0), (k.onward, 4, 4, 4), (k.ones, 0, 8, 8)):
                    mm = pe.matmul(ps[:, 7, t * 16 + at:t * 16 + at + n], lhs[:, :], lf[:, t, lo:lo + n],
                                   start=True, stop=True)
            mm.then_inc(cum_done, 1)
            pe.wait_ge(conv_done, 4)
            for n in range(3):
                for j in range(4):
                    t, blk = (4 * n + j) // 2, j % 2
                    mm = pe.transpose(ps[:, n, j * P:(j + 1) * P], conv[:, 2 + blk, t * P:(t + 1) * P], k.ident[:, :])
                mm.then_inc(k_turned, 1)
            for i in range(TT - 1):
                for d in range(2):
                    t = order[d][i]
                    pe.wait_ge(kw_done, 2 * i + d + 1)
                    if i:
                        pe.wait_ge(state_done, 2 * (i - 1) + d + 1)
                    for h in range(4):
                        q0 = 64 * (h % 2)
                        mm = pe.matmul(ps[q0:q0 + 64, 5 + d, (h // 2) * VW:(h // 2 + 1) * VW],
                                       kw[:, d, t, h * DQK:(h + 1) * DQK], k.v_ml[:, t, h, :], start=True, stop=True)
                    mm.then_inc(upd_ready, 1)

            def before(n):
                t, d = n // 2, n % 2
                if d == 0:
                    if t:
                        pe.wait_ge(w_done, 2 * t)
                    else:
                        pe.wait_ge(k_kept, 3)
                    for h in range(4):
                        q0 = 64 * (h % 2)
                        mm = pe.matmul(ps[:, h % 2, (h // 2) * P:(h // 2 + 1) * P],
                                       conv[q0:q0 + 64, 2 + h // 2, t * P:(t + 1) * P],
                                       conv[q0:q0 + 64, h // 2, t * P:(t + 1) * P], start=True, stop=True)
                    mm.then_inc(s_ready, 1)
                if n:
                    pe.wait_ge(exp_done, n)
                for h in range(4):
                    pe.matmul(ps[:, 2, h * P:(h + 1) * P], lf[:, t, 4 * d + h:4 * d + h + 1].to_broadcast([P, P]),
                              (k.onward if d else k.upto)[:, :], start=True, stop=False)
                    mm = pe.matmul(ps[:, 2, h * P:(h + 1) * P], k.ident[:, :],
                                   (k.neg_onward if d else k.neg_upto)[:, :], start=False, stop=True)
                mm.then_inc(e_ready, 1)
                i = order[d].index(t) - 1
                pe.wait_ge(state_done, 2 * (TT - 1))
                if n:
                    pe.wait_ge(inter_kept, n)
                for h in range(4):
                    q0 = 64 * (h % 2)
                    mm = pe.matmul(ps[:, 5 + h % 2, (h // 2) * VW:(h // 2 + 1) * VW],
                                   conv[q0:q0 + 64, h // 2, t * P:(t + 1) * P], Cs[q0:q0 + 64, d, i, h // 2, :],
                                   start=True, stop=True)
                mm.then_inc(inter_ready, 1)
            before(0)
            for n in range(2 * TL):
                if n + 1 < 2 * TL:
                    before(n + 1)
                pe.wait_ge(w_done, n + 1)
                if n:
                    pe.wait_ge(intra_used, n)
                for h in range(4):
                    mm = pe.matmul(ps[:, 3 + h // 2, (h % 2) * VW:(h % 2 + 1) * VW], Wt[n % 2][:, h, :],
                                   k.v_ml[:, n // 2, h, :], start=True, stop=True)
                mm.then_inc(intra_ready, 1)
            for t in range(TL):
                pe.wait_ge(gated, t + 1)
                for j in range(4):
                    mm = pe.transpose(ps[:, t, j * P:(j + 1) * P], hs[:, t, j, :], k.ident[:, :])
                mm.then_inc(a_turned, 1)

        @block.scalar
        def _(act):
            act.wait_ge(pads, 6)
            for b in range(4):
                if b >= 2:
                    act.wait_ge(conv_done, b - 1)
                act.activation(pad[b % 2][:, 1:1 + GRID_H, 1:1 + GRID_W],
                               k.qkT[:, b, 0:SEQ].rearrange("p (r w) -> p r w", w=GRID_W), ACT.Copy)
                act.activation(line[b % 2][:, 1:1 + CTX], k.qkT[:, b, SEQ:T], ACT.Copy).then_inc(raw_in, 1)
            act.wait_ge(pre_done, 1)
            act.activation(pre[:, :, :], pre[:, :, :], ACT.Tanh, scale=1.0 / GATE_CAP).then_inc(pre_t, 1)
            act.wait_ge(pre_t, 1)
            act.activation(lf[:, :, :], pre[:, :, 8:16], ACT.Exp, scale=-GATE_CAP).then_inc(soft, 1)
            act.wait_ge(soft, 2)
            act.activation(lf[:, :, :], lf[:, :, :], ACT.Ln).then_inc(soft, 1)
            for n in range(3):
                act.wait_ge(k_turned, n + 1)
                act.activation(kN[:, 2 * n:2 * n + 2, :].rearrange("p t c -> p (t c)"), ps[:, n, :], ACT.Copy)\
                   .then_inc(k_kept, 1)
            act.wait_ge(dec_done, 3)
            act.activation(eb[:, :, :], dec[:, :, 0:8], ACT.Exp).then_inc(exps_done, 1)
            act.activation(carry[:, :, :], dec[:, :, 8:16], ACT.Exp).then_inc(exps_done, 1)
            act.activation(wk[:, :, :], wk[:, :, :], ACT.Exp).then_inc(exps_done, 1)
            act.wait_ge(exps_done, 3)
            for n in range(2 * TL):
                t, d = n // 2, n % 2
                act.wait_ge(e_ready, n + 1)
                if n >= 2:
                    act.wait_ge(w_done, n - 1)
                for h in range(4):
                    ins = act.activation(E[n % 2][:, h, :], ps[:, 2, h * P:(h + 1) * P], ACT.Exp,
                                         bias=ib[:, t, 4 * d + h:4 * d + h + 1])
                ins.then_inc(exp_done, 1)
                act.wait_ge(inter_ready, n + 1)
                if n >= 2:
                    act.wait_ge(h_done, n - 1)
                for h in range(4):
                    ins = act.activation(tmp[n % 2][:, h, :], ps[:, 5 + h % 2, (h // 2) * VW:(h // 2 + 1) * VW],
                                         ACT.Copy, scale=eb[:, t, 4 * d + h:4 * d + h + 1])
                ins.then_inc(inter_kept, 1)
            act.wait_ge(ms_done, 1)
            act.activation(ms[:, :, :], ms[:, :, :], ACT.Sqrt).then_inc(rms_done, 1)
            for t in range(TL):
                act.wait_ge(a_turned, t + 1)
                for j in range(4):
                    act.activation(aT[:, j, t * P:(t + 1) * P], ps[:, t, j * P:(j + 1) * P], ACT.Copy,
                                   scale=norm_g[:, j:j + 1]).then_inc(a_kept, 1)

        @block.vector
        def _(dve):
            link = Chain(dve, dch)

            def gates():
                dve.wait_ge(soft, 1)
                dve.tensor_scalar(lf[:, :, :], lf[:, :, :], 1.0, None, ALU.add).then_inc(soft, 1)
                dve.wait_ge(soft, 3)
                dve.tensor_scalar(lf[:, :, :], lf[:, :, :], -1.0, None, ALU.mult).then_inc(lf_done, 1)
                dve.wait_ge(cum_done, 1)
                link(dve.tensor_copy(dec[:, :, :].rearrange("p t g -> p (t g)"), ps[:, 7, 0:16 * TT]))
                dve.scalar_tensor_tensor(ib[:, :, :], pre[:, :, 0:8], GATE_CAP, dec[:, :, 0:8], ALU.mult,
                                         ALU.subtract).then_inc(dec_done, 1)
                dve.wait_ge(dec_done, 1)
                dve.tensor_tensor(wk[:, :, :], ib[:, :, :], dec[:, :, 8:16], ALU.add).then_inc(dec_done, 1)
                dve.tensor_copy(den[:, :], dec[:, 0, 0:4]).then_inc(dec_done, 1)

            dve.wait_ge(small_in, 16 * 7)
            for b in range(4):
                s = b % 2
                dve.wait_ge(raw_in, b + 1)
                lat = conv[:, b, 0:SEQ].rearrange("p (r w) -> p r w", w=GRID_W)
                cx = conv[:, b, SEQ:T]
                for tap in range(9):
                    dy, dx = tap // 3, tap % 3
                    img = pad[s][:, dy:dy + GRID_H, dx:dx + GRID_W]
                    if tap == 0:
                        ins = dve.tensor_scalar(lat, img, taps[:, b, 0:1], conv_b[:, b:b + 1], ALU.mult, ALU.add)
                    else:
                        ins = dve.scalar_tensor_tensor(lat, img, taps[:, b, tap:tap + 1], lat, ALU.mult, ALU.add)
                    if b >= 2 and 3 <= tap < 6:
                        ln = line[s][:, dx:dx + CTX]
                        if tap == 3:
                            ins2 = dve.tensor_scalar(cx, ln, taps[:, b, 3:4], conv_b[:, b:b + 1], ALU.mult, ALU.add)
                        else:
                            ins2 = dve.scalar_tensor_tensor(cx, ln, taps[:, b, tap:tap + 1], cx, ALU.mult, ALU.add)
                        link(ins)
                        link(ins2)
                    else:
                        link(ins)
                if b >= 2:
                    ins = dve.tensor_scalar(conv[:, b, :], conv[:, b, :], DQK ** -0.5, None, ALU.mult)
                    ins.then_inc(conv_done, 1)
                else:
                    dve.tensor_copy(conv[:, b, SEQ:T], conv[:, b, 0:CTX]).then_inc(conv_done, 1)
                if b == 1:
                    gates()
            dve.wait_ge(exps_done, 3)
            for p in range(2):
                for half in range(2):
                    q = slice(64 * half, 64 * half + 64)
                    for d in range(2):
                        ins = dve.tensor_copy(carry2[q, :, d, p], carry[q, :, 4 * d + 2 * p + half])
            link(ins)
            for i in range(TT - 1):
                for d in range(2):
                    t = order[d][i]
                    dve.wait_ge(upd_ready, 2 * i + d + 1)
                    if i == 0:
                        ins = dve.tensor_copy(Cs[:, d, 0, :, :].rearrange("p a v -> p (a v)"), ps[:, 5 + d, 0:2 * VW])
                    else:
                        dve.wait_ge(state_done, 2 * (i - 1) + d + 1)
                        for p in range(2):
                            ins = dve.scalar_tensor_tensor(Cs[:, d, i, p, :], Cs[:, d, i - 1, p, :],
                                                           carry2[:, t, d, p:p + 1], ps[:, 5 + d, p * VW:(p + 1) * VW],
                                                           ALU.mult, ALU.add)
                    ins.then_inc(state_done, 1)

            def weigh(n):
                t = n // 2
                dve.wait_ge(s_ready, t + 1)
                dve.wait_ge(exp_done, n + 1)
                if n >= 2:
                    dve.wait_ge(intra_ready, n - 1)
                for par in range(2):
                    ins = dve.tensor_tensor(Wt[n % 2][:, par::2, :], ps[:, par, 0:2 * P].rearrange("p (a t) -> p a t", a=2),
                                            E[n % 2][:, par::2, :], ALU.mult)
                ins.then_inc(w_done, 1)
            weigh(0)
            for n in range(2 * TL):
                if n + 1 < 2 * TL:
                    weigh(n + 1)
                t, d = n // 2, n % 2
                x = tmp[n % 2]
                dve.wait_ge(intra_ready, n + 1)
                dve.wait_ge(inter_kept, n + 1)
                for a in range(2):
                    ins = dve.tensor_tensor(x[:, 2 * a:2 * a + 2, :], x[:, 2 * a:2 * a + 2, :],
                                            ps[:, 3 + a, 0:2 * VW].rearrange("p (a v) -> p a v", a=2), ALU.add)
                ins.then_inc(intra_used, 1)
                dve.wait_ge(intra_used, n + 1)
                link(dve.scalar_tensor_tensor(den[:, :], x[:, :, DV], -1.0, x[:, :, DV], ALU.mult, ALU.max))
                link(dve.tensor_scalar(den2[:, :], den[:, :], 1.0, None, ALU.max))
                link(dve.reciprocal(den[:, :], den2[:, :]))
                for h in range(4):
                    if d == 0:
                        ins = dve.tensor_scalar(hs[:, t, h, :], x[:, h, 0:DV], den[:, h:h + 1], None, ALU.mult)
                    else:
                        ins = dve.scalar_tensor_tensor(hs[:, t, h, :], x[:, h, 0:DV], den[:, h:h + 1],
                                                       hs[:, t, h, :], ALU.mult, ALU.add)
                ins.then_inc(h_done, 1)
                dve.wait_ge(h_done, n + 1)
            dve.wait_ge(sq_done, TL)
            link(dve.tensor_reduce(ms[:, :, :], hq[:, :, :, :], AX.X, ALU.add))
            dve.tensor_scalar(ms[:, :, :], ms[:, :, :], 1.0 / DV, EPS, ALU.mult, ALU.add).then_inc(ms_done, 1)
            dve.wait_ge(rms_done, 1)
            link(dve.reciprocal(hq[:, 0, 0, 0:4 * TL], ms[:, :, :].rearrange("p t h -> p (t h)")))
            for t in range(TL):
                dve.tensor_tensor(hs[:, t, :, :], hs[:, t, :, :], bc(hq[:, 0, 0, 4 * t:4 * t + 4], DV), ALU.mult)\
                   .then_inc(hn_done, 1)


CTX_GROUP = 2
NG = NC // 4
LEVELS = [2, 4, 8, 16, 32]
NV_ = 10
V_KK, V_HKA, V_1HKA, V_RK, V_W0, V_A0 = 0, 1, 2, 3, 4, 6


def rwkv_keys(nc, k):
    ctx = ExitStack()
    with ctx:
        def sb(name, shape):
            return ctx.enter_context(nc.sbuf_tensor(name, shape, F32))
        kT, sq = sb("kT_all", [P, 4, T]), sb("ksq_all", [P, 4, T])
        kn = sb("kk_all", [P, 4, T])
        k_k = sb("k_k", [P, 4])
        ps = k.ps
        k_in, sq_done, sum_done, nrm, rooted, kk_done, kk_out, dch = (
            k.sem(n) for n in ("k_in", "ksq_done", "ksum_done", "knrm", "k_rooted", "kk_done", "kk_out", "kk_dve"))
        block = ctx.enter_context(nc.Block())

        @block.sync
        def _(sp):
            with nc.allow_non_contiguous_dma(reason="a vector over partitions"):
                sp.dma_start(k_k[:, :], k.w["rw_k_k"][0].rearrange("(b p) -> p b", p=P)).then_inc(k_in, 16)
            sp.dma_start(kT[:, :, :], k.rw_d[4:8].rearrange("b p t -> p b t")).then_inc(k_in, 16)
            sp.wait_ge(kk_done, 4)
            sp.dma_start(k.kk_d.rearrange("b p t -> p b t"), kn[:, :, :]).then_inc(kk_out, 16)
            sp.wait_ge(kk_out, 16)

        @block.scalar
        def _(act):
            act.wait_ge(k_in, 32)
            for b in range(4):
                act.activation(sq[:, b, :], kT[:, b, :], ACT.Square, scale=k_k[:, b:b + 1]).then_inc(sq_done, 1)
            act.wait_ge(nrm, 8)
            act.activation(sq[:, :, :], sq[:, :, :], ACT.Sqrt).then_inc(rooted, 1)

        @block.tensor
        def _(pe):
            for b in range(4):
                pe.wait_ge(sq_done, b + 1)
                for lo, n, j in ((0, SEQ, 0), (SEQ, CTX, 1)):
                    mm = pe.matmul(ps[:, 2 * b + j, 0:n], k.same_head[:, :], sq[:, b, lo:lo + n], start=True, stop=True)
                mm.then_inc(sum_done, 1)

        @block.vector
        def _(dve):
            for b in range(4):
                dve.wait_ge(sum_done, b + 1)
                for lo, n, j in ((0, SEQ, 0), (SEQ, CTX, 1)):
                    dve.tensor_scalar(sq[:, b, lo:lo + n], ps[:, 2 * b + j, 0:n], 1e-12, None, ALU.add).then_inc(nrm, 1)
            dve.wait_ge(rooted, 1)
            link = Chain(dve, dch)
            link(dve.reciprocal(kn[:, :, :], sq[:, :, :]))
            for b in range(4):
                dve.scalar_tensor_tensor(kn[:, b, :], kT[:, b, :], k_k[:, b:b + 1], kn[:, b, :], ALU.mult, ALU.mult)\
                   .then_inc(kk_done, 1)


def rwkv_masks(nc, k):
    with nc.Block() as block:
        made = k.sem("rw_mask_made")
        sel = k.sem("rw_mask_cut")
        half = (slice(0, 64), slice(64, 128))

        @block.gpsimd
        def _(pool):
            n = 0
            for d in range(2):
                for i in range(6):
                    pool.memset(k.join[:, d, i, :], 0.0).then_inc(made, 1)
                    n += 1
            pool.memset(k.reset[:, :, :], 1.0).then_inc(made, 1)
            pool.memset(k.same_head[:, :], 0.0).then_inc(made, 1)
            n += 2
            pool.wait_ge(made, n)
            for q in half:
                pool.memset(k.same_head[q, q], 1.0).then_inc(made, 1)
                n += 1
                pool.wait_ge(made, n)
            pool.memset(k.reset[:, :, 0:1], 0.0).then_inc(made, 1)
            n += 1
            for d in range(2):
                for i in range(6):
                    b = 1 << i
                    v = k.join[:, d, i, :].rearrange("p (q two s) -> p q two s", two=2, s=b)[:, :, d, :]
                    pool.memset(v, 1.0).then_inc(made, 1)
                    n += 1
                    pool.wait_ge(made, n)
                    lo = 0 if d else b
                    pool.affine_select(out=v, in_=v, compare_op=ALU.is_ge, fill=0.0, base=-lo,
                                       pattern=[[-2 * b, 64 // b], [0, b]], channel_multiplier=1).then_inc(made, 1)
                    n += 1
                    pool.wait_ge(made, n)
                    pool.affine_select(out=v, in_=v, compare_op=ALU.is_ge, fill=0.0, base=lo + b - 1,
                                       pattern=[[2 * b, 64 // b], [0, b]], channel_multiplier=-1).then_inc(made, 1)
                    n += 1
            pool.wait_ge(made, n)

        @block.vector
        def _(dve):
            for d in range(2):
                incl, other = (k.onward, k.upto) if d else (k.upto, k.onward)
                for q in half:
                    dve.tensor_scalar(k.cut[q, d, 0, :], other[q, q], -1.0, 1.0, ALU.mult, ALU.add).then_inc(sel, 1)
                    dve.tensor_copy(k.cut[q, d, 1, :], incl[q, q]).then_inc(sel, 1)
            dve.wait_ge(sel, 8)


def rwkv(nc, k):
    ctx = ExitStack()
    with ctx:
        def sb(name, shape):
            return ctx.enter_context(nc.sbuf_tensor(name, shape, F32))
        E_, O_ = slice(0, 64), slice(64, 128)
        wd_t, ad = sb("wd_t", [P, T]), sb("ad", [P, T])
        w_up, a_up = sb("w_up_b", [P, P]), sb("a_up_b", [P, P])
        vec = sb("rw_vec", [P, 4 * NV_])
        vec3 = vec[:, :].rearrange("p (b n) -> p b n", b=4)
        rT, kT, vT, kk = sb("rT_b", [P, SEQ]), sb("kT_b", [P, T]), sb("vT_b", [P, T]), sb("kk_b", [P, T])
        th_w, th_a = sb("th_w", [P, T]), sb("th_a", [P, T])
        cum, cumx = sb("cum", [P, T]), sb("cumx", [P, T])
        e_inc, e_neg, e_exc = sb("e_inc", [P, T]), sb("e_neg", [P, T]), sb("e_exc", [P, T])
        kf, nb = sb("k_factor", [P, T]), sb("minus_b", [P, T])
        kd_sum = sb("kd_sum", [P, SEQ])
        rk_head = sb("rk_head", [P, P])
        AR = sb("AR", [P, NC, 2, C])
        BKB = sb("BKB", [P, NC, 3, C])
        BKn = sb("BK_rows", [P, NC, 2, C])
        mva = sb("MV_A", [P, NC, 2, C])
        LT, Tm, Um, X = (sb(n, [P, NC, P]) for n in ("LT", "Tm", "Um", "Xm"))
        GA = sb("GA", [P, NC, 2, C])
        TA = sb("TA", [P, NC, P])
        BP = sb("BP", [P, NC, 2, C])
        vz = sb("v_rows", [P, NC, 2, C])
        GR = [sb(f"GR{d}", [P, NCL, 2, C]) for d in range(2)]
        sv = [sb(f"sa_v{d}", [P, NC, 2, C]) for d in range(2)]
        GT = [sb(f"GT{d}", [P, NC, P]) for d in range(2)]
        RT = [sb(f"RT{d}", [P, NCL, P]) for d in range(2)]
        Hg = [sb(f"Hg{d}", [P, NC, C]) for d in range(2)]
        S = [sb(f"S{d}", [P, NC, C]) for d in range(2)]
        gam = [sb(f"gam{d}", [P, NC]) for d in range(2)]
        y_sb, bon = sb("y_sb", [P, SEQ]), sb("bonus", [P, SEQ])
        ps = k.ps
        names = ("rw_static rw_vec_done up_in key_in v_in th_done lora_done v_turned v_kept scan_done cum_done exps "
                 "dve_prep pool_prep s1_ready s1_kept tr_ready tr_kept lt_done u0_done t0_ready t0_kept mv_ready mv_kept "
                 "x_ready x_kept tu_ready tu_kept tm_ready pool_half sa_kept ta_kept gr_ready gr_kept hh_ready hh_kept "
                 "step_ready step_done y_ready y_kept y_out bonus_in bonus_ready bonus_kept bonus_out zeroed rw_dve").split()
        s = {n: k.sem("r_" + n) for n in names}
        order = [[8, 9, 10, 11, 0, 1, 2, 3, 4, 5, 6, 7], [11, 10, 9, 8, 7, 6, 5, 4, 3, 2, 1, 0]]
        MV_BANK, TM_BANK = (6, 7, 5), (6, 7, 0)
        steps = NC - 2

        def grp(g):
            return slice(4 * g, 4 * g + 4)

        def bank(i, n=128):
            return ps[:, i, 0:4 * n].rearrange("p (c x) -> p c x", c=4)

        def col(b, j):
            return vec[:, bass.ds(b * NV_ + j, 1)]
        block = ctx.enter_context(nc.Block())

        def out_prev(sp, b):
            sp.wait_ge(s["y_kept"], b + 1)
            sp.dma_start(k.y_d[bass.ds(b, 1)].rearrange("a p t -> p (a t)"), y_sb[:, :]).then_inc(s["y_out"], 16)
            sp.wait_ge(s["bonus_kept"], b + 1)
            sp.dma_start(k.bonus_d[bass.ds(b, 1)].rearrange("a p t -> p (a t)"), bon[:, :]).then_inc(s["bonus_out"], 16)

        @block.sync
        def _(sp):
            sp.dma_start(wd_t[:, :], k.rw_d[12]).then_inc(s["rw_static"], 16)
            sp.dma_start(ad[:, :], k.rw_d[13]).then_inc(s["rw_static"], 16)
            with nc.allow_non_contiguous_dma(reason="vectors over partitions"):
                for j, src in ((V_HKA, k.w["rw_k_a"][0]), (V_RK, k.w["rw_r_k"][0].rearrange("h n -> (h n)")),
                               (V_W0, k.w["rw_w0"][0, 0]), (V_W0 + 1, k.w["rw_w0"][0, 1]),
                               (V_A0, k.w["rw_a0"][0, 0]), (V_A0 + 1, k.w["rw_a0"][0, 1])):
                    sp.dma_start(vec3[:, :, j], src.rearrange("(b p) -> p b", p=P)).then_inc(s["rw_static"], 16)
            for b in rounds(sp, 4):
                wait(sp, s["lora_done"], 2 * b)
                for src, dst in ((k.w["rw_w_up"], w_up), (k.w["rw_a_up"], a_up)):
                    sp.dma_start(dst[:, :], src[0].rearrange("d r (b c) -> b (d r) c", c=P)[bass.ds(b, 1)]
                                 .rearrange("a r c -> r (a c)")).then_inc(s["up_in"], 16)
                wait(sp, s["dve_prep"], 2 * b)
                wait(sp, s["pool_prep"], 2 * b)
                for src, dst, n in ((k.rw_d[bass.ds(b, 1), :, 0:SEQ], rT, SEQ), (k.rw_d[bass.ds(b + 4, 1)], kT, T),
                                    (k.kk_d[bass.ds(b, 1)], kk, T)):
                    sp.dma_start(dst[:, :], src.rearrange("a p t -> p (a t)")).then_inc(s["key_in"], 16)
                wait(sp, s["bonus_kept"], b)
                sp.dma_start(vT[:, :], k.rw_d[bass.ds(b + 8, 1)].rearrange("a p t -> p (a t)")).then_inc(s["v_in"], 16)
                if isinstance(b, int) and b == 0:
                    continue
                out_prev(sp, b - 1)
            out_prev(sp, 3)
            sp.wait_ge(s["y_out"], 64)
            sp.wait_ge(s["bonus_out"], 64)

        @block.tensor
        def _(pe):
            pe.wait_ge(s["rw_vec_done"], 2)
            pe.wait_ge(s["zeroed"], 7)
            for b in rounds(pe, 4):
                for d in range(2):
                    u = 2 * b + d
                    D_ = E_ if d == 0 else O_
                    wait(pe, s["gr_kept"], NG * u)
                    wait(pe, s["hh_kept"], NG * u)
                    pe.wait_ge(s["up_in"], 32 * b + 32)
                    for j, (up, src) in enumerate(((w_up, wd_t), (a_up, ad))):
                        pe.matmul(ps[:, 2 * j, 0:SEQ], up[D_, :], src[D_, 0:SEQ], start=True, stop=True)
                        mm = pe.matmul(ps[:, 2 * j + 1, 0:CTX], up[D_, :], src[D_, SEQ:T], start=True, stop=True)
                    mm.then_inc(s["lora_done"], 1)
                    if d == 0:
                        wait(pe, s["y_kept"], b)
                        pe.wait_ge(s["v_in"], 16 * b + 16)
                        pe.nop(nofuse=True)
                        for g in range(NG):
                            for c in range(4):
                                t0 = (4 * g + c) * C
                                mm = pe.transpose(ps[0:64, 4 + g, c * P:(c + 1) * P], vT[:, t0:t0 + C], k.ident[:, :])
                            mm.then_inc(s["v_turned"], 1)
                        pe.wait_ge(s["v_kept"], NG * b + NG)
                    pe.wait_ge(s["dve_prep"], u + 1)
                    pe.wait_ge(s["pool_prep"], u + 1)
                    for g in range(NG):
                        n = 64 if g == CTX_GROUP else 128
                        pe_b = 4 * (g % 2)
                        if g == 2:
                            pe.wait_ge(s["s1_kept"], NG * u + 1)
                            pe.wait_ge(s["tr_kept"], NG * u + 1)
                        for c in range(4):
                            cc = 4 * g + c
                            for hh, (q, lo) in enumerate(((E_, 0), (O_, 1))):
                                mm = pe.matmul(ps[:, pe_b + hh, c * n:(c + 1) * n], BKB[q, cc, lo:lo + 2, :],
                                               AR[q, cc, 0:n // 64, :], start=True, stop=True)
                        mm.then_inc(s["s1_ready"], 1)
                        for hh, (q, lo) in enumerate(((E_, 0), (O_, 1))):
                            for c in range(4):
                                pe.transpose(ps[:, pe_b + 2 + hh, c * C:(c + 1) * C], BKB[q, 4 * g + c, lo:lo + 2, :],
                                             k.ident[q, q])
                        for c in range(4):
                            at = 256 + (c % 2) * P
                            mm = pe.transpose(ps[0:64, pe_b + 2 + c // 2, at:at + P], AR[:, 4 * g + c, 0, :], k.ident[:, :])
                        mm.then_inc(s["tr_ready"], 1)
                    pe.wait_ge(s["s1_kept"], NG * u + NG)
                    pe.wait_ge(s["tr_kept"], NG * u + NG)
                    for g in range(NG):
                        for c in range(4):
                            cc = 4 * g + c
                            for hh, q in enumerate((E_, O_)):
                                at = c * C
                                mm = pe.matmul(ps[q, MV_BANK[g], at:at + C], GA[:, cc, hh, :], vz[:, cc, hh, :],
                                               start=True, stop=True)
                        mm.then_inc(s["mv_ready"], 1)
                    for g in range(NG):
                        pe.wait_ge(s["u0_done"], NG * u + g + 1)
                        for c in range(4):
                            mm = pe.transpose(ps[:, g, c * P:(c + 1) * P], Um[:, 4 * g + c, :], k.ident[:, :])
                        mm.then_inc(s["t0_ready"], 1)
                    NX = NG * len(LEVELS)
                    for l in range(len(LEVELS)):
                        for g in range(NG):
                            n = NG * l + g
                            if l == 0:
                                pe.wait_ge(s["t0_kept"], NG * u + (NG if g == 0 else g + 1))
                            else:
                                pe.wait_ge(s["tu_kept"], NX * u + n - NG + 1)
                            if n >= 2:
                                pe.wait_ge(s["x_kept"], NX * u + n - 1)
                            for c in range(4):
                                mm = pe.matmul(ps[:, n % 2, c * P:(c + 1) * P], LT[:, 4 * g + c, :], Tm[:, 4 * g + c, :],
                                               start=True, stop=True)
                            mm.then_inc(s["x_ready"], 1)
                        for g in range(NG):
                            n = NG * l + g
                            pe.wait_ge(s["x_kept"], NX * u + n + 1)
                            if n >= 2:
                                pe.wait_ge(s["tu_kept"], NX * u + n - 1)
                            bt = 2 + 2 * (n % 2)
                            for c in range(4):
                                cc = 4 * g + c
                                if l < len(LEVELS) - 1:
                                    pe.matmul(ps[:, bt, c * P:(c + 1) * P], Um[:, cc, :], X[:, cc, :], start=True, stop=True)
                                mm = pe.matmul(ps[:, bt + 1, c * P:(c + 1) * P], X[:, cc, :], Um[:, cc, :],
                                               start=True, stop=True)
                            mm.then_inc(s["tu_ready"], 1)
                    pe.wait_ge(s["mv_kept"], NG * u + NG)
                    for g in range(NG):
                        pe.wait_ge(s["tu_kept"], NX * u + NX - NG + g + 1)
                        for c in range(4):
                            cc = 4 * g + c
                            mm = pe.matmul(ps[:, TM_BANK[g], c * P:(c + 1) * P], Um[:, cc, :],
                                           mva[:, cc, :, :], start=True, stop=True)
                        mm.then_inc(s["tm_ready"], 1)
                    pe.wait_ge(s["pool_half"], POOL_HALVES * b + 6 * d + 6)
                    for g in range(NG):
                        n = 1 if g == CTX_GROUP else 2
                        pe.wait_ge(s["ta_kept"], NG * u + g + 1)
                        for c in range(4):
                            cc = 4 * g + c
                            mm = pe.matmul(ps[:, 1 + g, c * P:c * P + 64 * n], TA[:, cc, :], BP[:, cc, 0:n, :],
                                           start=True, stop=True)
                        mm.then_inc(s["gr_ready"], 1)
                        pe.wait_ge(s["sa_kept"], NG * u + g + 1)
                        for c in range(4):
                            cc = 4 * g + c
                            at = c * C
                            for hh, q in enumerate((E_, O_)):
                                mm = pe.matmul(ps[q, 4 + g, at:at + C], BKn[:, cc, hh, :], sv[d][:, cc, hh, :],
                                               start=True, stop=True)
                        mm.then_inc(s["hh_ready"], 1)
                pe.wait_ge(s["gr_kept"], NG * (2 * b + 2))
                pe.wait_ge(s["hh_kept"], NG * (2 * b + 2))
                for i in range(1, steps + 1):
                    for d in range(2):
                        if i > 1:
                            pe.wait_ge(s["step_done"], 2 * steps * b + 2 * (i - 2) + d + 1)
                        before = Hg[d][:, order[d][0], :] if i == 1 else S[d][:, i - 1, :]
                        pe.matmul(ps[:, 4 + d, 0:C], GT[d][:, order[d][i], :], before,
                                  start=True, stop=True).then_inc(s["step_ready"], 1)
                pe.wait_ge(s["step_done"], 2 * steps * b + 2 * steps)
                for c in range(NCL):
                    out = ps[:, 6, c * C:(c + 1) * C]
                    for d in range(2):
                        pe.matmul(out, RT[d][:, c, :], S[d][:, order[d].index(c) - 1, :], start=(d == 0), stop=False)
                    for d in range(2):
                        for hh, q in enumerate((E_, O_)):
                            mm = pe.matmul(ps[q, 6, c * C:(c + 1) * C], GR[d][:, c, hh, :], sv[d][:, c, hh, :],
                                           start=False, stop=(d == 1))
                mm.then_inc(s["y_ready"], 1)
                pe.wait_ge(s["bonus_in"], b + 1)
                pe.matmul(ps[:, 7, :], rk_head[:, :], kd_sum[:, :], start=True, stop=True).then_inc(s["bonus_ready"], 1)

        @block.scalar
        def _(act):
            act.wait_ge(s["rw_static"], 16 * 8)
            act.activation(wd_t[:, :], wd_t[:, :], ACT.Tanh).then_inc(s["rw_vec_done"], 1)
            act.wait_ge(s["rw_vec_done"], 2)
            for b in rounds(act, 4):
                for d in range(2):
                    u = 2 * b + d
                    act.wait_ge(s["lora_done"], u + 1)
                    for j, (th, v0) in enumerate(((th_w, V_W0), (th_a, V_A0))):
                        act.activation(th[:, 0:SEQ], ps[:, 2 * j, 0:SEQ], ACT.Tanh, scale=0.5, bias=col(b, v0 + d))
                        act.activation(th[:, SEQ:T], ps[:, 2 * j + 1, 0:CTX], ACT.Tanh, scale=0.5, bias=col(b, v0 + d))\
                           .then_inc(s["th_done"], 1)
                    if d == 0:
                        for g in range(NG):
                            act.wait_ge(s["v_turned"], NG * b + g + 1)
                            pv = ps[0:64, 4 + g, :].rearrange("p (c x) -> p c x", c=4)
                            act.activation(vz[O_, grp(g), 0, :], pv[:, :, 0:64], ACT.Copy)
                            act.activation(vz[E_, grp(g), 1, :], pv[:, :, 64:128], ACT.Copy).then_inc(s["v_kept"], 1)
                    act.wait_ge(s["cum_done"], 2 * u + 1)
                    act.activation(e_neg[:, :], cum[:, :], ACT.Exp, scale=KAPPA).then_inc(s["exps"], 1)
                    act.activation(e_inc[:, :], cum[:, :], ACT.Exp, scale=-KAPPA).then_inc(s["exps"], 1)
                    act.wait_ge(s["cum_done"], 2 * u + 2)
                    act.activation(e_exc[:, :], cumx[:, :], ACT.Exp, scale=-KAPPA).then_inc(s["exps"], 1)
                    for g in range(NG):
                        act.wait_ge(s["tr_ready"], NG * u + g + 1)
                        pb = 4 * (g % 2)
                        for j in range(2):
                            act.activation(BKn[:, grp(g), j, :], ps[:, pb + 2 + j, 0:256].rearrange("p (c x) -> p c x", c=4),
                                           ACT.Copy)
                            pa = ps[0:64, pb + 2 + j, 256:512].rearrange("p (c h x) -> p c h x", c=2, h=2)
                            cs = slice(4 * g + 2 * j, 4 * g + 2 * j + 2)
                            act.activation(mva[E_, cs, 1, :], pa[:, :, 0, :], ACT.Copy)
                            ins = act.activation(mva[O_, cs, 1, :], pa[:, :, 1, :], ACT.Copy)
                        ins.then_inc(s["tr_kept"], 1)
                    for g in range(NG):
                        act.wait_ge(s["mv_ready"], NG * u + g + 1)
                        act.activation(mva[:, grp(g), 0, :], bank(MV_BANK[g], C),
                                       ACT.Copy).then_inc(s["mv_kept"], 1)
                    for g in range(NG):
                        act.wait_ge(s["t0_ready"], NG * u + g + 1)
                        act.activation(Tm[:, grp(g), :], bank(g), ACT.Copy).then_inc(s["t0_kept"], 1)
                    act.wait_ge(s["pool_half"], POOL_HALVES * b + 6 * d + 2)
                    for g in range(NG):
                        act.wait_ge(s["ta_kept"], NG * u + g + 1)
                        tm = bank(TM_BANK[g])
                        act.activation(sv[d][E_, grp(g), 0, :], tm[E_, :, 0:64], ACT.Copy)
                        act.activation(sv[d][O_, grp(g), 1, :], tm[O_, :, 0:64], ACT.Copy).then_inc(s["sa_kept"], 1)
                act.wait_ge(s["y_ready"], b + 1)
                wait(act, s["y_out"], 16 * b)
                act.activation(y_sb[:, :], ps[:, 6, :], ACT.Copy).then_inc(s["y_kept"], 1)

        @block.gpsimd
        def _(pool):
            for m in (LT, TA, GT[0], GT[1], RT[0], RT[1]):
                pool.memset(m[:, :, :], 0.0).then_inc(s["zeroed"], 1)
            pool.memset(vz[:, :, :, :], 0.0).then_inc(s["zeroed"], 1)
            for b in rounds(pool, 4):
                count = [0]

                def alone(ins):
                    count[0] += 1
                    ins.then_inc(s["pool_half"], 1)
                    pool.wait_ge(s["pool_half"], POOL_HALVES * b + count[0])
                for d in range(2):
                    u = 2 * b + d
                    wait(pool, s["gr_kept"], NG * u)
                    if d == 0:
                        pool.wait_ge(s["key_in"], 48 * b + 48)
                    pool.wait_ge(s["exps"], 3 * u + 2)
                    pool.tensor_tensor(AR[:, 0:NCL, 1, :], rT[:, :].rearrange("p (c x) -> p c x", x=C),
                                       e_inc[:, 0:SEQ].rearrange("p (c x) -> p c x", x=C), ALU.mult)
                    pool.wait_ge(s["exps"], 3 * u + 3)
                    pool.tensor_tensor(AR[:, :, 0, :], kk[:, :].rearrange("p (c x) -> p c x", x=C),
                                       e_exc[:, :].rearrange("p (c x) -> p c x", x=C), ALU.mult).then_inc(s["pool_prep"], 1)
                    pool.wait_ge(s["pool_prep"], u + 1)
                    if d == 0:
                        pool.wait_ge(s["v_kept"], NG * b + NG)
                        wait(pool, s["y_ready"], b)
                    pool.nop(nofuse=True)
                    alone(pool.tensor_copy(sv[d][O_, :, 0, :], vz[O_, :, 0, :]))
                    pool.nop(nofuse=True)
                    alone(pool.tensor_copy(sv[d][E_, :, 1, :], vz[E_, :, 1, :]))
                    pool.wait_ge(s["s1_kept"], NG * u + NG)
                    pool.wait_ge(s["tr_kept"], NG * u + NG)
                    for dst, src in ((BP[E_, 0:NCL, 1, :], GR[d][E_, :, 0, :]), (BP[O_, 0:NCL, 1, :], GR[d][O_, :, 1, :]),
                                     (BP[E_, :, 0, :], BKn[E_, :, 0, :]), (BP[O_, :, 0, :], BKn[O_, :, 1, :])):
                        pool.nop(nofuse=True)
                        alone(pool.tensor_copy(dst, src))
                assert count[0] == POOL_HALVES

        @block.vector
        def _(dve):
            link = Chain(dve, s["rw_dve"])
            dve.wait_ge(s["rw_static"], 16 * 8)
            for j in (V_HKA, V_W0, V_W0 + 1, V_A0, V_A0 + 1):
                link(dve.tensor_scalar(vec3[:, :, j], vec3[:, :, j], 0.5, None, ALU.mult))
            dve.tensor_scalar(vec3[:, :, V_1HKA], vec3[:, :, V_HKA], -1.0, 1.0, ALU.mult, ALU.add).then_inc(s["rw_vec_done"], 1)
            dve.wait_ge(s["rw_vec_done"], 2)
            for b in rounds(dve, 4):
                count = [0]

                def then(ins):
                    count[0] += 1
                    ins.then_inc(s["scan_done"], 1)
                    dve.wait_ge(s["scan_done"], PER * b + count[0])
                for d in range(2):
                    u = 2 * b + d
                    if d == 0:
                        dve.wait_ge(s["key_in"], 48 * b + 48)
                        wait(dve, s["bonus_ready"], b)
                        then(dve.tensor_scalar(rk_head[:, :], k.same_head[:, :], col(b, V_RK), None, ALU.mult))
                    dve.wait_ge(s["th_done"], 2 * u + 1)
                    then(dve.tensor_scalar(th_w[:, :], th_w[:, :], 0.5, 0.5, ALU.mult, ALU.add))
                    st = slice(None, None, -1) if d else slice(None)
                    rs = k.reset[:, :, :].rearrange("p c x -> p (c x)")
                    ins = dve.tensor_tensor_scan(cum[:, st], rs, th_w[:, st], 0.0, ALU.mult, ALU.add)
                    ins.then_inc(s["cum_done"], 1)
                    dve.wait_ge(s["cum_done"], 2 * u + 1)
                    dve.tensor_tensor(cumx[:, :], cum[:, :], th_w[:, :], ALU.subtract).then_inc(s["cum_done"], 1)
                    dve.wait_ge(s["th_done"], 2 * u + 2)
                    dve.tensor_scalar(kf[:, :], th_a[:, :], col(b, V_HKA), col(b, V_1HKA), ALU.mult, ALU.add)
                    then(dve.tensor_scalar(nb[:, :], th_a[:, :], -0.5, -0.5, ALU.mult, ALU.add))
                    dve.tensor_tensor(kf[:, :], kf[:, :], kT[:, :], ALU.mult)
                    then(dve.tensor_tensor(nb[:, :], nb[:, :], kk[:, :], ALU.mult))
                    if d == 0:
                        dve.tensor_copy(kd_sum[:, :], kf[:, 0:SEQ])
                    else:
                        then(dve.tensor_tensor(kd_sum[:, :], kd_sum[:, :], kf[:, 0:SEQ], ALU.add))
                        dve.tensor_tensor(kd_sum[:, :], kd_sum[:, :], rT[:, :], ALU.mult).then_inc(s["bonus_in"], 1)
                    dve.wait_ge(s["exps"], 3 * u + 1)
                    en = e_neg[:, :].rearrange("p (c x) -> p c x", x=C)
                    nb3, kf3 = (a[:, :].rearrange("p (c x) -> p c x", x=C) for a in (nb, kf))
                    dve.tensor_tensor(BKB[:, :, 0, :], nb3, en, ALU.mult)
                    dve.tensor_tensor(BKB[:, :, 2, :], nb3, en, ALU.mult)
                    dve.tensor_tensor(BKB[:, :, 1, :], kf3, en, ALU.mult)
                    dve.wait_ge(s["exps"], 3 * u + 2)
                    end = 0 if d else C - 1
                    then(dve.tensor_copy(gam[d][:, :], e_inc[:, :].rearrange("p (c x) -> p c x", x=C)[:, :, end]))
                    dve.tensor_copy(gam[d][:, 0:1], gam[d][:, 0:1]).then_inc(s["dve_prep"], 1)
                    for g in range(NG):
                        dve.wait_ge(s["s1_ready"], NG * u + g + 1)
                        pb = 4 * (g % 2)
                        n = 64 if g == CTX_GROUP else 128
                        for hh in range(2):
                            v = bank(pb + hh, n)
                            ins = dve.tensor_tensor(GA[:, grp(g), hh, :], v[:, :, 0:64],
                                                    k.cut[:, d, 0, :].unsqueeze(1).to_broadcast([P, 4, 64]), ALU.mult)
                            if n == 128:
                                ins = dve.tensor_tensor(GR[d][:, grp(g), hh, :], v[:, :, 64:128],
                                                        k.cut[:, d, 1, :].unsqueeze(1).to_broadcast([P, 4, 64]), ALU.mult)
                        ins.then_inc(s["s1_kept"], 1)
                        dve.wait_ge(s["s1_kept"], NG * u + g + 1)
                        dve.tensor_copy(LT[E_, grp(g), 0:64], GA[E_, grp(g), 0, :])
                        then(dve.tensor_copy(LT[O_, grp(g), 64:128], GA[O_, grp(g), 1, :]))
                        then(dve.tensor_tensor(Um[:, grp(g), :], LT[:, grp(g), :],
                                               k.join[:, 1 - d, 0, :].unsqueeze(1).to_broadcast([P, 4, P]), ALU.mult))
                        dve.tensor_tensor(Um[:, grp(g), :], Um[:, grp(g), :],
                                          k.ident[:, :].unsqueeze(1).to_broadcast([P, 4, P]), ALU.add).then_inc(s["u0_done"], 1)
                    NX = NG * len(LEVELS)
                    for l in range(len(LEVELS)):
                        for g in range(NG):
                            n = NG * l + g
                            dve.wait_ge(s["x_ready"], NX * u + n + 1)
                            dve.tensor_tensor(X[:, grp(g), :], bank(n % 2),
                                              k.join[:, d, l + 1, :].unsqueeze(1).to_broadcast([P, 4, P]), ALU.mult)\
                               .then_inc(s["x_kept"], 1)
                        for g in range(NG):
                            n = NG * l + g
                            bt = 2 + 2 * (n % 2)
                            dve.wait_ge(s["tu_ready"], NX * u + n + 1)
                            if l < len(LEVELS) - 1:
                                dve.tensor_tensor(Tm[:, grp(g), :], Tm[:, grp(g), :], bank(bt), ALU.add)
                            dve.tensor_tensor(Um[:, grp(g), :], Um[:, grp(g), :], bank(bt + 1), ALU.add)\
                               .then_inc(s["tu_kept"], 1)
                    for g in range(NG):
                        dve.wait_ge(s["tm_ready"], NG * u + g + 1)
                        tm = bank(TM_BANK[g])
                        dve.tensor_copy(TA[E_, grp(g), 0:64], tm[E_, :, 64:128])
                        dve.tensor_copy(TA[O_, grp(g), 64:128], tm[O_, :, 64:128]).then_inc(s["ta_kept"], 1)
                    for g in range(NG):
                        dve.wait_ge(s["gr_ready"], NG * u + g + 1)
                        v = bank(1 + g)
                        for q in (E_, O_):
                            ins = dve.tensor_tensor(GT[d][q, grp(g), q], v[q, :, 0:64],
                                                    k.ident[q, q].unsqueeze(1).to_broadcast([64, 4, 64]), ALU.add)
                            if g != CTX_GROUP:
                                ins = dve.tensor_tensor(RT[d][q, grp(g), q], v[q, :, 64:128], AR[q, grp(g), 1, :], ALU.add)
                        ins.then_inc(s["gr_kept"], 1)
                        dve.wait_ge(s["hh_ready"], NG * u + g + 1)
                        dve.tensor_tensor(Hg[d][:, grp(g), :], bank(4 + g, C),
                                          bc(gam[d][:, grp(g)], C), ALU.mult).then_inc(s["hh_kept"], 1)
                dve.wait_ge(s["hh_kept"], NG * (2 * b + 2))
                for i in range(1, steps + 1):
                    for d in range(2):
                        c = order[d][i]
                        dve.wait_ge(s["step_ready"], 2 * steps * b + 2 * (i - 1) + d + 1)
                        dve.scalar_tensor_tensor(S[d][:, i, :], ps[:, 4 + d, 0:C], gam[d][:, c:c + 1],
                                                 Hg[d][:, c, :], ALU.mult, ALU.add).then_inc(s["step_done"], 1)
                dve.wait_ge(s["bonus_ready"], b + 1)
                wait(dve, s["bonus_out"], 16 * b)
                dve.tensor_tensor(bon[:, :], ps[:, 7, :], vT[:, 0:SEQ], ALU.mult).then_inc(s["bonus_kept"], 1)
                assert count[0] == PER


PER = 22
POOL_HALVES = 12


def rwkv_readout(nc, k):
    ctx = ExitStack()
    with ctx:
        def sb(name, shape):
            return ctx.enter_context(nc.sbuf_tensor(name, shape, F32))
        y = sb("y_all", [P, 4, NCL, C])
        y2 = sb("y_sq", [P, 4, NCL, C])
        bonus = sb("bonus_all", [P, 4, SEQ])
        gd, g_up = sb("gd", [P, SEQ]), sb("g_up", [P, 512])
        lw, lb = sb("ln_w", [P, 4]), sb("ln_b", [P, 4])
        mean, var = sb("gn_mean", [P, 4 * NCL]), sb("gn_var", [P, 4 * NCL])
        bT = sb("bT", [P, 4, SEQ])
        ps = k.ps
        ins_in, dch, cent, sqd, var_done, rooted, norm, turned, kept, gd_t, gd_s, g_ready, b_done, b_out = (
            k.sem("ro_" + n) for n in "in dve centred sq var rooted norm turned kept gd_t gd_s g_ready b_done b_out".split())
        block = ctx.enter_context(nc.Block())

        @block.sync
        def _(sp):
            sp.dma_start(y[:, :, :, :].rearrange("p b c x -> p b (c x)"), k.y_d.rearrange("b p t -> p b t")).then_inc(ins_in, 16)
            sp.dma_start(gd[:, :], k.rw_d[14, :, 0:SEQ]).then_inc(ins_in, 16)
            sp.dma_start(g_up[:, :], k.w["rw_g_up"][0]).then_inc(ins_in, 16)
            with nc.allow_non_contiguous_dma(reason="vectors over partitions"):
                sp.dma_start(lw[:, :], k.w["rw_ln_w"][0].rearrange("(b p) -> p b", p=P)).then_inc(ins_in, 16)
                sp.dma_start(lb[:, :], k.w["rw_ln_b"][0].rearrange("(b p) -> p b", p=P)).then_inc(ins_in, 16)
            sp.dma_start(bonus[:, :, :], k.bonus_d.rearrange("b p t -> p b t")).then_inc(ins_in, 16)
            sp.wait_ge(b_done, 4)
            sp.dma_start(k.bT_d.rearrange("b p t -> p b t"), bT[:, :, :]).then_inc(b_out, 16)
            sp.wait_ge(b_out, 16)

        @block.gpsimd
        def _(pool):
            pool.wait_ge(cent, 1)
            pool.tensor_tensor(y2[:, :, :, :], y[:, :, :, :], y[:, :, :, :], ALU.mult).then_inc(sqd, 1)

        @block.tensor
        def _(pe):
            pe.wait_ge(gd_s, 1)
            for b in range(4):
                mm = pe.matmul(ps[:, 4 + b, :], g_up[:, b * P:(b + 1) * P], gd[:, :], start=True, stop=True)
            mm.then_inc(g_ready, 1)
            pe.wait_ge(norm, 1)
            for b in range(4):
                for half in range(2):
                    n = 2 * b + half
                    if n >= 4:
                        pe.wait_ge(kept, n - 3)
                    for c in range(4):
                        mm = pe.transpose(ps[0:64, n % 4, c * P:(c + 1) * P], y[:, b, 4 * half + c, :], k.ident[:, :])
                    mm.then_inc(turned, 1)

        @block.scalar
        def _(act):
            act.wait_ge(ins_in, 96)
            act.activation(gd[:, :], gd[:, :], ACT.Tanh, scale=0.5).then_inc(gd_t, 1)
            act.wait_ge(var_done, 1)
            act.activation(var[:, :], var[:, :], ACT.Sqrt).then_inc(rooted, 1)
            for n in range(8):
                b, half = n // 2, n % 2
                act.wait_ge(turned, n + 1)
                for hh in range(2):
                    q = slice(64 * hh, 64 * hh + 64)
                    ins = act.activation(bT[q, b, 256 * half:256 * half + 256].rearrange("p (c x) -> p c x", c=4),
                                         ps[0:64, n % 4, :].rearrange("p (c h x) -> p c h x", c=4, h=2)[:, :, hh, :], ACT.Copy)
                ins.then_inc(kept, 1)

        @block.vector
        def _(dve):
            link = Chain(dve, dch)
            dve.wait_ge(gd_t, 1)
            dve.tensor_scalar(gd[:, :], gd[:, :], 0.5, 0.5, ALU.mult, ALU.add).then_inc(gd_s, 1)
            y3, y23 = (a[:, :, :, :].rearrange("p b c x -> p (b c) x") for a in (y, y2))
            link(dve.tensor_reduce(mean[:, :], y3, AX.X, ALU.add))
            link(dve.tensor_scalar(mean[:, :], mean[:, :], 1.0 / RN, None, ALU.mult))
            dve.tensor_tensor(y3, y3, bc(mean[:, :], C), ALU.subtract).then_inc(cent, 1)
            dve.wait_ge(sqd, 1)
            link(dve.tensor_reduce(var[:, :], y23, AX.X, ALU.add))
            dve.tensor_scalar(var[:, :], var[:, :], 1.0 / RN, GN_EPS, ALU.mult, ALU.add).then_inc(var_done, 1)
            dve.wait_ge(rooted, 1)
            link(dve.reciprocal(mean[:, :], var[:, :]))
            dve.tensor_tensor(y3, y3, bc(mean[:, :], C), ALU.mult).then_inc(norm, 1)
            dve.wait_ge(g_ready, 1)
            for b in range(4):
                dve.wait_ge(kept, 2 * b + 2)
                link(dve.tensor_scalar(bT[:, b, :], bT[:, b, :], lw[:, b:b + 1], lb[:, b:b + 1], ALU.mult, ALU.add))
                link(dve.tensor_tensor(bT[:, b, :], bT[:, b, :], bonus[:, b, :], ALU.add))
                dve.tensor_tensor(bT[:, b, :], bT[:, b, :], ps[:, 4 + b, :], ALU.mult).then_inc(b_done, 1)


def merge(nc, k):
    ctx = ExitStack()
    with ctx:
        def sb(name, shape):
            return ctx.enter_context(nc.sbuf_tensor(name, shape, F32))
        aT, bT = sb("aT_in", [P, 4, SEQ]), sb("bT_in", [P, 4, SEQ])
        pa, pb, wo = sb("pa", [P, 4, D]), sb("pb", [P, 4, D]), sb("wo", [P, DB, D])
        gate = [sb(f"gate_in{j}", [P, DB, SEQ]) for j in range(2)]
        xT = sb("xT_in", [P, DB, SEQ])
        g2n = sb("norm2_in", [P, DB])
        scale2 = sb("scale2", [P, DB])
        rstd = sb("rstd2", [P, SEQ])
        ps = k.ps
        mg = gate[0]
        sq = gate[1]
        names = "a_in b_in wo_in x_in ab_ready ab_used halves merged out_ready x1_done sq_done ss_done ms_done rms_done dve hn".split()
        s = {n: k.sem("m_" + n) for n in names}
        block = ctx.enter_context(nc.Block())

        @block.sync
        def _(sp):
            sp.dma_start(aT[:, :, :], k.aT_d.rearrange("b p t -> p b t")).then_inc(s["a_in"], 16)
            sp.dma_start(pa[:, :, :], k.w["merge_pa"][0].rearrange("(b p) n -> p b n", p=P)).then_inc(s["a_in"], 16)
            sp.dma_start(gate[0][:, :, :], k.gt_d[0:8].rearrange("b p t -> p b t")).then_inc(s["a_in"], 16)
            sp.dma_start(bT[:, :, :], k.bT_d.rearrange("b p t -> p b t")).then_inc(s["b_in"], 16)
            sp.dma_start(pb[:, :, :], k.w["merge_pb"][0].rearrange("(b p) n -> p b n", p=P)).then_inc(s["b_in"], 16)
            sp.dma_start(gate[1][:, :, :], k.gt_d[8:16].rearrange("b p t -> p b t")).then_inc(s["b_in"], 16)
            sp.dma_start(wo[:, :, :], k.w["w_out"][0].rearrange("(b p) n -> p b n", p=P)).then_inc(s["wo_in"], 16)
            sp.dma_start(xT[:, :, :], k.xT_d.rearrange("(b p) t -> p b t", p=P)).then_inc(s["x_in"], 16)
            with nc.allow_non_contiguous_dma(reason="a vector over partitions"):
                sp.dma_start(g2n[:, :], k.w["norm2_g"][0].rearrange("(b p) -> p b", p=P)).then_inc(s["x_in"], 16)

        @block.tensor
        def _(pe):
            pe.wait_ge(s["a_in"], 48)
            pe.wait_ge(s["b_in"], 48)
            for m in range(DB):
                if m >= 2:
                    pe.wait_ge(s["ab_used"], m - 1)
                for j, (w, src) in enumerate(((pa, aT), (pb, bT))):
                    for b in range(4):
                        mm = pe.matmul(ps[:, 2 * (m % 2) + j, :], w[:, b, m * P:(m + 1) * P], src[:, b, :],
                                       start=(b == 0), stop=(b == 3))
                mm.then_inc(s["ab_ready"], 1)
            pe.wait_ge(s["wo_in"], 16)
            pe.wait_ge(s["merged"], DB)
            for m in range(DB):
                if m >= 2:
                    pe.wait_ge(s["x1_done"], m - 1)
                for b in range(DB):
                    mm = pe.matmul(ps[:, 4 + m % 2, :], wo[:, b, m * P:(m + 1) * P], mg[:, b, :],
                                   start=(b == 0), stop=(b == DB - 1))
                mm.then_inc(s["out_ready"], 1)
            for b in range(DB):
                pe.wait_ge(s["sq_done"], b + 1)
                mm = pe.matmul(ps[:, 6, :], k.ones[:, :], sq[:, b, :], start=(b == 0), stop=(b == DB - 1))
            mm.then_inc(s["ss_done"], 1)

        @block.gpsimd
        def _(pool):
            for m in range(DB):
                pool.wait_ge(s["halves"], m + 1)
                pool.tensor_tensor(mg[:, m, :], gate[0][:, m, :], gate[1][:, m, :], ALU.add).then_inc(s["merged"], 1)

        @block.scalar
        def _(act):
            for m in range(DB):
                act.wait_ge(s["x1_done"], m + 1)
                act.activation(sq[:, m, :], k.x1T[:, m, :], ACT.Square).then_inc(s["sq_done"], 1)
            act.wait_ge(s["ms_done"], 1)
            act.activation(rstd[:, :], rstd[:, :], ACT.Sqrt).then_inc(s["rms_done"], 1)

        @block.vector
        def _(dve):
            link = Chain(dve, s["dve"])
            dve.wait_ge(s["x_in"], 32)
            link(dve.tensor_scalar(scale2[:, :], k.mod[:, 0, 4 * DB:5 * DB], 1.0, None, ALU.add))
            link(dve.tensor_tensor(scale2[:, :], scale2[:, :], g2n[:, :], ALU.mult))
            for m in range(DB):
                dve.wait_ge(s["ab_ready"], m + 1)
                for j in range(2):
                    ins = dve.tensor_tensor(gate[j][:, m, :], gate[j][:, m, :], ps[:, 2 * (m % 2) + j, :], ALU.mult)
                    if j:
                        ins.then_inc(s["halves"], 1)
                dve.wait_ge(s["halves"], m + 1)
                dve.tensor_copy(rstd[:, 0:1], scale2[:, 0:1]).then_inc(s["ab_used"], 1)
            for m in range(DB):
                dve.wait_ge(s["out_ready"], m + 1)
                dve.scalar_tensor_tensor(k.x1T[:, m, :], ps[:, 4 + m % 2, :], k.mod[:, 0, 2 * DB + m:2 * DB + m + 1],
                                         xT[:, m, :], ALU.mult, ALU.add).then_inc(s["x1_done"], 1)
            dve.wait_ge(s["ss_done"], 1)
            dve.tensor_scalar(rstd[:, :], ps[:, 6, :], 1.0 / D, EPS, ALU.mult, ALU.add).then_inc(s["ms_done"], 1)
            dve.wait_ge(s["rms_done"], 1)
            link(dve.reciprocal(k.h2T[:, 0, :], rstd[:, :]))
            link(dve.tensor_copy(rstd[:, :], k.h2T[:, 0, :]))
            for m in range(DB):
                dve.scalar_tensor_tensor(k.h2T[:, m, :], k.x1T[:, m, :], scale2[:, m:m + 1], rstd[:, :],
                                         ALU.mult, ALU.mult).then_inc(s["hn"], 1)
                dve.wait_ge(s["hn"], m + 1)
                dve.tensor_scalar(k.h2T[:, m, :], k.h2T[:, m, :], k.mod[:, 0, 3 * DB + m:3 * DB + m + 1], None, ALU.add)


NG_E, EPG = 4, 4
BLOCKS = SEQ * 2 // P + NE
PAIRS = BLOCKS // 2
SLOTS = BLOCKS * P
FEWEST = SEQ * 2 // P


def route(nc, k):
    ctx = ExitStack()
    with ctx:
        def sb(name, shape, dt=F32):
            return ctx.enter_context(nc.sbuf_tensor(name, shape, dt))
        h2N = sb("h2_rows", [P, TL, D])
        rw = sb("router_w_sb", [P, DB, NE])
        rb = sb("router_b_sb", [P, NE])
        sc, sel, selm = sb("scores", [P, TL, NE]), sb("sel", [P, TL, NE]), sb("sel_masked", [P, TL, NE])
        hi, lo = sb("pair_hi", [P, TL, NG_E, 2]), sb("pair_lo", [P, TL, NG_E, 2])
        gs, t1, t2 = sb("group_score", [P, TL, NG_E]), sb("t1", [P, TL, NG_E]), sb("t2", [P, TL, NG_E])
        top = sb("top", [P, TL])
        oh = [sb(f"one_hot{j}", [P, TL, NE]) for j in range(2)]
        both, work = sb("chosen", [P, TL, NE]), sb("work", [P, TL, NE])
        prio, gprio = sb("priority", [P, NE]), sb("group_priority", [P, NG_E])
        strict = sb("strict", [P, P])
        rank = sb("rank", [P, TL + 1, NE])
        nb, end, ones16 = sb("n_blocks", [P, NE]), sb("end_block", [P, NE]), sb("ones16", [P, NE])
        acc = sb("acc", [P, NE])
        slot_f = sb("slot_f", [P, 2, TL])
        blk = sb("block_no", [P, BLOCKS])
        cmp_ = sb("block_cmp", [P, BLOCKS, NE])
        plan_f = sb("plan_f", [P, BLOCKS + 1])
        zero_i = sb("zero_i", [P, BLOCKS], I32)
        tok = sb("token_no", [P, TL], I32)
        ws = sb("w_sum", [P, TL])
        ps = k.ps
        names = ("small consts turned kept h2_out logits e_done dve chosen rank_done slots zero_out tab_out idx_in mod_out row_in").split()
        s = {n: k.sem("r2_" + n) for n in names}
        block = ctx.enter_context(nc.Block())
        tab_v = k.tab_d.rearrange("(j p) a -> p (j a)", p=P)

        @block.sync
        def _(sp):
            sp.dma_start(rw[:, :, :], k.w["router_w"].rearrange("(b p) e -> p b e", p=P)).then_inc(s["small"], 16)
            sp.dma_start(rb[:, :], k.w["router_b"].rearrange("(a e) -> a e", a=1).to_broadcast([P, NE])).then_inc(s["small"], 16)
            with nc.allow_non_contiguous_dma(reason="a vector over partitions"):
                sp.dma_start(k.g2_d.rearrange("(b p) -> p b", p=P), k.mod[:, 0, 5 * DB:6 * DB]).then_inc(s["mod_out"], 16)
            sp.wait_ge(s["consts"], 5)
            with nc.allow_non_contiguous_dma(reason="a small table"):
                sp.dma_start(tab_v, zero_i[:, :]).then_inc(s["zero_out"], 16)
            sp.wait_ge(s["mod_out"], 16)
            sp.dma_start(k.g2_row[:, :], k.g2_d.rearrange("(a n) -> a n", a=1).to_broadcast([P, D])).then_inc(s["row_in"], 16)
            sp.wait_ge(s["kept"], 2 * TL)
            sp.dma_start(k.h2_d.rearrange("(t p) d -> p t d", p=P), h2N[:, :, :]).then_inc(s["h2_out"], 16)
            sp.wait_ge(s["tab_out"], 16 * 2 * TL)
            with nc.allow_non_contiguous_dma(reason="a small table"):
                sp.dma_start(k.idx[:, :], tab_v).then_inc(s["idx_in"], 16)
            sp.wait_ge(s["idx_in"], 16)
            sp.wait_ge(s["h2_out"], 16)
            sp.wait_ge(s["row_in"], 16)

        @block.tensor
        def _(pe):
            pe.wait_ge(s["small"], 32)
            for t in range(TL):
                for b in range(DB):
                    mm = pe.matmul(ps[:, 4, t * NE:(t + 1) * NE], k.h2T[:, b, t * P:(t + 1) * P], rw[:, b, :],
                                   start=(b == 0), stop=(b == DB - 1))
            mm.then_inc(s["logits"], 1)
            n = 0
            for src in (k.h2T, k.x1T):
                for t in range(TL):
                    for g in range(2):
                        if n >= 4:
                            pe.wait_ge(s["kept"], n - 3)
                        for j in range(4):
                            mm = pe.transpose(ps[:, n % 4, j * P:(j + 1) * P], src[:, 4 * g + j, t * P:(t + 1) * P],
                                              k.ident[:, :])
                        mm.then_inc(s["turned"], 1)
                        n += 1
            pe.wait_ge(s["chosen"], 2)
            pe.wait_ge(s["consts"], 5)
            for t in range(TL + 1):
                for t2_ in range(min(t + 1, TL)):
                    mm = pe.matmul(ps[:, 5, t * NE:(t + 1) * NE], strict[:, :] if t2_ == t else k.ones[:, :],
                                   both[:, t2_, :], start=(t2_ == 0), stop=(t2_ == min(t, TL - 1)))
            mm.then_inc(s["rank_done"], 1)

        @block.scalar
        def _(act):
            act.wait_ge(s["logits"], 1)
            act.activation(sc[:, :, :], ps[:, 4, 0:TL * NE].rearrange("p (t e) -> p t e", t=TL), ACT.Exp, scale=-1.0)\
               .then_inc(s["e_done"], 1)
            n = 0
            for dst in (h2N, k.x1N):
                for t in range(TL):
                    for g in range(2):
                        act.wait_ge(s["turned"], n + 1)
                        act.activation(dst[:, t, 512 * g:512 * g + 512], ps[:, n % 4, :], ACT.Copy).then_inc(s["kept"], 1)
                        n += 1

        @block.gpsimd
        def _(pool):
            pool.iota(prio[:, :], pattern=[[-1, NE]], base=NE, channel_multiplier=0, allow_small_or_imprecise_dtypes=True)\
                .then_inc(s["consts"], 1)
            pool.iota(gprio[:, :], pattern=[[-1, NG_E]], base=NG_E, channel_multiplier=0,
                      allow_small_or_imprecise_dtypes=True).then_inc(s["consts"], 1)
            pool.iota(blk[:, :], pattern=[[1, BLOCKS]], base=0, channel_multiplier=0, allow_small_or_imprecise_dtypes=True)\
                .then_inc(s["consts"], 1)
            pool.iota(tok[:, :], pattern=[[P, TL]], base=0, channel_multiplier=1).then_inc(s["consts"], 1)
            pool.memset(zero_i[:, :], 0).then_inc(s["consts"], 1)
            pool.wait_ge(s["consts"], 5)
            pool.wait_ge(s["slots"], 1)
            pool.wait_ge(s["zero_out"], 16)
            for j in range(2):
                for t in range(TL):
                    pool.indirect_dma_start(out=k.tab_d, out_offset=bass.IndirectOffsetOnAxis(ap=k.slot_t[2 * t + j][:, :], axis=0),
                                            in_=tok[:, t:t + 1], in_offset=None).then_inc(s["tab_out"], 16)
            pool.wait_ge(s["tab_out"], 16 * 2 * TL)

        @block.vector
        def _(dve):
            link = Chain(dve, s["dve"])

            def over(ap, n):
                return ap.unsqueeze(1).to_broadcast([P, TL, n])
            dve.wait_ge(s["small"], 32)
            dve.wait_ge(s["consts"], 5)
            dve.tensor_scalar(strict[:, :], k.onward[:, :], -1.0, 1.0, ALU.mult, ALU.add)
            link(dve.memset(ones16[:, :], 1.0))
            dve.wait_ge(s["e_done"], 1)
            link(dve.tensor_scalar(selm[:, :, :], sc[:, :, :], 1.0, None, ALU.add))
            link(dve.reciprocal(sc[:, :, :], selm[:, :, :]))
            link(dve.tensor_tensor(sel[:, :, :], sc[:, :, :], over(rb[:, :], NE), ALU.add))
            v = sel[:, :, :].rearrange("p t (g a) -> p (t g) a", a=EPG)
            hi_, lo_ = (a[:, :, :, :].rearrange("p t g a -> p (t g) a") for a in (hi, lo))
            link(dve.tensor_tensor(hi_, v[:, :, 0:2], v[:, :, 2:4], ALU.max))
            link(dve.tensor_tensor(lo_, v[:, :, 0:2], v[:, :, 2:4], ALU.min))
            gs_, t1_, t2_ = (a[:, :, :].rearrange("p t g -> p (t g)") for a in (gs, t1, t2))
            link(dve.tensor_tensor(gs_, hi_[:, :, 0], hi_[:, :, 1], ALU.max))
            link(dve.tensor_tensor(t1_, hi_[:, :, 0], hi_[:, :, 1], ALU.min))
            link(dve.tensor_tensor(t2_, lo_[:, :, 0], lo_[:, :, 1], ALU.max))
            link(dve.tensor_tensor(t1_, t1_, t2_, ALU.max))
            link(dve.tensor_tensor(gs_, gs_, t1_, ALU.add))

            def first_best(values, prior, n, onehot, scratch):
                link(dve.tensor_reduce(top[:, :], values[:, :, :], AX.X, ALU.max))
                link(dve.tensor_tensor(scratch[:, :, :], values[:, :, :], bc(top[:, :], n), ALU.is_equal))
                link(dve.tensor_tensor(scratch[:, :, :], scratch[:, :, :], over(prior[:, :], n), ALU.mult))
                link(dve.tensor_reduce(top[:, :], scratch[:, :, :], AX.X, ALU.max))
                link(dve.tensor_tensor(onehot[:, :, :], scratch[:, :, :], bc(top[:, :], n), ALU.is_equal))
            first_best(gs, gprio, NG_E, t1, t2)
            link(dve.tensor_copy(both[:, :, :].rearrange("p t (g a) -> p (t g) a", a=EPG), bc(t1_, EPG)))
            link(dve.tensor_scalar(work[:, :, :], both[:, :, :], OUTSIDE, -OUTSIDE, ALU.mult, ALU.add))
            link(dve.tensor_tensor(selm[:, :, :], sel[:, :, :], both[:, :, :], ALU.mult))
            link(dve.tensor_tensor(selm[:, :, :], selm[:, :, :], work[:, :, :], ALU.add))
            first_best(selm, prio, NE, oh[0], work)
            link(dve.tensor_scalar(work[:, :, :], oh[0][:, :, :], -2 * OUTSIDE, None, ALU.mult))
            link(dve.tensor_tensor(selm[:, :, :], selm[:, :, :], work[:, :, :], ALU.add))
            first_best(selm, prio, NE, oh[1], work)
            dve.tensor_tensor(both[:, :, :], oh[0][:, :, :], oh[1][:, :, :], ALU.add).then_inc(s["chosen"], 1)
            for j in range(2):
                link(dve.tensor_tensor(work[:, :, :], sc[:, :, :], oh[j][:, :, :], ALU.mult))
                link(dve.tensor_reduce(k.comb[:, j, :], work[:, :, :], AX.X, ALU.add))
            link(dve.tensor_tensor(ws[:, :], k.comb[:, 0, :], k.comb[:, 1, :], ALU.add))
            link(dve.reciprocal(top[:, :], ws[:, :]))
            for j in range(2):
                ins = dve.tensor_tensor(k.comb[:, j, :], k.comb[:, j, :], top[:, :], ALU.mult)
            ins.then_inc(s["chosen"], 1)
            dve.wait_ge(s["rank_done"], 1)
            link(dve.tensor_copy(rank[:, :, :].rearrange("p t e -> p (t e)"), ps[:, 5, 0:(TL + 1) * NE]))
            cnt = rank[:, TL, :]
            link(dve.tensor_scalar(nb[:, :], cnt, 0.0, None, ALU.is_gt))
            for m in range(1, TL):
                link(dve.tensor_scalar(acc[:, :], cnt, float(P * m), None, ALU.is_gt))
                link(dve.tensor_tensor(nb[:, :], nb[:, :], acc[:, :], ALU.add))
            link(dve.tensor_tensor_scan(end[:, :], ones16[:, :], nb[:, :], 0.0, ALU.mult, ALU.add))
            link(dve.tensor_tensor(acc[:, :], end[:, :], nb[:, :], ALU.subtract))
            link(dve.tensor_scalar(acc[:, :], acc[:, :], float(P), None, ALU.mult))
            link(dve.tensor_tensor(work[:, :, :], rank[:, 0:TL, :], over(acc[:, :], NE), ALU.add))
            for j in range(2):
                link(dve.tensor_tensor(selm[:, :, :], work[:, :, :], oh[j][:, :, :], ALU.mult))
                link(dve.tensor_reduce(slot_f[:, j, :], selm[:, :, :], AX.X, ALU.add))
                for t in range(TL):
                    link(dve.tensor_copy(k.slot_t[2 * t + j][:, :], slot_f[:, j, t:t + 1]))
            dve.tensor_copy(ws[:, 0:1], top[:, 0:1]).then_inc(s["slots"], 1)
            link(dve.tensor_tensor(cmp_[:, :, :], bc(blk[:, :], NE), end[:, :].unsqueeze(1).to_broadcast([P, BLOCKS, NE]),
                                   ALU.is_ge))
            link(dve.tensor_reduce(plan_f[:, 0:BLOCKS], cmp_[:, :, :], AX.X, ALU.add))
            link(dve.tensor_scalar(plan_f[:, 0:BLOCKS], plan_f[:, 0:BLOCKS], float(NE - 1), None, ALU.min))
            link(dve.tensor_scalar(cmp_[:, 0, 0:PAIRS], blk[:, 0:BLOCKS:2], end[:, NE - 1:NE], None, ALU.is_lt))
            link(dve.tensor_reduce(plan_f[:, BLOCKS:BLOCKS + 1], cmp_[:, 0, 0:PAIRS], AX.X, ALU.add))
            link(dve.tensor_copy(k.plan[:, :], plan_f[:, :]))


OUTSIDE = 1e4


def experts(nc, k):
    ctx = ExitStack()
    with ctx:
        def sb(name, shape, dt=F32):
            return ctx.enter_context(nc.sbuf_tensor(name, shape, dt))
        wg = [sb(f"wg{s}", [P, DB, DE]) for s in range(2)]
        wu = [sb(f"wu{s}", [P, DB, DE]) for s in range(2)]
        wd = [sb(f"wd{s}", [P, EB, D]) for s in range(2)]
        ids = [sb(f"ids{s}", [P, 1], I32) for s in range(2)]
        xg = [sb(f"xg{s}", [P, D]) for s in range(2)]
        xgT = [sb(f"xgT{s}", [P, DB, P]) for s in range(2)]
        th = [sb(f"th{s}", [P, DE]) for s in range(2)]
        hid = [sb(f"hid{s}", [P, DE]) for s in range(2)]
        hidT = [sb(f"hidT{s}", [P, EB, P]) for s in range(2)]
        yr = [sb(f"yr{s}", [P, D]) for s in range(2)]
        ps = k.ps
        names = "gu_in d_in id_done x_in x_turned x_kept g_ready gu_ready th_done hid_half hid_u hid_done h_turned h_kept y_ready y_kept y_out".split()
        s = {n: [k.sem(f"e_{n}{j}") for j in range(2)] for n in names}
        block = ctx.enter_context(nc.Block())

        def pairs(eng):
            n = eng.value_load(k.plan[0:1, BLOCKS:BLOCKS + 1], min_val=FEWEST // 2, max_val=PAIRS)
            yield 0, n
            with eng.Fori(1, n) as i:
                yield i, n

        @block.sync
        def _(sp):
            for i, n in pairs(sp):
                for j in range(2):
                    e = sp.value_load(k.plan[0:1, bass.ds(2 * i + j, 1)], min_val=0, max_val=NE - 1)
                    wait(sp, s["gu_ready"][j], i)
                    sp.dma_start(wg[j][:, :, :], k.w["exp_w_gate"][0][bass.ds(e, 1)].rearrange("a (b p) n -> p (a b) n", p=P))\
                        .then_inc(s["gu_in"][j], 16)
                    sp.dma_start(wu[j][:, :, :], k.w["exp_w_up"][0][bass.ds(e, 1)].rearrange("a (b p) n -> p (a b) n", p=P))\
                        .then_inc(s["gu_in"][j], 16)
                    wait(sp, s["y_ready"][j], i)
                    sp.dma_start(wd[j][:, :, :], k.w["exp_w_down"][0][bass.ds(e, 1)].rearrange("a (b p) n -> p (a b) n", p=P))\
                        .then_inc(s["d_in"][j], 16)

        @block.gpsimd
        def _(pool):
            for i, n in pairs(pool):
                for j in range(2):
                    pool.wait_ge(s["id_done"][j], i + 1)
                    pool.nop(nofuse=True)
                    pool.indirect_dma_start(out=xg[j][:, :], out_offset=None, in_=k.h2_d,
                                            in_offset=bass.IndirectOffsetOnAxis(ap=ids[j][:, :], axis=0))\
                        .then_inc(s["x_in"][j], 16)

        @block.tensor
        def _(pe):
            def gate_up(i, j):
                b0 = 4 * j
                wait(pe, s["y_kept"][j], i)
                pe.wait_ge(s["x_in"][j], 16 * i + 16)
                for h in range(2):
                    for c in range(4):
                        mm = pe.transpose(ps[:, b0 + h, c * P:(c + 1) * P], xg[j][:, (4 * h + c) * P:(4 * h + c + 1) * P],
                                          k.ident[:, :])
                mm.then_inc(s["x_turned"][j], 1)
                pe.wait_ge(s["gu_in"][j], 32 * i + 32)
                pe.wait_ge(s["x_kept"][j], i + 1)
                for w, bank, done in ((wg, b0 + 2, "g_ready"), (wu, b0 + 3, "gu_ready")):
                    for b in range(DB):
                        mm = pe.matmul(ps[:, bank, :], xgT[j][:, b, :], w[j][:, b, :], start=(b == 0), stop=(b == DB - 1))
                    mm.then_inc(s[done][j], 1)

            def down(c1, j):
                b0 = 4 * j
                pe.wait_ge(s["hid_done"][j], c1)
                for c in range(EB):
                    mm = pe.transpose(ps[:, b0, c * P:(c + 1) * P], hid[j][:, c * P:(c + 1) * P], k.ident[:, :])
                mm.then_inc(s["h_turned"][j], 1)
                pe.wait_ge(s["d_in"][j], 16 * c1)
                pe.wait_ge(s["h_kept"][j], c1)
                for h in range(2):
                    for b in range(EB):
                        mm = pe.matmul(ps[:, b0 + 1 + h, :], hidT[j][:, b, :], wd[j][:, b, 512 * h:512 * h + 512],
                                       start=(b == 0), stop=(b == EB - 1))
                mm.then_inc(s["y_ready"][j], 1)
            for i, n in pairs(pe):
                gate_up(i, 0)
                if not (isinstance(i, int) and i == 0):
                    down(i, 1)
                gate_up(i, 1)
                down(i + 1, 0)
            down(n, 1)

        @block.scalar
        def _(act):
            def first(i, j):
                b0 = 4 * j
                act.wait_ge(s["x_turned"][j], i + 1)
                for h in range(2):
                    ins = act.activation(xgT[j][:, 4 * h:4 * h + 4, :].rearrange("p b c -> p (b c)"), ps[:, b0 + h, :], ACT.Copy)
                ins.then_inc(s["x_kept"][j], 1)
                act.wait_ge(s["g_ready"][j], i + 1)
                act.activation(th[j][:, :], ps[:, b0 + 2, :], ACT.Tanh, scale=0.5).then_inc(s["th_done"][j], 1)

            def second(c1, j):
                b0 = 4 * j
                act.wait_ge(s["h_turned"][j], c1)
                act.activation(hidT[j][:, :, :].rearrange("p b c -> p (b c)"), ps[:, b0, :], ACT.Copy).then_inc(s["h_kept"][j], 1)
                act.wait_ge(s["y_ready"][j], c1)
                for h in range(2):
                    ins = act.activation(yr[j][:, 512 * h:512 * h + 512], ps[:, b0 + 1 + h, :], ACT.Copy)
                ins.then_inc(s["y_kept"][j], 1)
                act.wait_ge(s["y_kept"][j], c1)
                act.dma_start(k.ys_d[bass.ds((2 * c1 - 2 + j) * P, P), :], yr[j][:, :]).then_inc(s["y_out"][j], 16)
            for i, n in pairs(act):
                first(i, 0)
                if not (isinstance(i, int) and i == 0):
                    second(i, 1)
                first(i, 1)
                for j in range(2):
                    wait(act, s["y_out"][j], 16 * i)
                second(i + 1, 0)
            second(n, 1)
            for j in range(2):
                act.wait_ge(s["y_out"][j], 16 * n)
            act.nop(nofuse=True)

        @block.vector
        def _(dve):
            for i, n in pairs(dve):
                for j in range(2):
                    wait(dve, s["x_turned"][j], i)
                    dve.tensor_copy(ids[j][:, :], k.idx[:, bass.ds(2 * i + j, 1)]).then_inc(s["id_done"][j], 1)
                for j in range(2):
                    b0 = 4 * j
                    dve.wait_ge(s["th_done"][j], i + 1)
                    dve.scalar_tensor_tensor(th[j][:, :], th[j][:, :], 1.0, ps[:, b0 + 2, :], ALU.add, ALU.mult)\
                       .then_inc(s["hid_half"][j], 1)
                    dve.wait_ge(s["hid_half"][j], i + 1)
                    dve.wait_ge(s["gu_ready"][j], i + 1)
                    dve.scalar_tensor_tensor(hid[j][:, :], th[j][:, :], 0.5, ps[:, b0 + 3, :], ALU.mult, ALU.mult)\
                       .then_inc(s["hid_done"][j], 1)


def finish(nc, k):
    ctx = ExitStack()
    with ctx:
        def sb(name, shape, dt=F32):
            return ctx.enter_context(nc.sbuf_tensor(name, shape, dt))
        y = [[sb(f"y{j}_{t}", [P, D]) for t in range(TL)] for j in range(2)]
        fg = sb("final_row", [P, D])
        ss, inv = sb("ss", [P, TL]), sb("inv", [P, TL])
        sq = sb("fin_sq", [P, D])
        y_in = [k.sem(f"f_y{n}") for n in range(2 * TL)]
        names = "row_in part mixed x2 sq_done ms rooted dve done out".split()
        s = {n: k.sem("f_" + n) for n in names}
        block = ctx.enter_context(nc.Block())

        @block.sync
        def _(sp):
            sp.dma_start(fg[:, :], k.w["final_g"].rearrange("(a n) -> a n", a=1).to_broadcast([P, D])).then_inc(s["row_in"], 16)
            for t in range(TL):
                sp.wait_ge(s["done"], t + 1)
                sp.dma_start(k.out[0, t * P:(t + 1) * P, :], y[0][t][:, :]).then_inc(s["out"], 16)
            sp.wait_ge(s["out"], 16 * TL)

        @block.gpsimd
        def _(pool):
            for t in range(TL):
                for j in range(2):
                    pool.indirect_dma_start(out=y[j][t][:, :], out_offset=None, in_=k.ys_d,
                                            in_offset=bass.IndirectOffsetOnAxis(ap=k.slot_t[2 * t + j][:, :], axis=0))\
                        .then_inc(y_in[2 * t + j], 16)

        @block.scalar
        def _(act):
            for t in range(TL):
                act.wait_ge(s["x2"], t + 1)
                if t:
                    act.wait_ge(s["sq_done"], t)
                act.activation(sq[:, :], y[1][t][:, :], ACT.Square, accum_out=ss[:, t:t + 1]).then_inc(s["sq_done"], 1)
            act.wait_ge(s["ms"], 1)
            act.activation(inv[:, :], inv[:, :], ACT.Sqrt).then_inc(s["rooted"], 1)

        @block.vector
        def _(dve):
            link = Chain(dve, s["dve"])
            dve.wait_ge(s["row_in"], 16)
            for t in range(TL):
                dve.wait_ge(y_in[2 * t], 16)
                dve.wait_ge(y_in[2 * t + 1], 16)
                a, b = y[0][t][:, :], y[1][t][:, :]
                link(dve.tensor_scalar(a, a, k.comb[:, 0, t:t + 1], None, ALU.mult))
                link(dve.scalar_tensor_tensor(b, b, k.comb[:, 1, t:t + 1], a, ALU.mult, ALU.add))
                link(dve.tensor_tensor(b, b, k.g2_row[:, :], ALU.mult))
                dve.tensor_tensor(b, b, k.x1N[:, t, :], ALU.add).then_inc(s["x2"], 1)
            dve.wait_ge(s["sq_done"], TL)
            dve.tensor_scalar(inv[:, :], ss[:, :], 1.0 / D, EPS, ALU.mult, ALU.add).then_inc(s["ms"], 1)
            dve.wait_ge(s["rooted"], 1)
            link(dve.reciprocal(ss[:, :], inv[:, :]))
            for t in range(TL):
                dve.scalar_tensor_tensor(y[0][t][:, :], y[1][t][:, :], ss[:, t:t + 1], fg[:, :], ALU.mult, ALU.mult)\
                   .then_inc(s["done"], 1)


def merge_and_moe(nc, k):
    with ExitStack() as c1:
        def sb(name, shape, dt=F32):
            return c1.enter_context(nc.sbuf_tensor(name, shape, dt))
        k.x1N = sb("x1_rows", [P, TL, D])
        k.g2_row = sb("g2_row", [P, D])
        k.comb = sb("comb", [P, 2, TL])
        k.slot_t = [sb(f"slot{n}", [P, 1], I32) for n in range(2 * TL)]
        k.idx = sb("slot_tokens", [P, BLOCKS], I32)
        k.plan = sb("plan", [P, BLOCKS + 1], I32)
        with ExitStack() as c2:
            k.x1T, k.h2T = (c2.enter_context(nc.sbuf_tensor(n, [P, DB, SEQ], F32)) for n in ("x1T", "h2T"))
            phase(nc, k, merge)
            phase(nc, k, route)
        phase(nc, k, experts)
        phase(nc, k, finish, give_back=False)


def build(nc, ins, out):
    k = Core()
    k.w = ins
    ctx = ExitStack()
    with ctx:
        def dram(name, shape, dt=F32):
            return nc.dram_tensor(name, shape, dt, kind="Internal").ap()

        def sb(name, shape, dt=F32):
            return ctx.enter_context(nc.sbuf_tensor(name, shape, dt))
        k.out = out
        k.ps = ctx.enter_context(nc.psum_tensor("ps", [P, 8, 512], F32))
        k.xT_d = dram("xT_d", [D, SEQ])
        k.rw_d = dram("rw_d", [NRW, P, T])
        k.gt_d = dram("gt_d", [16, P, SEQ])
        k.aT_d = dram("aT_d", [4, P, SEQ])
        k.kk_d = dram("kk_d", [4, P, T])
        k.y_d = dram("y_d", [4, P, SEQ])
        k.bonus_d = dram("bonus_d", [4, P, SEQ])
        k.h2_d = dram("h2_d", [SEQ, D])
        k.ys_d = dram("ys_d", [SLOTS, D])
        k.tab_d = dram("tab_d", [SLOTS, 1], I32)
        k.g2_d = dram("g2_d", [D])
        k.bT_d = dram("bT_d", [4, P, SEQ])
        k.ident, k.ones = sb("ident", [P, P]), sb("ones", [P, P])
        k.mod = sb("mod", [P, 2, 48])
        k.upto, k.onward = sb("upto", [P, P]), sb("onward", [P, P])
        k.neg_upto, k.neg_onward = sb("neg_upto", [P, P]), sb("neg_onward", [P, P])
        phase(nc, k, constants, give_back=False)
        phase(nc, k, masks, give_back=False)
        with ExitStack() as c2:
            def sb2(name, shape):
                return c2.enter_context(nc.sbuf_tensor(name, shape, F32))
            k.qkT = sb2("qkT", [P, 4, T])
            k.v_ml = sb2("v_ml", [P, TT, ML_H, DV + 1])
            k.o_ml = sb2("o_ml", [P, TL, 512])
            k.g_ml = sb2("g_ml", [P, TT, 16])
            with ExitStack() as c3:
                k.hT = c3.enter_context(nc.sbuf_tensor("hT", [P, DB, T], F32))
                phase(nc, k, modulate)
                phase(nc, k, project)
            phase(nc, k, mlstm)
        with ExitStack() as c4:
            def sb4(name, shape):
                return c4.enter_context(nc.sbuf_tensor(name, shape, F32))
            k.same_head = sb4("same_head", [P, P])
            k.cut = sb4("cut", [P, 2, 2, C])
            k.join = sb4("join", [P, 2, 6, P])
            k.reset = sb4("reset", [P, NC, C])
            phase(nc, k, rwkv_masks, give_back=False)
            phase(nc, k, rwkv_keys, give_back=False)
            phase(nc, k, rwkv)
        phase(nc, k, rwkv_readout, give_back=False)
        merge_and_moe(nc, k)


_INS = ["x", "c", "ctx", "c_ctx", "w_ada", "b_ada", "norm1_g", "norm2_g", "w_in", "ml_conv_k", "ml_conv_b",
        "ml_gate_b", "ml_norm_g", "rw_mu", "rw_w_up", "rw_w0", "rw_a_up", "rw_a0", "rw_g_up", "rw_k_k", "rw_k_a",
        "rw_r_k", "rw_ln_w", "rw_ln_b", "merge_pa", "merge_pb", "w_out", "router_w", "router_b", "exp_w_gate",
        "exp_w_up", "exp_w_down", "final_g"]


def kernel(**inputs):
    import numpy as _np
    import concourse.bacc as _bacc
    from concourse import mybir as _mybir
    from concourse.bass_utils import run_bass_kernel_spmd as _run

    nc = _bacc.Bacc("TRN2", target_bir_lowering=False, num_devices=1)
    arrays, aps = {}, {}
    for name in _INS:
        a = _np.ascontiguousarray(inputs[name])
        arrays[f"in_{name}"] = a
        aps[name] = nc.dram_tensor(f"in_{name}", a.shape, _mybir.dt.from_np(a.dtype), kind="ExternalInput").ap()
    out = nc.dram_tensor("out_latent", (1, SEQ, D), F32, kind="ExternalOutput").ap()
    build(nc, aps, out)
    r = _run(nc, [arrays], core_ids=[0])
    return r.results[0]["out_latent"]
```

```python
import numpy as np
import concourse.bass as bass
from concourse import mybir
from contextlib import ExitStack

F32 = mybir.dt.float32
I32 = mybir.dt.int32
ALU = mybir.AluOpType
ACT = mybir.ActivationFunctionType
AX = mybir.AxisListType

P = 128
D = 1024
DB = D // P
SEQ, CTX = 512, 256
T = SEQ + CTX
TT = T // P
TL = SEQ // P
GRID_W = 64
GRID_H = SEQ // GRID_W
ML_H, DQK, DV = 4, 64, 128
RW_H, RN = 8, 64
RW_W = RW_H * RN
C = 64
NC = T // C
NCL = SEQ // C
COL_Q, COL_K, COL_V, COL_O, COL_G, COL_RW = 0, 256, 512, 1024, 1536, 1552
NRW = 15
COL_GT = COL_RW + NRW * P
NE, DE = 16, 512
EB = DE // P
EPS = 1e-6
GN_EPS = 6.4e-4
KAPPA = float(np.exp(-0.5))


class Chain:

    def __init__(self, eng, sem):
        self.eng, self.sem, self.n = eng, sem, 0

    def __call__(self, ins):
        self.n += 1
        ins.then_inc(self.sem, 1)
        self.eng.wait_ge(self.sem, self.n)


class Core:
    pass


def bc(ap, n):
    return ap.unsqueeze(2).to_broadcast([ap.shape[0], ap.shape[1], n])



def rounds(eng, n):
    yield 0
    with eng.Fori(1, n) as i:
        yield i


def wait(eng, sem, value):
    if not (isinstance(value, int) and value == 0):
        eng.wait_ge(sem, value)


def phase(nc, k, program, give_back=True):
    sems = []

    def sem(name):
        sems.append(nc.alloc_semaphore(name=name))
        return sems[-1]
    k.sem = sem
    program(nc, k)
    if give_back:
        nc.clear_and_free_semaphores(sems)
        nc.all_engine_barrier()




def constants(nc, k):
    with nc.Block() as block:
        made = k.sem("const_made")

        @block.gpsimd
        def _(pool):
            pool.memset(k.ident[:, :], 0.0).then_inc(made, 1)
            pool.memset(k.ones[:, :], 1.0).then_inc(made, 1)
            pool.wait_ge(made, 2)
            pool.affine_select(out=k.ident[:, :], in_=k.ident[:, :], compare_op=ALU.not_equal, fill=1.0,
                               base=0, pattern=[[-1, P]], channel_multiplier=1).then_inc(made, 1)
            pool.wait_ge(made, 3)


def chunk_masks(pool, k, made):
    n = 0
    for d in range(2):
        for i in range(6):
            pool.memset(k.join[:, d, i, :], 0.0).then_inc(made, 1)
            n += 1
    pool.memset(k.reset[:, :, :], 1.0).then_inc(made, 1)
    pool.memset(k.same_head[:, :], 0.0).then_inc(made, 1)
    n += 2
    pool.wait_ge(made, n)
    for q in (slice(0, 64), slice(64, 128)):
        pool.memset(k.same_head[q, q], 1.0).then_inc(made, 1)
        n += 1
        pool.wait_ge(made, n)
    pool.memset(k.reset[:, :, 0:1], 0.0).then_inc(made, 1)
    n += 1
    for d in range(2):
        for i in range(6):
            b = 1 << i
            v = k.join[:, d, i, :].rearrange("p (q two s) -> p q two s", two=2, s=b)[:, :, d, :]
            pool.memset(v, 1.0).then_inc(made, 1)
            n += 1
            pool.wait_ge(made, n)
            lo = 0 if d else b
            pool.affine_select(out=v, in_=v, compare_op=ALU.is_ge, fill=0.0, base=-lo,
                               pattern=[[-2 * b, 64 // b], [0, b]], channel_multiplier=1).then_inc(made, 1)
            n += 1
            pool.wait_ge(made, n)
            pool.affine_select(out=v, in_=v, compare_op=ALU.is_ge, fill=0.0, base=lo + b - 1,
                               pattern=[[2 * b, 64 // b], [0, b]], channel_multiplier=-1).then_inc(made, 1)
            n += 1
    pool.wait_ge(made, n)


def cut_masks(dve, k, cut_made):
    for d in range(2):
        incl, other = (k.onward, k.upto) if d else (k.upto, k.onward)
        for q in (slice(0, 64), slice(64, 128)):
            dve.tensor_scalar(k.cut[q, d, 0, :], other[q, q], -1.0, 1.0, ALU.mult, ALU.add).then_inc(cut_made, 1)
            dve.tensor_copy(k.cut[q, d, 1, :], incl[q, q]).then_inc(cut_made, 1)
    dve.wait_ge(cut_made, 8)


def modulate(nc, k):
    ctx = ExitStack()
    with ctx:
        def sb(name, shape):
            return ctx.enter_context(nc.sbuf_tensor(name, shape, F32))
        x_rows = sb("x_rows", [P, TT, D])
        xT = sb("xT", [P, DB, T])
        wada = [sb(f"wada{s}", [P, DB, 512]) for s in range(2)]
        sT = sb("sT", [P, DB, 2])
        sT_t = sb("sT_t", [P, DB, 2])
        b_ada = sb("b_ada_sb", [P, 48])
        g1n = sb("g1n", [P, DB])
        scale1 = sb("scale1", [P, 2, DB])
        rstd = sb("rstd", [P, T])
        rms = sb("rms", [P, T])
        ps = k.ps
        x_in, small_in, silu_t, silu = k.sem("x_in"), k.sem("small_in"), k.sem("silu_t"), k.sem("silu")
        ada_in = [k.sem(f"ada_in{s}") for s in range(2)]
        rows, mod_turned = sb("mod_rows", [2, 6 * D]), k.sem("mod_turned")
        row_kept = [k.sem(f"row_kept{s}") for s in range(2)]
        ada_used = [k.sem(f"ada_used{s}") for s in range(2)]
        x_turned, x_kept, sq_done, ss_done = k.sem("x_turned"), k.sem("x_kept"), k.sem("sq_done"), k.sem("ss_done")
        ms_done, rms_done, norm_done = k.sem("ms_done"), k.sem("rms_done"), k.sem("norm_done")
        xt_out, h_done, dch = k.sem("xt_out"), k.sem("h_done"), k.sem("mod_dve")
        sq = x_rows[:, :, :].rearrange("p a b -> p (a b)").rearrange("p (k t) -> p k t", k=DB)
        block = ctx.enter_context(nc.Block())
        ada_v = k.w["w_ada"][0].rearrange("(k p) n -> p k n", p=P)
        ADA = 12
        masks_made, cut_made = k.sem("masks_made"), k.sem("cut_made")

        @block.gpsimd
        def _(pool):
            chunk_masks(pool, k, masks_made)

        @block.sync
        def _(sp):
            with nc.allow_non_contiguous_dma(reason="vectors over partitions"):
                sp.dma_start(sT_t[:, :, 0], k.w["c"][0].rearrange("(k p) -> p k", p=P)).then_inc(small_in, 16)
                sp.dma_start(sT_t[:, :, 1], k.w["c_ctx"].rearrange("(k p) -> p k", p=P)).then_inc(small_in, 16)
                sp.dma_start(b_ada[:, :], k.w["b_ada"][0].rearrange("(k p) -> p k", p=P)).then_inc(small_in, 16)
                sp.dma_start(g1n[:, :], k.w["norm1_g"][0].rearrange("(k p) -> p k", p=P)).then_inc(small_in, 16)
            sp.dma_start(x_rows[:, 0:TL, :], k.w["x"][0].rearrange("(t p) d -> p t d", p=P)).then_inc(x_in, 16)
            sp.dma_start(x_rows[:, TL:TT, :], k.w["ctx"][0].rearrange("(t p) d -> p t d", p=P)).then_inc(x_in, 16)
            for i in rounds(sp, ADA // 2):
                for s in range(2):
                    wait(sp, ada_used[s], i)
                    sp.dma_start(wada[s][:, :, :], ada_v[:, :, bass.ds((2 * i + s) * 512, 512)]).then_inc(ada_in[s], 16)
            sp.wait_ge(x_kept, TT * 2)
            sp.dma_start(k.xT_d.rearrange("(k p) t -> p k t", p=P), xT[:, :, 0:SEQ]).then_inc(xt_out, 16)
            sp.wait_ge(xt_out, 16)

        @block.tensor
        def _(pe):
            pe.wait_ge(x_in, 32)
            for t in range(TT):
                for g in range(2):
                    n = 2 * t + g
                    if n >= 4:
                        pe.wait_ge(x_kept, n - 3)
                    for j in range(4):
                        mm = pe.transpose(ps[:, n % 4, j * P:(j + 1) * P],
                                          x_rows[:, t, (4 * g + j) * P:(4 * g + j + 1) * P], k.ident[:, :])
                    mm.then_inc(x_turned, 1)
            pe.wait_ge(silu, 1)
            for i in rounds(pe, ADA // 2):
                for s in range(2):
                    pe.wait_ge(ada_in[s], 16 * i + 16)
                    wait(pe, row_kept[s], i)
                    for kb in range(DB):
                        mm = pe.matmul(ps[0:2, 6 + s, :], sT[:, kb, :], wada[s][:, kb, :],
                                       start=(kb == 0), stop=(kb == DB - 1))
                    mm.then_inc(ada_used[s], 1)
                if isinstance(i, int):
                    pe.wait_ge(sq_done, 1)
                    for lo, n, b in ((0, SEQ, 4), (SEQ, CTX, 5)):
                        for kb in range(DB):
                            mm = pe.matmul(ps[:, b, 0:n], k.ones[:, :], sq[:, kb, lo:lo + n],
                                           start=(kb == 0), stop=(kb == DB - 1))
                    mm.then_inc(ss_done, 1)
            for s in range(2):
                pe.wait_ge(row_kept[s], ADA // 2)
            for m in range(6 * DB):
                mm = pe.transpose(ps[:, 0, 2 * m:2 * m + 2], rows[:, m * P:(m + 1) * P], k.ident[0:2, 0:2])
            mm.then_inc(mod_turned, 1)

        @block.scalar
        def _(act):
            act.wait_ge(small_in, 64)
            act.activation(sT[:, :, :], sT_t[:, :, :], ACT.Tanh, scale=0.5).then_inc(silu_t, 1)
            for n in range(2 * TT):
                t, g = n // 2, n % 2
                act.wait_ge(x_turned, n + 1)
                act.activation(xT[:, 4 * g:4 * g + 4, t * P:(t + 1) * P],
                               ps[:, n % 4, :].rearrange("p (j t) -> p j t", j=4), ACT.Copy).then_inc(x_kept, 1)
            act.wait_ge(x_kept, 2 * TT)
            act.activation(sq, xT[:, :, :], ACT.Square).then_inc(sq_done, 1)
            for i in rounds(act, ADA // 2):
                for s in range(2):
                    act.wait_ge(ada_used[s], i + 1)
                    act.activation(rows[:, bass.ds((2 * i + s) * 512, 512)], ps[0:2, 6 + s, :], ACT.Copy)\
                       .then_inc(row_kept[s], 1)
                if isinstance(i, int):
                    act.wait_ge(ms_done, 1)
                    act.activation(rms[:, :], rms[:, :], ACT.Sqrt).then_inc(rms_done, 1)
            for kb in range(DB):
                act.wait_ge(norm_done, kb + 1)
                act.activation(k.hT[:, kb, 0:SEQ], k.hT[:, kb, 0:SEQ], ACT.Identity,
                               bias=k.mod[:, 0, kb:kb + 1]).then_inc(h_done, 1)
                act.activation(k.hT[:, kb, SEQ:T], k.hT[:, kb, SEQ:T], ACT.Identity,
                               bias=k.mod[:, 1, kb:kb + 1]).then_inc(h_done, 1)
            act.wait_ge(h_done, 2 * DB)

        @block.vector
        def _(dve):
            link = Chain(dve, dch)
            cut_masks(dve, k, cut_made)
            dve.wait_ge(silu_t, 1)
            link(dve.tensor_scalar(sT[:, :, :], sT[:, :, :], 0.5, 0.5, ALU.mult, ALU.add))
            dve.tensor_tensor(sT[:, :, :], sT[:, :, :], sT_t[:, :, :], ALU.mult).then_inc(silu, 1)
            dve.wait_ge(ss_done, 1)
            dve.tensor_scalar(rms[:, 0:SEQ], ps[:, 4, :], 1.0 / D, EPS, ALU.mult, ALU.add)
            dve.tensor_scalar(rms[:, SEQ:T], ps[:, 5, 0:CTX], 1.0 / D, EPS, ALU.mult, ALU.add).then_inc(ms_done, 1)
            dve.wait_ge(rms_done, 1)
            link(dve.reciprocal(rstd[:, :], rms[:, :]))
            dve.wait_ge(mod_turned, 1)
            for w in range(2):
                link(dve.tensor_tensor(k.mod[:, w, :], ps[:, 0, 0:96].rearrange("p (m w) -> p m w", w=2)[:, :, w],
                                       b_ada[:, :], ALU.add))
                link(dve.tensor_scalar(scale1[:, w, :], k.mod[:, w, DB:2 * DB], 1.0, None, ALU.add))
                link(dve.tensor_tensor(scale1[:, w, :], scale1[:, w, :], g1n[:, :], ALU.mult))
            for kb in range(DB):
                dve.scalar_tensor_tensor(k.hT[:, kb, 0:SEQ], xT[:, kb, 0:SEQ], scale1[:, 0, kb:kb + 1],
                                         rstd[:, 0:SEQ], ALU.mult, ALU.mult)
                dve.scalar_tensor_tensor(k.hT[:, kb, SEQ:T], xT[:, kb, SEQ:T], scale1[:, 1, kb:kb + 1],
                                         rstd[:, SEQ:T], ALU.mult, ALU.mult).then_inc(norm_done, 1)


def project(nc, k):
    ctx = ExitStack()
    with ctx:
        def sb(name, shape):
            return ctx.enter_context(nc.sbuf_tensor(name, shape, F32))
        w = [sb(f"w_slot{s}", [P, DB, P]) for s in range(2)]
        wv = [sb(f"wv{s}", [P, DB, 512]) for s in range(2)]
        wg = sb("wg", [P, DB, 16])
        raw = [sb(f"raw{s}", [P, T + 4]) for s in range(2)]
        own = [sb(f"own{s}", [P, T]) for s in range(2)]
        nb = sb("nb", [P, T])
        res = [sb(f"res{s}", [P, T]) for s in range(2)]
        pad = [sb(f"pad{b}", [P, GRID_H + 2, GRID_W + 2]) for b in range(4)]
        line = [sb(f"line{b}", [P, CTX + 2]) for b in range(4)]
        taps, conv_b = sb("taps", [P, 4, 9]), sb("conv_bias", [P, 4])
        kT, sq, kn, k_k = sb("kT_all", [P, 4, T]), sb("ksq_all", [P, 4, T]), sb("kk_all", [P, 4, T]), sb("k_k", [P, 4])
        mu = sb("mu", [P, NRW])
        mu1 = sb("mu1", [P, NRW])
        muh = sb("muh", [P, NRW])
        ps = k.ps
        w_in_s = [k.sem(f"w_in{s}") for s in range(2)]
        wv_in, wg_in, mu_in, mu_done = k.sem("wv_in"), k.sem("wg_in"), k.sem("mu_in"), k.sem("mu_done")
        rows_done, rows_kept, nbs = k.sem("rows_done"), k.sem("rows_kept"), k.sem("neighbours_added")
        mm_done, ps_kept, shifted, stored = (
            [k.sem(f"{what}{s}") for s in range(2)] for what in ("mm_done", "ps_kept", "shifted", "stored"))
        borders, conv_in, conv_step, k_in, k_k_in, ksq_done, ksum_done, knorm, k_rooted, k_inv, kk_done, kk_out = (
            k.sem(n) for n in "borders conv_in conv_step k_in k_k_in ksq_done ksum_done knorm k_rooted k_inv kk_done kk_out".split())
        block = ctx.enter_context(nc.Block())
        w_v = k.w["w_in"][0].rearrange("(k p) n -> p k n", p=P)
        QK, NGT = 4, 16
        RW_LOOP = (NRW - 1) // 2
        N_RW = [(NRW + 1) // 2, NRW // 2]
        GATE_N = [QK // 2 + N_RW[0], QK // 2 + N_RW[1]]
        GATE_SLOTS = (NRW % 2, 1 - NRW % 2)

        @block.sync
        def _(sp):
            def load(s, n, col, first=False):
                if not first:
                    sp.wait_ge(mm_done[s], n)
                sp.dma_start(w[s][:, :, :], w_v[:, :, bass.ds(col, P)]).then_inc(w_in_s[s], 16)
            with nc.allow_non_contiguous_dma(reason="a vector over partitions"):
                sp.dma_start(mu[:, :], k.w["rw_mu"][0].rearrange("(b p) -> p b", p=P)).then_inc(mu_in, 16)
                sp.dma_start(k_k[:, :], k.w["rw_k_k"][0].rearrange("(b p) -> p b", p=P)).then_inc(k_k_in, 16)
                for blk in range(4):
                    sp.dma_start(taps[:, blk, :], k.w["ml_conv_k"][0].rearrange("a b (k p) -> k p (a b)", p=P)[blk])\
                        .then_inc(conv_in, 16)
                sp.dma_start(conv_b[:, :], k.w["ml_conv_b"][0].rearrange("(k p) -> p k", p=P)).then_inc(conv_in, 16)
            for u in range(QK):
                load(u % 2, u // 2, COL_Q + u * P, first=u < 2)
            for i in rounds(sp, RW_LOOP):
                for s in range(2):
                    load(s, QK // 2 + i, COL_RW + (2 * i + s) * P)
            load(0, QK // 2 + RW_LOOP, COL_RW + (NRW - 1) * P)
            for s in range(2):
                sp.wait_ge(stored[s], 16 * 4)
            sp.dma_start(kT[:, :, :], k.rw_d[4:8].rearrange("b p t -> p b t")).then_inc(k_in, 16)
            for i in rounds(sp, NGT // 2):
                for j, s in enumerate(GATE_SLOTS):
                    load(s, GATE_N[s] + i, COL_GT + (2 * i + j) * P)
            sp.dma_start(wv[0][:, :, :], w_v[:, :, COL_V:COL_V + 512]).then_inc(wv_in, 16)
            sp.dma_start(wv[1][:, :, :], w_v[:, :, COL_O:COL_O + 512]).then_inc(wv_in, 16)
            sp.dma_start(wg[:, :, :], w_v[:, :, COL_G:COL_G + 16]).then_inc(wg_in, 16)
            sp.wait_ge(kk_done, 4)
            sp.dma_start(k.kk_d.rearrange("b p t -> p b t"), kn[:, :, :]).then_inc(kk_out, 16)
            sp.wait_ge(kk_out, 16)

        @block.tensor
        def _(pe):
            def cols(s, n, n_ctx, first=False):
                pe.wait_ge(w_in_s[s], n * 16 + 16)
                if not first:
                    pe.wait_ge(ps_kept[s], n)
                for lo, m, b in ((0, SEQ, 2 * s), (SEQ, n_ctx, 2 * s + 1)):
                    for kb in range(DB if m else 0):
                        mm = pe.matmul(ps[:, b, 0:m], w[s][:, kb, :], k.hT[:, kb, lo:lo + m],
                                       start=(kb == 0), stop=(kb == DB - 1))
                mm.then_inc(mm_done[s], 1)
            for u in range(QK):
                cols(u % 2, u // 2, CTX, first=u < 2)
            for i in rounds(pe, RW_LOOP):
                for s in range(2):
                    cols(s, QK // 2 + i, CTX)
            cols(0, QK // 2 + RW_LOOP, CTX)
            for i in rounds(pe, NGT // 2):
                for s in GATE_SLOTS:
                    cols(s, GATE_N[s] + i, 0)
                if isinstance(i, int):
                    for b in range(4):
                        pe.wait_ge(ksq_done, b + 1)
                        if b >= 2:
                            pe.wait_ge(knorm, b - 1)
                        for lo, n, j in ((0, SEQ, 0), (SEQ, CTX, 1)):
                            mm = pe.matmul(ps[:, 4 + 2 * (b % 2) + j, 0:n], k.same_head[:, :], sq[:, b, lo:lo + n],
                                           start=True, stop=True)
                        mm.then_inc(ksum_done, 1)
            pe.wait_ge(knorm, 4)
            pe.wait_ge(wv_in, 32)
            n = 0
            for j, tiles in ((0, TT), (1, TL)):
                for t in range(tiles):
                    if n >= 2:
                        pe.wait_ge(rows_kept, n - 1)
                    for kb in range(DB):
                        mm = pe.matmul(ps[:, 4 + n % 2, :], k.hT[:, kb, t * P:(t + 1) * P], wv[j][:, kb, :],
                                       start=(kb == 0), stop=(kb == DB - 1))
                    mm.then_inc(rows_done, 1)
                    n += 1
            pe.wait_ge(wg_in, 16)
            for t in range(TT):
                for kb in range(DB):
                    mm = pe.matmul(ps[:, 6, 16 * t:16 * t + 16], k.hT[:, kb, t * P:(t + 1) * P], wg[:, kb, :],
                                   start=(kb == 0), stop=(kb == DB - 1))
            mm.then_inc(rows_done, 1)

        @block.scalar
        def _(act):
            for u in range(QK):
                s = u % 2
                act.wait_ge(borders, 8)
                act.wait_ge(mm_done[s], u // 2 + 1)
                act.activation(pad[u][:, 1:1 + GRID_H, 1:1 + GRID_W],
                               ps[:, 2 * s, :].rearrange("p (r w) -> p r w", w=GRID_W), ACT.Copy)
                act.activation(line[u][:, 1:1 + CTX], ps[:, 2 * s + 1, 0:CTX], ACT.Copy).then_inc(ps_kept[s], 1)
            act.wait_ge(mu_done, 3)

            def keep(s, m, i):
                act.wait_ge(mm_done[s], QK // 2 + m + 1)
                wait(act, shifted[s], m)
                a, b = ps[:, 2 * s, :], ps[:, 2 * s + 1, 0:CTX]
                act.activation(raw[s][:, 1:SEQ + 1], a, ACT.Copy)
                act.activation(raw[s][:, SEQ + 3:T + 3], b, ACT.Copy)
                act.activation(own[s][:, 0:SEQ], a, ACT.Copy, scale=mu1[:, bass.ds(i, 1)])
                act.activation(own[s][:, SEQ:T], b, ACT.Copy, scale=mu1[:, bass.ds(i, 1)]).then_inc(ps_kept[s], 1)
            for i in rounds(act, RW_LOOP):
                for s in range(2):
                    keep(s, i, 2 * i + s)
            keep(0, RW_LOOP, NRW - 1)
            act.wait_ge(k_k_in, 16)
            act.wait_ge(k_in, 16)
            for b in range(4):
                act.activation(sq[:, b, :], kT[:, b, :], ACT.Square, scale=k_k[:, b:b + 1]).then_inc(ksq_done, 1)
            for s in range(2):
                act.wait_ge(shifted[s], N_RW[s])
            for i in rounds(act, NGT // 2):
                for s in GATE_SLOTS:
                    act.wait_ge(mm_done[s], GATE_N[s] + i + 1)
                    if not isinstance(i, int):
                        act.wait_ge(stored[s], 16 * i + 16 * N_RW[s])
                    act.activation(own[s][:, 0:SEQ], ps[:, 2 * s, :], ACT.Tanh, scale=0.5).then_inc(ps_kept[s], 1)
                if isinstance(i, int):
                    act.wait_ge(knorm, 4)
                    act.activation(sq[:, :, :], sq[:, :, :], ACT.Sqrt).then_inc(k_rooted, 1)
            n = 0
            for j, tiles in ((0, TT), (1, TL)):
                for t in range(tiles):
                    act.wait_ge(rows_done, n + 1)
                    if j:
                        ins = act.activation(k.o_ml[:, t, :], ps[:, 4 + n % 2, :], ACT.Tanh, scale=0.5)
                    else:
                        ins = act.activation(k.v_ml[:, t, :, 0:DV], ps[:, 4 + n % 2, :].rearrange("p (h v) -> p h v", v=DV),
                                             ACT.Copy)
                    ins.then_inc(rows_kept, 1)
                    n += 1
            act.wait_ge(rows_done, n + 1)
            act.activation(k.g_ml[:, :, :], ps[:, 6, 0:16 * TT].rearrange("p (t g) -> p t g", t=TT),
                           ACT.Copy).then_inc(rows_kept, 1)
            act.wait_ge(rows_kept, n + 1)

        @block.vector
        def _(dve):
            for s in range(2):
                dve.memset(raw[s][:, :], 0.0)
            dve.wait_ge(mu_in, 16)
            dve.tensor_scalar(mu1[:, :], mu[:, :], -1.0, 1.0, ALU.mult, ALU.add).then_inc(mu_done, 1)
            dve.tensor_scalar(muh[:, :], mu[:, :], 0.5, None, ALU.mult).then_inc(mu_done, 1)
            dve.wait_ge(mu_done, 2)
            dve.memset(nb[:, 0:1], 0.0).then_inc(mu_done, 1)
            dve.wait_ge(mu_done, 3)

            def shift(s, m, i):
                r = raw[s]
                dve.wait_ge(ps_kept[s], QK // 2 + m + 1)
                dve.tensor_tensor(nb[:, 0:SEQ], r[:, 0:SEQ], r[:, 2:SEQ + 2], ALU.add)
                dve.tensor_tensor(nb[:, SEQ:T], r[:, SEQ + 2:T + 2], r[:, SEQ + 4:T + 4], ALU.add).then_inc(nbs, 1)
                dve.wait_ge(nbs, i + 1)
                wait(dve, stored[s], 16 * m)
                dve.scalar_tensor_tensor(res[s][:, :], nb[:, :], muh[:, bass.ds(i, 1)], own[s][:, :],
                                         ALU.mult, ALU.add).then_inc(shifted[s], 1)
                dve.wait_ge(shifted[s], m + 1)
            for i in rounds(dve, RW_LOOP):
                for s in range(2):
                    shift(s, i, 2 * i + s)
            shift(0, RW_LOOP, NRW - 1)
            link = Chain(dve, conv_step)

            def conv(b):
                lat = k.conv[:, b, 0:SEQ].rearrange("p (r w) -> p r w", w=GRID_W)
                cx = k.conv[:, b, SEQ:T]
                for tap in range(9):
                    dy, dx = tap // 3, tap % 3
                    img = pad[b][:, dy:dy + GRID_H, dx:dx + GRID_W]
                    if tap == 0:
                        ins = dve.tensor_scalar(lat, img, taps[:, b, 0:1], conv_b[:, b:b + 1], ALU.mult, ALU.add)
                    else:
                        ins = dve.scalar_tensor_tensor(lat, img, taps[:, b, tap:tap + 1], lat, ALU.mult, ALU.add)
                    link(ins)
                    if b >= 2 and 3 <= tap < 6:
                        ln = line[b][:, dx:dx + CTX]
                        if tap == 3:
                            link(dve.tensor_scalar(cx, ln, taps[:, b, 3:4], conv_b[:, b:b + 1], ALU.mult, ALU.add))
                        else:
                            link(dve.scalar_tensor_tensor(cx, ln, taps[:, b, tap:tap + 1], cx, ALU.mult, ALU.add))
                if b >= 2:
                    link(dve.tensor_scalar(k.conv[:, b, :], k.conv[:, b, :], DQK ** -0.5, None, ALU.mult))
            dve.wait_ge(conv_in, 16 * 5)
            for s in range(2):
                dve.wait_ge(ps_kept[s], QK // 2)
            conv(0)
            for b in range(4):
                dve.wait_ge(ksum_done, b + 1)
                for lo, n, j in ((0, SEQ, 0), (SEQ, CTX, 1)):
                    ins = dve.tensor_scalar(sq[:, b, lo:lo + n], ps[:, 4 + 2 * (b % 2) + j, 0:n], 1e-12, None, ALU.add)
                ins.then_inc(knorm, 1)
            conv(1)
            dve.wait_ge(k_rooted, 1)
            dve.reciprocal(kn[:, :, :], sq[:, :, :]).then_inc(k_inv, 1)
            dve.wait_ge(k_inv, 1)
            for b in range(4):
                dve.scalar_tensor_tensor(kn[:, b, :], kT[:, b, :], k_k[:, b:b + 1], kn[:, b, :], ALU.mult, ALU.mult)\
                   .then_inc(kk_done, 1)
            conv(2)
            conv(3)
            dve.wait_ge(rows_kept, TT + TL)
            dve.tensor_scalar(k.o_ml[:, :, :], k.o_ml[:, :, :], 0.5, 0.5, ALU.mult, ALU.add).then_inc(mu_done, 1)
            dve.wait_ge(mu_done, 4)

        @block.gpsimd
        def _(pool):
            for b in range(4):
                pool.memset(pad[b][:, :, :], 0.0).then_inc(borders, 1)
                pool.memset(line[b][:, :], 0.0).then_inc(borders, 1)

            def store(s, m, i):
                pool.wait_ge(shifted[s], m + 1)
                pool.dma_start(k.rw_d[bass.ds(i, 1)].rearrange("a p t -> p (a t)"), res[s][:, :]).then_inc(stored[s], 16)
            for i in rounds(pool, RW_LOOP):
                for s in range(2):
                    store(s, i, 2 * i + s)
            store(0, RW_LOOP, NRW - 1)
            for i in rounds(pool, NGT // 2):
                for j, s in enumerate(GATE_SLOTS):
                    pool.wait_ge(ps_kept[s], GATE_N[s] + i + 1)
                    pool.dma_start(k.gt_d[bass.ds(2 * i + j, 1)].rearrange("a p t -> p (a t)"), own[s][:, 0:SEQ])\
                        .then_inc(stored[s], 16)
            for s in range(2):
                pool.wait_ge(stored[s], 16 * (N_RW[s] + NGT // 2))


def masks(nc, k):
    with nc.Block() as block:
        made = k.sem("mask_made")

        @block.gpsimd
        def _(pool):
            n = 0
            for value, mask in ((1.0, k.upto), (1.0, k.onward), (0.0, k.neg_upto), (0.0, k.neg_onward)):
                pool.memset(mask[:, :], value).then_inc(made, 1)
                n += 1
            pool.wait_ge(made, n)
            for fill, sign, mask in ((0.0, 1, k.upto), (0.0, -1, k.onward), (LOG_ZERO, 1, k.neg_upto), (LOG_ZERO, -1, k.neg_onward)):
                pool.affine_select(out=mask[:, :], in_=mask[:, :], compare_op=ALU.is_ge, fill=fill, base=0,
                                   pattern=[[sign, P]], channel_multiplier=-sign).then_inc(made, 1)
                n += 1
            pool.wait_ge(made, n)


LOG_ZERO = -1e6
GATE_CAP = 15.0
VW = DV + 1


def mlstm(nc, k):
    ctx = ExitStack()
    with ctx:
        def sb(name, shape):
            return ctx.enter_context(nc.sbuf_tensor(name, shape, F32))
        gate_b = sb("gate_bias", [P, 16])
        norm_g = sb("ml_norm", [P, 4])
        conv = k.conv
        kN = sb("k_rows", [P, TT, 256])
        kw = sb("k_weighted", [P, 2, TT, 256])
        pre = sb("pre", [P, TT, 16])
        lf = sb("lf", [P, TT, 8])
        dec = sb("dec", [P, TT, 16])
        ib, eb, wk, carry = sb("ib", [P, TT, 8]), sb("eb", [P, TT, 8]), sb("wk", [P, TT, 8]), sb("carry", [P, TT, 8])
        carry2 = sb("carry2", [P, TT, 2, 2])
        Cs = sb("C_states", [P, 2, TT - 1, 2, VW])
        E = [sb(f"E{s}", [P, 4, P]) for s in range(2)]
        Wt = [sb(f"Wt{s}", [P, 4, P]) for s in range(2)]
        tmp = [sb(f"tmp{s}", [P, 4, VW]) for s in range(2)]
        den, den2 = sb("den", [P, 4]), sb("den2", [P, 4])
        hs = sb("h_sum", [P, TL, 4, DV])
        hq = sb("h_sq", [P, TL, 4, DV])
        ms = sb("h_ms", [P, TL, 4])
        aT = sb("aT", [P, 4, SEQ])
        ps = k.ps
        small_in, filled, dch = k.sem("ml_small"), k.sem("filled"), k.sem("ml_dve")
        pre_t, pre_done, soft, lf_done, cum_done = k.sem("pre_t"), k.sem("pre_done"), k.sem("soft"), k.sem("lf_done"), k.sem("cum_done")
        k_turned, k_kept, dec_done, exps_done = k.sem("k_turned"), k.sem("k_kept"), k.sem("dec_done"), k.sem("exps_done")
        kw_done, upd_ready, state_done, c2_done = k.sem("kw_done"), k.sem("upd_ready"), k.sem("state_done"), k.sem("c2_done")
        s_ready, e_ready, inter_ready, intra_ready = k.sem("s_ready"), k.sem("e_ready"), k.sem("inter_ready"), k.sem("intra_ready")
        exp_done, inter_kept, w_done, intra_used = k.sem("exp_done"), k.sem("inter_kept"), k.sem("w_done"), k.sem("intra_used")
        h_done, sq_done, ms_done, rms_done = k.sem("mh_done"), k.sem("msq_done"), k.sem("mms_done"), k.sem("mrms_done")
        hn_done, gated, a_turned, a_kept, a_out = k.sem("hn_done"), k.sem("gated"), k.sem("a_turned"), k.sem("a_kept"), k.sem("a_out")
        zeros, zero_out = sb("zero_rows", [P, D]), k.sem("zero_rows_out")
        order = [[4, 5, 0, 1, 2, 3], [5, 4, 3, 2, 1, 0]]
        block = ctx.enter_context(nc.Block())

        @block.sync
        def _(sp):
            with nc.allow_non_contiguous_dma(reason="vectors over partitions"):
                sp.dma_start(norm_g[:, :], k.w["ml_norm_g"][0].rearrange("(k p) -> p k", p=P)).then_inc(small_in, 16)
            sp.dma_start(gate_b[:, :], k.w["ml_gate_b"].rearrange("l a b h -> l (a b h)").to_broadcast([P, 16]))\
                .then_inc(small_in, 16)
            sp.wait_ge(filled, 2)
            for blk in range(FEWEST, BLOCKS):
                sp.dma_start(k.ys_d[blk * P:(blk + 1) * P, :], zeros[:, :]).then_inc(zero_out, 16)
            sp.wait_ge(zero_out, 16 * (BLOCKS - FEWEST))
            sp.wait_ge(a_kept, TL * 4)
            sp.dma_start(k.aT_d.rearrange("b p t -> p b t"), aT[:, :, :]).then_inc(a_out, 16)
            sp.wait_ge(a_out, 16)

        @block.gpsimd
        def _(pool):
            pool.memset(k.v_ml[:, :, :, DV:VW], 1.0).then_inc(filled, 1)
            pool.memset(zeros[:, :], 0.0).then_inc(filled, 1)
            pool.wait_ge(small_in, 16 * 2)
            pool.tensor_tensor(pre[:, :, :], k.g_ml[:, :, :], gate_b[:, :].unsqueeze(1).to_broadcast([P, TT, 16]),
                               ALU.add).then_inc(pre_done, 1)
            pool.wait_ge(k_kept, 3)
            pool.wait_ge(exps_done, 3)
            for i in range(TT - 1):
                for d in range(2):
                    t = order[d][i]
                    pool.tensor_tensor(kw[:, d, t, :].rearrange("p (h j) -> p h j", h=4),
                                       kN[:, t, :].rearrange("p (h j) -> p h j", h=4),
                                       bc(wk[:, t, 4 * d:4 * d + 4], DQK), ALU.mult).then_inc(kw_done, 1)
            for t in range(TL):
                pool.wait_ge(h_done, 2 * t + 2)
                pool.tensor_tensor(hq[:, t, :, :], hs[:, t, :, :], hs[:, t, :, :], ALU.mult).then_inc(sq_done, 1)
            for t in range(TL):
                pool.wait_ge(hn_done, t + 1)
                pool.tensor_tensor(hs[:, t, :, :].rearrange("p h v -> p (h v)"),
                                   hs[:, t, :, :].rearrange("p h v -> p (h v)"), k.o_ml[:, t, :],
                                   ALU.mult).then_inc(gated, 1)

        @block.tensor
        def _(pe):
            pe.wait_ge(lf_done, 1)
            for t in range(TT):
                for lhs, lo, n, at in ((k.upto, 0, 4, 0), (k.onward, 4, 4, 4), (k.ones, 0, 8, 8)):
                    mm = pe.matmul(ps[:, 7, t * 16 + at:t * 16 + at + n], lhs[:, :], lf[:, t, lo:lo + n],
                                   start=True, stop=True)
            mm.then_inc(cum_done, 1)
            pe.wait_ge(filled, 2)
            for n in range(3):
                for j in range(4):
                    t, blk = (4 * n + j) // 2, j % 2
                    mm = pe.transpose(ps[:, n, j * P:(j + 1) * P], conv[:, 2 + blk, t * P:(t + 1) * P], k.ident[:, :])
                mm.then_inc(k_turned, 1)
            for i in range(TT - 1):
                for d in range(2):
                    t = order[d][i]
                    pe.wait_ge(kw_done, 2 * i + d + 1)
                    if i:
                        pe.wait_ge(state_done, 2 * (i - 1) + d + 1)
                    for h in range(4):
                        q0 = 64 * (h % 2)
                        mm = pe.matmul(ps[q0:q0 + 64, 5 + d, (h // 2) * VW:(h // 2 + 1) * VW],
                                       kw[:, d, t, h * DQK:(h + 1) * DQK], k.v_ml[:, t, h, :], start=True, stop=True)
                    mm.then_inc(upd_ready, 1)

            def before(n):
                t, d = n // 2, n % 2
                if d == 0:
                    if t:
                        pe.wait_ge(w_done, 2 * t)
                    else:
                        pe.wait_ge(k_kept, 3)
                    for h in range(4):
                        q0 = 64 * (h % 2)
                        mm = pe.matmul(ps[:, h % 2, (h // 2) * P:(h // 2 + 1) * P],
                                       conv[q0:q0 + 64, 2 + h // 2, t * P:(t + 1) * P],
                                       conv[q0:q0 + 64, h // 2, t * P:(t + 1) * P], start=True, stop=True)
                    mm.then_inc(s_ready, 1)
                if n:
                    pe.wait_ge(exp_done, n)
                for h in range(4):
                    pe.matmul(ps[:, 2, h * P:(h + 1) * P], lf[:, t, 4 * d + h:4 * d + h + 1].to_broadcast([P, P]),
                              (k.onward if d else k.upto)[:, :], start=True, stop=False)
                    mm = pe.matmul(ps[:, 2, h * P:(h + 1) * P], k.ident[:, :],
                                   (k.neg_onward if d else k.neg_upto)[:, :], start=False, stop=True)
                mm.then_inc(e_ready, 1)
                i = order[d].index(t) - 1
                pe.wait_ge(state_done, 2 * (TT - 1))
                if n:
                    pe.wait_ge(inter_kept, n)
                for h in range(4):
                    q0 = 64 * (h % 2)
                    mm = pe.matmul(ps[:, 5 + h % 2, (h // 2) * VW:(h // 2 + 1) * VW],
                                   conv[q0:q0 + 64, h // 2, t * P:(t + 1) * P], Cs[q0:q0 + 64, d, i, h // 2, :],
                                   start=True, stop=True)
                mm.then_inc(inter_ready, 1)
            before(0)
            for n in range(2 * TL):
                if n + 1 < 2 * TL:
                    before(n + 1)
                pe.wait_ge(w_done, n + 1)
                if n:
                    pe.wait_ge(intra_used, n)
                for h in range(4):
                    mm = pe.matmul(ps[:, 3 + h // 2, (h % 2) * VW:(h % 2 + 1) * VW], Wt[n % 2][:, h, :],
                                   k.v_ml[:, n // 2, h, :], start=True, stop=True)
                mm.then_inc(intra_ready, 1)
            for t in range(TL):
                pe.wait_ge(gated, t + 1)
                for j in range(4):
                    mm = pe.transpose(ps[:, t, j * P:(j + 1) * P], hs[:, t, j, :], k.ident[:, :])
                mm.then_inc(a_turned, 1)

        @block.scalar
        def _(act):
            act.wait_ge(pre_done, 1)
            act.activation(pre[:, :, :], pre[:, :, :], ACT.Tanh, scale=1.0 / GATE_CAP).then_inc(pre_t, 1)
            act.wait_ge(pre_t, 1)
            act.activation(lf[:, :, :], pre[:, :, 8:16], ACT.Exp, scale=-GATE_CAP).then_inc(soft, 1)
            act.wait_ge(soft, 2)
            act.activation(lf[:, :, :], lf[:, :, :], ACT.Ln).then_inc(soft, 1)
            for n in range(3):
                act.wait_ge(k_turned, n + 1)
                act.activation(kN[:, 2 * n:2 * n + 2, :].rearrange("p t c -> p (t c)"), ps[:, n, :], ACT.Copy)\
                   .then_inc(k_kept, 1)
            act.wait_ge(dec_done, 3)
            act.activation(eb[:, :, :], dec[:, :, 0:8], ACT.Exp).then_inc(exps_done, 1)
            act.activation(carry[:, :, :], dec[:, :, 8:16], ACT.Exp).then_inc(exps_done, 1)
            act.activation(wk[:, :, :], wk[:, :, :], ACT.Exp).then_inc(exps_done, 1)
            act.wait_ge(exps_done, 3)
            for n in range(2 * TL):
                t, d = n // 2, n % 2
                act.wait_ge(e_ready, n + 1)
                if n >= 2:
                    act.wait_ge(w_done, n - 1)
                for h in range(4):
                    ins = act.activation(E[n % 2][:, h, :], ps[:, 2, h * P:(h + 1) * P], ACT.Exp,
                                         bias=ib[:, t, 4 * d + h:4 * d + h + 1])
                ins.then_inc(exp_done, 1)
                act.wait_ge(inter_ready, n + 1)
                if n >= 2:
                    act.wait_ge(h_done, n - 1)
                for h in range(4):
                    ins = act.activation(tmp[n % 2][:, h, :], ps[:, 5 + h % 2, (h // 2) * VW:(h // 2 + 1) * VW],
                                         ACT.Copy, scale=eb[:, t, 4 * d + h:4 * d + h + 1])
                ins.then_inc(inter_kept, 1)
            act.wait_ge(ms_done, 1)
            act.activation(ms[:, :, :], ms[:, :, :], ACT.Sqrt).then_inc(rms_done, 1)
            for t in range(TL):
                act.wait_ge(a_turned, t + 1)
                for j in range(4):
                    act.activation(aT[:, j, t * P:(t + 1) * P], ps[:, t, j * P:(j + 1) * P], ACT.Copy,
                                   scale=norm_g[:, j:j + 1]).then_inc(a_kept, 1)

        @block.vector
        def _(dve):
            link = Chain(dve, dch)

            def gates():
                dve.wait_ge(soft, 1)
                dve.tensor_scalar(lf[:, :, :], lf[:, :, :], 1.0, None, ALU.add).then_inc(soft, 1)
                dve.wait_ge(soft, 3)
                dve.tensor_scalar(lf[:, :, :], lf[:, :, :], -1.0, None, ALU.mult).then_inc(lf_done, 1)
                dve.wait_ge(cum_done, 1)
                link(dve.tensor_copy(dec[:, :, :].rearrange("p t g -> p (t g)"), ps[:, 7, 0:16 * TT]))
                dve.scalar_tensor_tensor(ib[:, :, :], pre[:, :, 0:8], GATE_CAP, dec[:, :, 0:8], ALU.mult,
                                         ALU.subtract).then_inc(dec_done, 1)
                dve.wait_ge(dec_done, 1)
                dve.tensor_tensor(wk[:, :, :], ib[:, :, :], dec[:, :, 8:16], ALU.add).then_inc(dec_done, 1)
                dve.tensor_copy(den[:, :], dec[:, 0, 0:4]).then_inc(dec_done, 1)

            gates()
            dve.wait_ge(exps_done, 3)
            for p in range(2):
                for half in range(2):
                    q = slice(64 * half, 64 * half + 64)
                    for d in range(2):
                        ins = dve.tensor_copy(carry2[q, :, d, p], carry[q, :, 4 * d + 2 * p + half])
            link(ins)
            for i in range(TT - 1):
                for d in range(2):
                    t = order[d][i]
                    dve.wait_ge(upd_ready, 2 * i + d + 1)
                    if i == 0:
                        ins = dve.tensor_copy(Cs[:, d, 0, :, :].rearrange("p a v -> p (a v)"), ps[:, 5 + d, 0:2 * VW])
                    else:
                        dve.wait_ge(state_done, 2 * (i - 1) + d + 1)
                        for p in range(2):
                            ins = dve.scalar_tensor_tensor(Cs[:, d, i, p, :], Cs[:, d, i - 1, p, :],
                                                           carry2[:, t, d, p:p + 1], ps[:, 5 + d, p * VW:(p + 1) * VW],
                                                           ALU.mult, ALU.add)
                    ins.then_inc(state_done, 1)

            def weigh(n):
                t = n // 2
                dve.wait_ge(s_ready, t + 1)
                dve.wait_ge(exp_done, n + 1)
                if n >= 2:
                    dve.wait_ge(intra_ready, n - 1)
                for par in range(2):
                    ins = dve.tensor_tensor(Wt[n % 2][:, par::2, :], ps[:, par, 0:2 * P].rearrange("p (a t) -> p a t", a=2),
                                            E[n % 2][:, par::2, :], ALU.mult)
                ins.then_inc(w_done, 1)
            weigh(0)
            for n in range(2 * TL):
                if n + 1 < 2 * TL:
                    weigh(n + 1)
                t, d = n // 2, n % 2
                x = tmp[n % 2]
                dve.wait_ge(intra_ready, n + 1)
                dve.wait_ge(inter_kept, n + 1)
                for a in range(2):
                    ins = dve.tensor_tensor(x[:, 2 * a:2 * a + 2, :], x[:, 2 * a:2 * a + 2, :],
                                            ps[:, 3 + a, 0:2 * VW].rearrange("p (a v) -> p a v", a=2), ALU.add)
                ins.then_inc(intra_used, 1)
                dve.wait_ge(intra_used, n + 1)
                link(dve.scalar_tensor_tensor(den[:, :], x[:, :, DV], -1.0, x[:, :, DV], ALU.mult, ALU.max))
                link(dve.tensor_scalar(den2[:, :], den[:, :], 1.0, None, ALU.max))
                link(dve.reciprocal(den[:, :], den2[:, :]))
                for h in range(4):
                    if d == 0:
                        ins = dve.tensor_scalar(hs[:, t, h, :], x[:, h, 0:DV], den[:, h:h + 1], None, ALU.mult)
                    else:
                        ins = dve.scalar_tensor_tensor(hs[:, t, h, :], x[:, h, 0:DV], den[:, h:h + 1],
                                                       hs[:, t, h, :], ALU.mult, ALU.add)
                ins.then_inc(h_done, 1)
                dve.wait_ge(h_done, n + 1)
            dve.wait_ge(sq_done, TL)
            link(dve.tensor_reduce(ms[:, :, :], hq[:, :, :, :], AX.X, ALU.add))
            dve.tensor_scalar(ms[:, :, :], ms[:, :, :], 1.0 / DV, EPS, ALU.mult, ALU.add).then_inc(ms_done, 1)
            dve.wait_ge(rms_done, 1)
            link(dve.reciprocal(hq[:, 0, 0, 0:4 * TL], ms[:, :, :].rearrange("p t h -> p (t h)")))
            for t in range(TL):
                dve.tensor_tensor(hs[:, t, :, :], hs[:, t, :, :], bc(hq[:, 0, 0, 4 * t:4 * t + 4], DV), ALU.mult)\
                   .then_inc(hn_done, 1)


CTX_GROUP = 2
NG = NC // 4
LEVELS = [2, 4, 8, 16, 32]
NV_ = 10
V_HALF, V_HKA, V_1HKA, V_RK, V_W0, V_A0, V_MHALF = 0, 1, 2, 3, 4, 6, 8


def rwkv(nc, k):
    ctx = ExitStack()
    with ctx:
        def sb(name, shape):
            return ctx.enter_context(nc.sbuf_tensor(name, shape, F32))
        E_, O_ = slice(0, 64), slice(64, 128)
        wd_t, ad = sb("wd_t", [P, T]), sb("ad", [P, T])
        w_up, a_up = sb("w_up_b", [P, P]), sb("a_up_b", [P, P])
        vec = sb("rw_vec", [P, 4 * NV_])
        vec3 = vec[:, :].rearrange("p (b n) -> p b n", b=4)
        rT, kT, vT, kk = sb("rT_b", [P, SEQ]), sb("kT_b", [P, T]), sb("vT_b", [P, T]), sb("kk_b", [P, T])
        th_w, th_a = sb("th_w", [P, T]), sb("th_a", [P, T])
        cum, cumx = sb("cum", [P, T]), sb("cumx", [P, T])
        e_inc, e_neg, e_exc = sb("e_inc", [P, T]), sb("e_neg", [P, T]), sb("e_exc", [P, T])
        kf, nb = sb("k_factor", [P, T]), sb("minus_b", [P, T])
        kd_sum = sb("kd_sum", [P, SEQ])
        rk_head = sb("rk_head", [P, P])
        AR = [sb(f"AR{d}", [P, NC, 2, C]) for d in range(2)]
        BKB = sb("BKB", [P, NC, 3, C])
        BKn = sb("BK_rows", [P, NC, 2, C])
        mva = sb("MV_A", [P, NC, 2, C])
        LT, Tm, Um, X = (sb(n, [P, NC, P]) for n in ("LT", "Tm", "Um", "Xm"))
        GA = sb("GA", [P, NC, 2, C])
        TA = sb("TA", [P, NC, P])
        BP = sb("BP", [P, NC, 2, C])
        vz = sb("v_rows", [P, NC, 2, C])
        GR = [sb(f"GR{d}", [P, NCL, 2, C]) for d in range(2)]
        sv = [sb(f"sa_v{d}", [P, NC, 2, C]) for d in range(2)]
        GT = [sb(f"GT{d}", [P, NC, P]) for d in range(2)]
        RT = [sb(f"RT{d}", [P, NCL, P]) for d in range(2)]
        Hg = [sb(f"Hg{d}", [P, NC, C]) for d in range(2)]
        S = [sb(f"S{d}", [P, NC, C]) for d in range(2)]
        gam = [sb(f"gam{d}", [P, NC]) for d in range(2)]
        gam_next = sb("gam_next", [P, NC])
        y_sb, bon = sb("y_sb", [P, SEQ]), sb("bonus", [P, SEQ])
        ps = k.ps
        names = ("rw_static rw_vec_done up_in key_in v_in th_done lora_done v_turned v_kept cum_done exps "
                 "dve_prep pool_prep s1_ready s1_kept tr_ready tr_kept lt_done u0_done t0_ready t0_kept mv_ready mv_kept "
                 "x_ready x_kept tu_ready tu_kept tm_ready pool_half sa_kept ta_kept gr_ready gr_kept hh_ready hh_kept "
                 "step_ready step_done y_ready y_kept y_out bonus_in bonus_ready bonus_kept bonus_out zeroed rw_dve own_result w_done keys_step kf_made share_ready share_kept").split()
        s = {n: k.sem("r_" + n) for n in names}
        order = [[8, 9, 10, 11, 0, 1, 2, 3, 4, 5, 6, 7], [11, 10, 9, 8, 7, 6, 5, 4, 3, 2, 1, 0]]
        MV_BANK, TM_BANK = (6, 7, 5), (6, 7, 0)
        steps = NC - 2

        def grp(g):
            return slice(4 * g, 4 * g + 4)

        def bank(i, n=128):
            return ps[:, i, 0:4 * n].rearrange("p (c x) -> p c x", c=4)

        def col(b, j):
            return vec[:, bass.ds(b * NV_ + j, 1)]
        block = ctx.enter_context(nc.Block())

        def results_out(sp, n):
            sp.wait_ge(s["bonus_kept"], n)
            sp.dma_start(k.bonus_d[bass.ds(n - 1, 1)].rearrange("a p t -> p (a t)"), bon[:, :]).then_inc(s["bonus_out"], 16)
            sp.wait_ge(s["y_kept"], n)
            sp.dma_start(k.y_d[bass.ds(n - 1, 1)].rearrange("a p t -> p (a t)"), y_sb[:, :]).then_inc(s["y_out"], 16)

        def blocks(eng):
            yield 0
            with eng.Fori(1, PAIRS_H - 1) as b:
                yield b
            yield PAIRS_H - 1

        def following(b, d):
            if d == 0:
                return b, 1
            return None if isinstance(b, int) and b == PAIRS_H - 1 else (b + 1, 0)

        @block.sync
        def _(sp):
            sp.dma_start(wd_t[:, :], k.rw_d[12]).then_inc(s["rw_static"], 16)
            sp.dma_start(ad[:, :], k.rw_d[13]).then_inc(s["rw_static"], 16)
            with nc.allow_non_contiguous_dma(reason="vectors over partitions"):
                for j, src in ((V_HKA, k.w["rw_k_a"][0]), (V_RK, k.w["rw_r_k"][0].rearrange("h n -> (h n)")),
                               (V_W0, k.w["rw_w0"][0, 0]), (V_W0 + 1, k.w["rw_w0"][0, 1]),
                               (V_A0, k.w["rw_a0"][0, 0]), (V_A0 + 1, k.w["rw_a0"][0, 1])):
                    sp.dma_start(vec3[:, :, j], src.rearrange("(b p) -> p b", p=P)).then_inc(s["rw_static"], 16)
            for b in rounds(sp, PAIRS_H):
                wait(sp, s["lora_done"], 4 * b)
                for src, dst in ((k.w["rw_w_up"], w_up), (k.w["rw_a_up"], a_up)):
                    sp.dma_start(dst[:, :], src[0].rearrange("d r (b c) -> b (d r) c", c=P)[bass.ds(b, 1)]
                                 .rearrange("a r c -> r (a c)")).then_inc(s["up_in"], 16)
                wait(sp, s["dve_prep"], 2 * b)
                wait(sp, s["pool_prep"], 2 * b)
                for src, dst in ((k.rw_d[bass.ds(b, 1), :, 0:SEQ], rT), (k.rw_d[bass.ds(b + 4, 1)], kT),
                                 (k.kk_d[bass.ds(b, 1)], kk)):
                    sp.dma_start(dst[:, :], src.rearrange("a p t -> p (a t)")).then_inc(s["key_in"], 16)
                wait(sp, s["bonus_kept"], b)
                sp.dma_start(vT[:, :], k.rw_d[bass.ds(b + 8, 1)].rearrange("a p t -> p (a t)")).then_inc(s["v_in"], 16)
                if isinstance(b, int) and b == 0:
                    continue
                results_out(sp, b)
            results_out(sp, PAIRS_H)
            sp.wait_ge(s["y_out"], 16 * PAIRS_H)
            sp.wait_ge(s["bonus_out"], 16 * PAIRS_H)

        NX = NG * len(LEVELS)

        @block.tensor
        def _(pe):
            def lora(b, d, j):
                q = E_ if d == 0 else O_
                up, src = ((w_up, wd_t), (a_up, ad))[j]
                if j == 0:
                    pe.wait_ge(s["up_in"], 32 * b + 32)
                else:
                    pe.wait_ge(s["th_done"], 2 * (2 * b + d) + 1)
                pe.matmul(ps[:, 6, 0:SEQ], up[q, :], src[q, 0:SEQ], start=True, stop=True)
                pe.matmul(ps[:, 7, 0:CTX], up[q, :], src[q, SEQ:T], start=True, stop=True).then_inc(s["lora_done"], 1)

            def turn_v(b):
                pe.wait_ge(s["th_done"], 4 * b + 2)
                pe.wait_ge(s["v_in"], 16 * b + 16)
                pe.nop(nofuse=True)
                for g in range(NG):
                    if g == 2:
                        pe.wait_ge(s["v_kept"], NG * b + 1)
                        pe.nop(nofuse=True)
                    for c in range(4):
                        t0 = (4 * g + c) * C
                        mm = pe.transpose(ps[0:64, 6 + g % 2, c * P:(c + 1) * P], vT[:, t0:t0 + C], k.ident[:, :])
                    mm.then_inc(s["v_turned"], 1)

            def scores(b, d):
                u = 2 * b + d
                pe.wait_ge(s["dve_prep"], u + 1)
                pe.wait_ge(s["pool_prep"], u + 1)
                wait(pe, s["gr_kept"], NG * u)
                wait(pe, s["hh_kept"], NG * u)
                if d == 0:
                    wait(pe, s["y_kept"], b)
                    pe.wait_ge(s["v_kept"], NG * b + NG)
                for g in range(NG):
                    n = 64 if g == CTX_GROUP else 128
                    pe_b = 4 * (g % 2)
                    if g == 2:
                        pe.wait_ge(s["s1_kept"], NG * u + 1)
                        pe.wait_ge(s["tr_kept"], NG * u + 1)
                    for c in range(4):
                        cc = 4 * g + c
                        for hh, (q, lo) in enumerate(((E_, 0), (O_, 1))):
                            mm = pe.matmul(ps[:, pe_b + hh, c * n:(c + 1) * n], BKB[q, cc, lo:lo + 2, :],
                                           AR[d][q, cc, 0:n // 64, :], start=True, stop=True)
                    mm.then_inc(s["s1_ready"], 1)
                    for hh, (q, lo) in enumerate(((E_, 0), (O_, 1))):
                        for c in range(4):
                            pe.transpose(ps[:, pe_b + 2 + hh, c * C:(c + 1) * C], BKB[q, 4 * g + c, lo:lo + 2, :],
                                         k.ident[q, q])
                    for c in range(4):
                        at = 256 + (c % 2) * P
                        mm = pe.transpose(ps[0:64, pe_b + 2 + c // 2, at:at + P], AR[d][:, 4 * g + c, 0, :], k.ident[:, :])
                    mm.then_inc(s["tr_ready"], 1)
                pe.wait_ge(s["s1_kept"], NG * u + NG)
                pe.wait_ge(s["tr_kept"], NG * u + NG)
                for g in range(NG):
                    for c in range(4):
                        cc = 4 * g + c
                        for hh, q in enumerate((E_, O_)):
                            at = c * C
                            mm = pe.matmul(ps[q, MV_BANK[g], at:at + C], GA[:, cc, hh, :], vz[:, cc, hh, :],
                                           start=True, stop=True)
                    mm.then_inc(s["mv_ready"], 1)
                for g in range(NG):
                    pe.wait_ge(s["u0_done"], NG * u + g + 1)
                    for c in range(4):
                        mm = pe.transpose(ps[:, g, c * P:(c + 1) * P], Um[:, 4 * g + c, :], k.ident[:, :])
                    mm.then_inc(s["t0_ready"], 1)

            def level(b, d, l):
                u = 2 * b + d
                for g in range(NG):
                    n = NG * l + g
                    if l == 0:
                        pe.wait_ge(s["t0_kept"], NG * u + (NG if g == 0 else g + 1))
                    else:
                        pe.wait_ge(s["tu_kept"], NX * u + n - NG + 1)
                    if n >= 2:
                        pe.wait_ge(s["x_kept"], NX * u + n - 1)
                    for c in range(4):
                        mm = pe.matmul(ps[:, n % 2, c * P:(c + 1) * P], LT[:, 4 * g + c, :], Tm[:, 4 * g + c, :],
                                       start=True, stop=True)
                    mm.then_inc(s["x_ready"], 1)
                for g in range(NG):
                    n = NG * l + g
                    pe.wait_ge(s["x_kept"], NX * u + n + 1)
                    if n >= 2:
                        pe.wait_ge(s["tu_kept"], NX * u + n - 1)
                    bt = 2 + 2 * (n % 2)
                    for c in range(4):
                        cc = 4 * g + c
                        if l < len(LEVELS) - 1:
                            pe.matmul(ps[:, bt, c * P:(c + 1) * P], Um[:, cc, :], X[:, cc, :], start=True, stop=True)
                        mm = pe.matmul(ps[:, bt + 1, c * P:(c + 1) * P], X[:, cc, :], Um[:, cc, :],
                                       start=True, stop=True)
                    mm.then_inc(s["tu_ready"], 1)

            def solve(b, d):
                u = 2 * b + d
                for g in range(NG):
                    pe.wait_ge(s["tu_kept"], NX * u + NX - NG + g + 1)
                    for c in range(4):
                        cc = 4 * g + c
                        mm = pe.matmul(ps[:, TM_BANK[g], c * P:(c + 1) * P], Um[:, cc, :],
                                       mva[:, cc, :, :], start=True, stop=True)
                    mm.then_inc(s["tm_ready"], 1)
                pe.wait_ge(s["pool_half"], POOL_HALVES * b + 6 * d + 6)
                for g in range(NG):
                    n = 1 if g == CTX_GROUP else 2
                    pe.wait_ge(s["ta_kept"], NG * u + g + 1)
                    for c in range(4):
                        cc = 4 * g + c
                        mm = pe.matmul(ps[:, 1 + g, c * P:c * P + 64 * n], TA[:, cc, :], BP[:, cc, 0:n, :],
                                       start=True, stop=True)
                    mm.then_inc(s["gr_ready"], 1)
                    pe.wait_ge(s["sa_kept"], NG * u + g + 1)
                    for c in range(4):
                        cc = 4 * g + c
                        at = c * C
                        for hh, q in enumerate((E_, O_)):
                            mm = pe.matmul(ps[q, 4 + g, at:at + C], BKn[:, cc, hh, :], sv[d][:, cc, hh, :],
                                           start=True, stop=True)
                    mm.then_inc(s["hh_ready"], 1)

            def chains(b):
                pe.wait_ge(s["gr_kept"], NG * (2 * b + 2))
                pe.wait_ge(s["hh_kept"], NG * (2 * b + 2))
                for i in range(1, steps + 1):
                    for d in range(2):
                        if i > 1:
                            pe.wait_ge(s["step_done"], 2 * steps * b + 2 * (i - 2) + d + 1)
                        before = Hg[d][:, order[d][0], :] if i == 1 else S[d][:, i - 1, :]
                        pe.matmul(ps[:, 4 + d, 0:C], GT[d][:, order[d][i], :], before,
                                  start=True, stop=True).then_inc(s["step_ready"], 1)
                    if i <= NCL:
                        c = i - 1
                        for d in range(2):
                            for hh, q in enumerate((E_, O_)):
                                mm = pe.matmul(ps[q, 7, c * C:(c + 1) * C], GR[d][:, c, hh, :], sv[d][:, c, hh, :],
                                               start=(d == 0), stop=(d == 1))
                        if i == NCL:
                            mm.then_inc(s["share_ready"], 1)
                pe.wait_ge(s["step_done"], 2 * steps * b + 2 * steps)
                for c in range(NCL):
                    for d in range(2):
                        mm = pe.matmul(ps[:, 6, c * C:(c + 1) * C], RT[d][:, c, :], S[d][:, order[d].index(c) - 1, :],
                                       start=(d == 0), stop=(d == 1))
                mm.then_inc(s["y_ready"], 1)
            pe.wait_ge(s["rw_vec_done"], 4)
            pe.wait_ge(s["zeroed"], 7)
            lora(0, 0, 0)
            lora(0, 0, 1)
            turn_v(0)
            for b in blocks(pe):
                for d in range(2):
                    scores(b, d)
                    pe.wait_ge(s["mv_kept"], NG * (2 * b + d) + NG)
                    if d == 1:
                        pe.wait_ge(s["bonus_in"], b + 1)
                        pe.matmul(ps[:, 7, :], rk_head[:, :], kd_sum[:, :], start=True, stop=True)\
                          .then_inc(s["bonus_ready"], 1)
                    nxt = following(b, d)
                    level(b, d, 0)
                    if nxt:
                        if d == 1:
                            pe.wait_ge(s["bonus_kept"], b + 1)
                        lora(*nxt, 0)
                    level(b, d, 1)
                    if nxt:
                        lora(*nxt, 1)
                    level(b, d, 2)
                    if nxt and d == 1:
                        turn_v(nxt[0])
                    level(b, d, 3)
                    level(b, d, 4)
                    if nxt:
                        pe.wait_ge(s["th_done"], 2 * (2 * b + d + 1) + 2)
                        if d == 1:
                            pe.wait_ge(s["v_kept"], NG * (b + 1) + NG)
                    else:
                        pe.wait_ge(s["bonus_kept"], b + 1)
                    solve(b, d)
                chains(b)

        @block.scalar
        def _(act):
            def squash(b, d, j):
                u = 2 * b + d
                th, v0 = ((th_w, V_W0), (th_a, V_A0))[j]
                act.wait_ge(s["lora_done"], 2 * u + j + 1)
                act.activation(th[:, 0:SEQ], ps[:, 6, 0:SEQ], ACT.Tanh, scale=0.5, bias=col(b, v0 + d))
                act.activation(th[:, SEQ:T], ps[:, 7, 0:CTX], ACT.Tanh, scale=0.5, bias=col(b, v0 + d))\
                   .then_inc(s["th_done"], 1)
                act.wait_ge(s["th_done"], 2 * u + j + 1)
                if j == 0:
                    act.activation(th[:, :], th[:, :], ACT.Identity, scale=0.5, bias=col(0, V_HALF)).then_inc(s["w_done"], 1)
                else:
                    act.activation(nb[:, :], th[:, :], ACT.Identity, scale=-0.5, bias=col(0, V_MHALF))
                    act.activation(kf[:, :], th[:, :], ACT.Identity, scale=col(b, V_HKA), bias=col(b, V_1HKA))\
                       .then_inc(s["kf_made"], 1)

            def decays(b, d):
                u = 2 * b + d
                act.wait_ge(s["cum_done"], 2 * u + 1)
                act.activation(e_neg[:, :], cum[:, :], ACT.Exp, scale=KAPPA).then_inc(s["exps"], 1)
                act.activation(e_inc[:, :], cum[:, :], ACT.Exp, scale=-KAPPA).then_inc(s["exps"], 1)
                act.wait_ge(s["cum_done"], 2 * u + 2)
                act.activation(e_exc[:, :], cumx[:, :], ACT.Exp, scale=-KAPPA).then_inc(s["exps"], 1)

            def keep_v(b):
                wait(act, s["pool_half"], POOL_HALVES * b)
                for g in range(NG):
                    act.wait_ge(s["v_turned"], NG * b + g + 1)
                    pv = ps[0:64, 6 + g % 2, :].rearrange("p (c x) -> p c x", c=4)
                    act.activation(vz[O_, grp(g), 0, :], pv[:, :, 0:64], ACT.Copy)
                    act.activation(vz[E_, grp(g), 1, :], pv[:, :, 64:128], ACT.Copy).then_inc(s["v_kept"], 1)
            act.wait_ge(s["rw_static"], 16 * 8)
            act.activation(wd_t[:, :], wd_t[:, :], ACT.Tanh).then_inc(s["rw_vec_done"], 1)
            act.wait_ge(s["rw_vec_done"], 4)
            squash(0, 0, 0)
            squash(0, 0, 1)
            keep_v(0)
            decays(0, 0)
            for b in blocks(act):
                for d in range(2):
                    u = 2 * b + d
                    for g in range(NG):
                        act.wait_ge(s["tr_ready"], NG * u + g + 1)
                        pb = 4 * (g % 2)
                        for j in range(2):
                            act.activation(BKn[:, grp(g), j, :], ps[:, pb + 2 + j, 0:256].rearrange("p (c x) -> p c x", c=4),
                                           ACT.Copy)
                            pa = ps[0:64, pb + 2 + j, 256:512].rearrange("p (c h x) -> p c h x", c=2, h=2)
                            cs = slice(4 * g + 2 * j, 4 * g + 2 * j + 2)
                            act.activation(mva[E_, cs, 1, :], pa[:, :, 0, :], ACT.Copy)
                            ins = act.activation(mva[O_, cs, 1, :], pa[:, :, 1, :], ACT.Copy)
                        ins.then_inc(s["tr_kept"], 1)
                    for g in range(NG):
                        act.wait_ge(s["mv_ready"], NG * u + g + 1)
                        act.activation(mva[:, grp(g), 0, :], bank(MV_BANK[g], C), ACT.Copy).then_inc(s["mv_kept"], 1)
                    for g in range(NG):
                        act.wait_ge(s["t0_ready"], NG * u + g + 1)
                        act.activation(Tm[:, grp(g), :], bank(g), ACT.Copy).then_inc(s["t0_kept"], 1)
                    nxt = following(b, d)
                    if nxt:
                        squash(*nxt, 0)
                        squash(*nxt, 1)
                        if d == 1:
                            keep_v(nxt[0])
                        decays(*nxt)
                    act.wait_ge(s["pool_half"], POOL_HALVES * b + 6 * d + 2)
                    for g in range(NG):
                        act.wait_ge(s["ta_kept"], NG * u + g + 1)
                        tm = bank(TM_BANK[g])
                        act.activation(sv[d][E_, grp(g), 0, :], tm[E_, :, 0:64], ACT.Copy)
                        act.activation(sv[d][O_, grp(g), 1, :], tm[O_, :, 0:64], ACT.Copy).then_inc(s["sa_kept"], 1)
                act.wait_ge(s["share_ready"], b + 1)
                wait(act, s["y_out"], 16 * b)
                act.activation(y_sb[:, :], ps[:, 7, :], ACT.Copy).then_inc(s["share_kept"], 1)

        @block.gpsimd
        def _(pool):
            def factors(b, d):
                u = 2 * b + d
                if d == 0:
                    pool.wait_ge(s["key_in"], 48 * b + 48)
                pool.wait_ge(s["exps"], 3 * u + 2)
                pool.tensor_tensor(AR[d][:, 0:NCL, 1, :], rT[:, :].rearrange("p (c x) -> p c x", x=C),
                                   e_inc[:, 0:SEQ].rearrange("p (c x) -> p c x", x=C), ALU.mult)
                pool.wait_ge(s["exps"], 3 * u + 3)
                pool.tensor_tensor(AR[d][:, :, 0, :], kk[:, :].rearrange("p (c x) -> p c x", x=C),
                                   e_exc[:, :].rearrange("p (c x) -> p c x", x=C), ALU.mult).then_inc(s["pool_prep"], 1)
            for m in (LT, TA, GT[0], GT[1], RT[0], RT[1]):
                pool.memset(m[:, :, :], 0.0).then_inc(s["zeroed"], 1)
            pool.memset(vz[:, :, :, :], 0.0).then_inc(s["zeroed"], 1)
            factors(0, 0)
            for b in blocks(pool):
                count = [0]

                def alone(ins):
                    count[0] += 1
                    ins.then_inc(s["pool_half"], 1)
                    pool.wait_ge(s["pool_half"], POOL_HALVES * b + count[0])
                for d in range(2):
                    u = 2 * b + d
                    pool.wait_ge(s["pool_prep"], u + 1)
                    if d == 0:
                        pool.wait_ge(s["v_kept"], NG * b + NG)
                        wait(pool, s["y_ready"], b)
                    pool.nop(nofuse=True)
                    alone(pool.tensor_copy(sv[d][O_, :, 0, :], vz[O_, :, 0, :]))
                    pool.nop(nofuse=True)
                    alone(pool.tensor_copy(sv[d][E_, :, 1, :], vz[E_, :, 1, :]))
                    pool.wait_ge(s["s1_kept"], NG * u + NG)
                    pool.wait_ge(s["tr_kept"], NG * u + NG)
                    for dst, src in ((BP[E_, 0:NCL, 1, :], GR[d][E_, :, 0, :]), (BP[O_, 0:NCL, 1, :], GR[d][O_, :, 1, :]),
                                     (BP[E_, :, 0, :], BKn[E_, :, 0, :]), (BP[O_, :, 0, :], BKn[O_, :, 1, :])):
                        pool.nop(nofuse=True)
                        alone(pool.tensor_copy(dst, src))
                    nxt = following(b, d)
                    if nxt:
                        factors(*nxt)
                assert count[0] == POOL_HALVES

        @block.vector
        def _(dve):
            link = Chain(dve, s["rw_dve"])
            dve.wait_ge(s["rw_static"], 16 * 8)
            for j in (V_HKA, V_W0, V_W0 + 1, V_A0, V_A0 + 1):
                link(dve.tensor_scalar(vec3[:, :, j], vec3[:, :, j], 0.5, None, ALU.mult))
            dve.memset(vec3[:, :, V_HALF], 0.5).then_inc(s["rw_vec_done"], 1)
            dve.memset(vec3[:, :, V_MHALF], -0.5).then_inc(s["rw_vec_done"], 1)
            dve.tensor_scalar(vec3[:, :, V_1HKA], vec3[:, :, V_HKA], -1.0, 1.0, ALU.mult, ALU.add).then_inc(s["rw_vec_done"], 1)
            dve.wait_ge(s["rw_vec_done"], 4)

            def then(b, d, place, ins):
                ins.then_inc(s["own_result"], 1)
                dve.wait_ge(s["own_result"], PER * (2 * b + d) + place)

            def cumulate(b, d, step):
                u = 2 * b + d
                if step == 0:
                    dve.wait_ge(s["w_done"], u + 1)
                    st = slice(None, None, -1) if d else slice(None)
                    rs = k.reset[:, :, :].rearrange("p c x -> p (c x)")
                    dve.tensor_tensor_scan(cum[:, st], rs, th_w[:, st], 0.0, ALU.mult, ALU.add).then_inc(s["cum_done"], 1)
                else:
                    dve.wait_ge(s["cum_done"], 2 * u + 1)
                    dve.tensor_tensor(cumx[:, :], cum[:, :], th_w[:, :], ALU.subtract).then_inc(s["cum_done"], 1)

            def keys(b, d, step):
                u = 2 * b + d
                if step == 0:
                    dve.wait_ge(s["kf_made"], u + 1)
                    if d == 0:
                        dve.wait_ge(s["key_in"], 48 * b + 48)
                    dve.tensor_tensor(kf[:, :], kf[:, :], kT[:, :], ALU.mult).then_inc(s["keys_step"], 1)
                elif step == 1:
                    dve.tensor_tensor(nb[:, :], nb[:, :], kk[:, :], ALU.mult).then_inc(s["keys_step"], 1)
                else:
                    dve.wait_ge(s["keys_step"], 3 * u + 2)
                    if d == 0:
                        wait(dve, s["bonus_ready"], b)
                        dve.tensor_scalar(rk_head[:, :], k.same_head[:, :], col(b, V_RK), None, ALU.mult)
                        dve.tensor_copy(kd_sum[:, :], kf[:, 0:SEQ]).then_inc(s["keys_step"], 1)
                    else:
                        dve.tensor_tensor(kd_sum[:, :], kd_sum[:, :], kf[:, 0:SEQ], ALU.add).then_inc(s["keys_step"], 1)
                        dve.wait_ge(s["keys_step"], 3 * u + 3)
                        dve.tensor_tensor(kd_sum[:, :], kd_sum[:, :], rT[:, :], ALU.mult).then_inc(s["bonus_in"], 1)

            def factors(b, d, step):
                u = 2 * b + d
                dve.wait_ge(s["exps"], 3 * u + 2)
                x = (nb, nb, kf)[step][:, :].rearrange("p (c x) -> p c x", x=C)
                dve.tensor_tensor(BKB[:, :, (0, 2, 1)[step], :], x, e_neg[:, :].rearrange("p (c x) -> p c x", x=C), ALU.mult)
                if step == 2:
                    end = 0 if d else C - 1
                    dve.tensor_copy(gam_next[:, :], e_inc[:, :].rearrange("p (c x) -> p c x", x=C)[:, :, end])\
                       .then_inc(s["dve_prep"], 1)
            for step in range(2):
                cumulate(0, 0, step)
            for step in range(3):
                keys(0, 0, step)
            for step in range(3):
                factors(0, 0, step)
            for b in blocks(dve):
                for d in range(2):
                    u = 2 * b + d
                    dve.wait_ge(s["dve_prep"], u + 1)
                    if d == 0:
                        wait(dve, s["step_done"], 2 * steps * b)
                    dve.tensor_copy(gam[d][:, :], gam_next[:, :])
                    for g in range(NG):
                        dve.wait_ge(s["s1_ready"], NG * u + g + 1)
                        pb = 4 * (g % 2)
                        n = 64 if g == CTX_GROUP else 128
                        for hh in range(2):
                            v = bank(pb + hh, n)
                            ins = dve.tensor_tensor(GA[:, grp(g), hh, :], v[:, :, 0:64],
                                                    k.cut[:, d, 0, :].unsqueeze(1).to_broadcast([P, 4, 64]), ALU.mult)
                            if n == 128:
                                ins = dve.tensor_tensor(GR[d][:, grp(g), hh, :], v[:, :, 64:128],
                                                        k.cut[:, d, 1, :].unsqueeze(1).to_broadcast([P, 4, 64]), ALU.mult)
                        ins.then_inc(s["s1_kept"], 1)
                        dve.wait_ge(s["s1_kept"], NG * u + g + 1)
                        dve.tensor_copy(LT[E_, grp(g), 0:64], GA[E_, grp(g), 0, :])
                        then(b, d, 2 * g + 1, dve.tensor_copy(LT[O_, grp(g), 64:128], GA[O_, grp(g), 1, :]))
                        then(b, d, 2 * g + 2, dve.tensor_tensor(Um[:, grp(g), :], LT[:, grp(g), :],
                                                                k.join[:, 1 - d, 0, :].unsqueeze(1).to_broadcast([P, 4, P]), ALU.mult))
                        dve.tensor_tensor(Um[:, grp(g), :], Um[:, grp(g), :],
                                          k.ident[:, :].unsqueeze(1).to_broadcast([P, 4, P]), ALU.add).then_inc(s["u0_done"], 1)
                    if d == 1:
                        dve.wait_ge(s["bonus_ready"], b + 1)
                        wait(dve, s["bonus_out"], 16 * b)
                        dve.tensor_tensor(bon[:, :], ps[:, 7, :], vT[:, 0:SEQ], ALU.mult).then_inc(s["bonus_kept"], 1)
                    nxt = following(b, d)
                    for l in range(len(LEVELS)):
                        for g in range(NG):
                            n = NG * l + g
                            dve.wait_ge(s["x_ready"], NX * u + n + 1)
                            dve.tensor_tensor(X[:, grp(g), :], bank(n % 2),
                                              k.join[:, d, l + 1, :].unsqueeze(1).to_broadcast([P, 4, P]), ALU.mult)\
                               .then_inc(s["x_kept"], 1)
                        for g in range(NG):
                            n = NG * l + g
                            bt = 2 + 2 * (n % 2)
                            dve.wait_ge(s["tu_ready"], NX * u + n + 1)
                            if l < len(LEVELS) - 1:
                                dve.tensor_tensor(Tm[:, grp(g), :], Tm[:, grp(g), :], bank(bt), ALU.add)
                            dve.tensor_tensor(Um[:, grp(g), :], Um[:, grp(g), :], bank(bt + 1), ALU.add)\
                               .then_inc(s["tu_kept"], 1)
                            if nxt and l == 1 and g < 2:
                                cumulate(*nxt, g)
                            if nxt and l == 2:
                                keys(*nxt, g)
                            if nxt and l == 3:
                                factors(*nxt, g)
                    for g in range(NG):
                        dve.wait_ge(s["tm_ready"], NG * u + g + 1)
                        tm = bank(TM_BANK[g])
                        dve.tensor_copy(TA[E_, grp(g), 0:64], tm[E_, :, 64:128])
                        dve.tensor_copy(TA[O_, grp(g), 64:128], tm[O_, :, 64:128]).then_inc(s["ta_kept"], 1)
                    for g in range(NG):
                        dve.wait_ge(s["gr_ready"], NG * u + g + 1)
                        v = bank(1 + g)
                        for q in (E_, O_):
                            ins = dve.tensor_tensor(GT[d][q, grp(g), q], v[q, :, 0:64],
                                                    k.ident[q, q].unsqueeze(1).to_broadcast([64, 4, 64]), ALU.add)
                            if g != CTX_GROUP:
                                ins = dve.tensor_tensor(RT[d][q, grp(g), q], v[q, :, 64:128], AR[d][q, grp(g), 1, :], ALU.add)
                        ins.then_inc(s["gr_kept"], 1)
                        dve.wait_ge(s["hh_ready"], NG * u + g + 1)
                        dve.tensor_tensor(Hg[d][:, grp(g), :], bank(4 + g, C),
                                          bc(gam[d][:, grp(g)], C), ALU.mult).then_inc(s["hh_kept"], 1)
                dve.wait_ge(s["hh_kept"], NG * (2 * b + 2))
                for i in range(1, steps + 1):
                    for d in range(2):
                        c = order[d][i]
                        dve.wait_ge(s["step_ready"], 2 * steps * b + 2 * (i - 1) + d + 1)
                        dve.scalar_tensor_tensor(S[d][:, i, :], ps[:, 4 + d, 0:C], gam[d][:, c:c + 1],
                                                 Hg[d][:, c, :], ALU.mult, ALU.add).then_inc(s["step_done"], 1)
                dve.wait_ge(s["share_kept"], b + 1)
                dve.wait_ge(s["y_ready"], b + 1)
                dve.tensor_tensor(y_sb[:, :], y_sb[:, :], ps[:, 6, :], ALU.add).then_inc(s["y_kept"], 1)


PER = 6
PAIRS_H = 4
POOL_HALVES = 12


def rwkv_readout(nc, k):
    ctx = ExitStack()
    with ctx:
        def sb(name, shape):
            return ctx.enter_context(nc.sbuf_tensor(name, shape, F32))
        y = sb("y_all", [P, 4, NCL, C])
        y2 = sb("y_sq", [P, 4, NCL, C])
        bonus = sb("bonus_all", [P, 4, SEQ])
        gd, g_up = sb("gd", [P, SEQ]), sb("g_up", [P, 512])
        lw, lb = sb("ln_w", [P, 4]), sb("ln_b", [P, 4])
        mean, var = sb("gn_mean", [P, 4 * NCL]), sb("gn_var", [P, 4 * NCL])
        bT = k.bT
        ps = k.ps
        ins_in, dch, cent, sqd, var_done, rooted, norm, turned, kept, gd_t, gd_s, g_ready, b_done = (
            k.sem("ro_" + n) for n in "in dve centred sq var rooted norm turned kept gd_t gd_s g_ready b_done".split())
        block = ctx.enter_context(nc.Block())

        @block.sync
        def _(sp):
            sp.dma_start(y[:, :, :, :].rearrange("p b c x -> p b (c x)"), k.y_d.rearrange("b p t -> p b t")).then_inc(ins_in, 16)
            sp.dma_start(gd[:, :], k.rw_d[14, :, 0:SEQ]).then_inc(ins_in, 16)
            sp.dma_start(g_up[:, :], k.w["rw_g_up"][0]).then_inc(ins_in, 16)
            with nc.allow_non_contiguous_dma(reason="vectors over partitions"):
                sp.dma_start(lw[:, :], k.w["rw_ln_w"][0].rearrange("(b p) -> p b", p=P)).then_inc(ins_in, 16)
                sp.dma_start(lb[:, :], k.w["rw_ln_b"][0].rearrange("(b p) -> p b", p=P)).then_inc(ins_in, 16)
            sp.dma_start(bonus[:, :, :], k.bonus_d.rearrange("b p t -> p b t")).then_inc(ins_in, 16)
            sp.dma_start(k.aT[:, :, :], k.aT_d.rearrange("b p t -> p b t")).then_inc(k.merge_in, 16)
            for j, name in enumerate(("merge_pa", "merge_pb")):
                sp.dma_start(k.merge_w[j][:, :, :], k.w[name][0].rearrange("(b p) n -> p b n", p=P)).then_inc(k.merge_in, 16)
                sp.dma_start(k.gate[j][:, :, :], k.gt_d[8 * j:8 * j + 8].rearrange("b p t -> p b t")).then_inc(k.merge_in, 16)
            sp.dma_start(k.wo[:, :, :], k.w["w_out"][0].rearrange("(b p) n -> p b n", p=P)).then_inc(k.wo_in, 16)

        @block.gpsimd
        def _(pool):
            pool.wait_ge(cent, 1)
            pool.tensor_tensor(y2[:, :, :, :], y[:, :, :, :], y[:, :, :, :], ALU.mult).then_inc(sqd, 1)

        @block.tensor
        def _(pe):
            pe.wait_ge(gd_s, 1)
            for b in range(4):
                mm = pe.matmul(ps[:, 4 + b, :], g_up[:, b * P:(b + 1) * P], gd[:, :], start=True, stop=True)
            mm.then_inc(g_ready, 1)
            pe.wait_ge(norm, 1)
            for b in range(4):
                for half in range(2):
                    n = 2 * b + half
                    if n >= 4:
                        pe.wait_ge(kept, n - 3)
                    for c in range(4):
                        mm = pe.transpose(ps[0:64, n % 4, c * P:(c + 1) * P], y[:, b, 4 * half + c, :], k.ident[:, :])
                    mm.then_inc(turned, 1)

        @block.scalar
        def _(act):
            act.wait_ge(ins_in, 96)
            act.activation(gd[:, :], gd[:, :], ACT.Tanh, scale=0.5).then_inc(gd_t, 1)
            act.wait_ge(var_done, 1)
            act.activation(var[:, :], var[:, :], ACT.Sqrt).then_inc(rooted, 1)
            for n in range(8):
                b, half = n // 2, n % 2
                act.wait_ge(turned, n + 1)
                for hh in range(2):
                    q = slice(64 * hh, 64 * hh + 64)
                    ins = act.activation(bT[q, b, 256 * half:256 * half + 256].rearrange("p (c x) -> p c x", c=4),
                                         ps[0:64, n % 4, :].rearrange("p (c h x) -> p c h x", c=4, h=2)[:, :, hh, :], ACT.Copy)
                ins.then_inc(kept, 1)

        @block.vector
        def _(dve):
            link = Chain(dve, dch)
            dve.wait_ge(gd_t, 1)
            dve.tensor_scalar(gd[:, :], gd[:, :], 0.5, 0.5, ALU.mult, ALU.add).then_inc(gd_s, 1)
            y3, y23 = (a[:, :, :, :].rearrange("p b c x -> p (b c) x") for a in (y, y2))
            link(dve.tensor_reduce(mean[:, :], y3, AX.X, ALU.add))
            link(dve.tensor_scalar(mean[:, :], mean[:, :], 1.0 / RN, None, ALU.mult))
            dve.tensor_tensor(y3, y3, bc(mean[:, :], C), ALU.subtract).then_inc(cent, 1)
            dve.wait_ge(sqd, 1)
            link(dve.tensor_reduce(var[:, :], y23, AX.X, ALU.add))
            dve.tensor_scalar(var[:, :], var[:, :], 1.0 / RN, GN_EPS, ALU.mult, ALU.add).then_inc(var_done, 1)
            dve.wait_ge(rooted, 1)
            link(dve.reciprocal(mean[:, :], var[:, :]))
            dve.tensor_tensor(y3, y3, bc(mean[:, :], C), ALU.mult).then_inc(norm, 1)
            dve.wait_ge(g_ready, 1)
            for b in range(4):
                dve.wait_ge(kept, 2 * b + 2)
                link(dve.tensor_scalar(bT[:, b, :], bT[:, b, :], lw[:, b:b + 1], lb[:, b:b + 1], ALU.mult, ALU.add))
                link(dve.tensor_tensor(bT[:, b, :], bT[:, b, :], bonus[:, b, :], ALU.add))
                dve.tensor_tensor(bT[:, b, :], bT[:, b, :], ps[:, 4 + b, :], ALU.mult).then_inc(b_done, 1)
            dve.wait_ge(b_done, 4)


def merge(nc, k):
    ctx = ExitStack()
    with ctx:
        def sb(name, shape):
            return ctx.enter_context(nc.sbuf_tensor(name, shape, F32))
        (pa, pb), wo, gate, aT, bT = k.merge_w, k.wo, k.gate, k.aT, k.bT
        xT = sb("xT_in", [P, DB, SEQ])
        g2n = sb("norm2_in", [P, DB])
        scale2, half_g1 = sb("scale2", [P, DB]), sb("half_g1", [P, DB])
        rms, rstd = sb("rms2", [P, SEQ]), sb("rstd2", [P, SEQ])
        ps = k.ps
        mg = gate[0]
        sq = gate[1]
        names = "x_in norm_in h2_scaled ab_ready ab_used halves merged out_ready x1_done sq_done ss_done ms_done rms_done dve hn".split()
        s = {n: k.sem("m_" + n) for n in names}
        block = ctx.enter_context(nc.Block())

        @block.sync
        def _(sp):
            sp.dma_start(xT[:, :, :], k.xT_d.rearrange("(b p) t -> p b t", p=P)).then_inc(s["x_in"], 16)
            with nc.allow_non_contiguous_dma(reason="a vector over partitions"):
                sp.dma_start(g2n[:, :], k.w["norm2_g"][0].rearrange("(b p) -> p b", p=P)).then_inc(s["norm_in"], 16)

        @block.tensor
        def _(pe):
            pe.wait_ge(k.merge_in, 16 * 5)
            for m in range(DB):
                if m >= 2:
                    pe.wait_ge(s["ab_used"], m - 1)
                for j, (w, src) in enumerate(((pa, aT), (pb, bT))):
                    for b in range(4):
                        mm = pe.matmul(ps[:, 2 * (m % 2) + j, :], w[:, b, m * P:(m + 1) * P], src[:, b, :],
                                       start=(b == 0), stop=(b == 3))
                mm.then_inc(s["ab_ready"], 1)
            pe.wait_ge(k.wo_in, 16)
            pe.wait_ge(s["merged"], DB)
            for m in range(DB):
                if m >= 2:
                    pe.wait_ge(s["x1_done"], m - 1)
                for b in range(DB):
                    mm = pe.matmul(ps[:, 4 + m % 2, :], wo[:, b, m * P:(m + 1) * P], mg[:, b, :],
                                   start=(b == 0), stop=(b == DB - 1))
                mm.then_inc(s["out_ready"], 1)
            for b in range(DB):
                pe.wait_ge(s["sq_done"], b + 1)
                mm = pe.matmul(ps[:, 6, :], k.ones[:, :], sq[:, b, :], start=(b == 0), stop=(b == DB - 1))
            mm.then_inc(s["ss_done"], 1)

        @block.gpsimd
        def _(pool):
            for m in range(DB):
                pool.wait_ge(s["halves"], m + 1)
                pool.tensor_tensor(mg[:, m, :], gate[0][:, m, :], gate[1][:, m, :], ALU.add).then_inc(s["merged"], 1)

        @block.scalar
        def _(act):
            for m in range(DB):
                act.wait_ge(s["x1_done"], m + 1)
                act.activation(sq[:, m, :], k.x1T[:, m, :], ACT.Square).then_inc(s["sq_done"], 1)
            act.wait_ge(s["ms_done"], 1)
            act.activation(rms[:, :], rms[:, :], ACT.Sqrt).then_inc(s["rms_done"], 1)
            for m in range(DB):
                act.wait_ge(s["h2_scaled"], m + 1)
                act.activation(k.h2T[:, m, :], k.h2T[:, m, :], ACT.Identity,
                               bias=k.mod[:, 0, 3 * DB + m:3 * DB + m + 1]).then_inc(s["hn"], 1)
            act.wait_ge(s["hn"], DB)

        @block.vector
        def _(dve):
            link = Chain(dve, s["dve"])
            dve.wait_ge(s["norm_in"], 16)
            dve.wait_ge(s["x_in"], 16)
            dve.wait_ge(k.merge_in, 16 * 5)
            link(dve.tensor_scalar(scale2[:, :], k.mod[:, 0, 4 * DB:5 * DB], 1.0, None, ALU.add))
            link(dve.tensor_tensor(scale2[:, :], scale2[:, :], g2n[:, :], ALU.mult))
            link(dve.tensor_scalar(half_g1[:, :], k.mod[:, 0, 2 * DB:3 * DB], 0.5, None, ALU.mult))
            for m in range(DB):
                dve.wait_ge(s["ab_ready"], m + 1)
                for j in range(2):
                    ins = dve.scalar_tensor_tensor(gate[j][:, m, :], gate[j][:, m, :], 1.0, ps[:, 2 * (m % 2) + j, :],
                                                   ALU.add, ALU.mult)
                    if j:
                        ins.then_inc(s["halves"], 1)
                dve.wait_ge(s["halves"], m + 1)
                dve.tensor_copy(rstd[:, 0:1], scale2[:, 0:1]).then_inc(s["ab_used"], 1)
            for m in range(DB):
                dve.wait_ge(s["out_ready"], m + 1)
                dve.scalar_tensor_tensor(k.x1T[:, m, :], ps[:, 4 + m % 2, :], half_g1[:, m:m + 1],
                                         xT[:, m, :], ALU.mult, ALU.add).then_inc(s["x1_done"], 1)
            dve.wait_ge(s["ss_done"], 1)
            dve.tensor_scalar(rms[:, :], ps[:, 6, :], 1.0 / D, EPS, ALU.mult, ALU.add).then_inc(s["ms_done"], 1)
            dve.wait_ge(s["rms_done"], 1)
            link(dve.reciprocal(rstd[:, :], rms[:, :]))
            for m in range(DB):
                dve.scalar_tensor_tensor(k.h2T[:, m, :], k.x1T[:, m, :], scale2[:, m:m + 1], rstd[:, :],
                                         ALU.mult, ALU.mult).then_inc(s["h2_scaled"], 1)


NG_E, EPG = 4, 4
BLOCKS = SEQ * 2 // P + NE
PAIRS = BLOCKS // 2
SLOTS = BLOCKS * P
FEWEST = SEQ * 2 // P


def route(nc, k):
    ctx = ExitStack()
    with ctx:
        def sb(name, shape, dt=F32):
            return ctx.enter_context(nc.sbuf_tensor(name, shape, dt))
        h2N = sb("h2_rows", [P, TL, D])
        rw = sb("router_w_sb", [P, DB, NE])
        rb = sb("router_b_sb", [P, NE])
        sc, sel, selm = sb("scores", [P, TL, NE]), sb("sel", [P, TL, NE]), sb("sel_masked", [P, TL, NE])
        hi, lo = sb("pair_hi", [P, TL, NG_E, 2]), sb("pair_lo", [P, TL, NG_E, 2])
        gs, t1, t2 = sb("group_score", [P, TL, NG_E]), sb("t1", [P, TL, NG_E]), sb("t2", [P, TL, NG_E])
        top = sb("top", [P, TL])
        oh = [sb(f"one_hot{j}", [P, TL, NE]) for j in range(2)]
        both, work = sb("chosen", [P, TL, NE]), sb("work", [P, TL, NE])
        prio, gprio = sb("priority", [P, NE]), sb("group_priority", [P, NG_E])
        strict = sb("strict", [P, P])
        rank = sb("rank", [P, TL + 1, NE])
        nb, end, ones16 = sb("n_blocks", [P, NE]), sb("end_block", [P, NE]), sb("ones16", [P, NE])
        acc = sb("acc", [P, NE])
        slot_f = sb("slot_f", [P, 2, TL])
        blk = sb("block_no", [P, BLOCKS])
        cmp_ = sb("block_cmp", [P, BLOCKS, NE])
        plan_f = sb("plan_f", [P, BLOCKS + 1])
        zero_i = sb("zero_i", [P, BLOCKS], I32)
        tok = sb("token_no", [P, TL], I32)
        ws = sb("w_sum", [P, TL])
        ps = k.ps
        names = ("small consts turned kept h2_out logits e_done dve chosen rank_done slots zero_out tab_out idx_in mod_out row_in").split()
        s = {n: k.sem("r2_" + n) for n in names}
        block = ctx.enter_context(nc.Block())
        tab_v = k.tab_d.rearrange("(j p) a -> p (j a)", p=P)

        @block.sync
        def _(sp):
            sp.dma_start(rw[:, :, :], k.w["router_w"].rearrange("(b p) e -> p b e", p=P)).then_inc(s["small"], 16)
            sp.dma_start(rb[:, :], k.w["router_b"].rearrange("(a e) -> a e", a=1).to_broadcast([P, NE])).then_inc(s["small"], 16)
            with nc.allow_non_contiguous_dma(reason="a vector over partitions"):
                sp.dma_start(k.g2_d.rearrange("(b p) -> p b", p=P), k.mod[:, 0, 5 * DB:6 * DB]).then_inc(s["mod_out"], 16)
            sp.wait_ge(s["consts"], 6)
            with nc.allow_non_contiguous_dma(reason="a small table"):
                sp.dma_start(tab_v, zero_i[:, :]).then_inc(s["zero_out"], 16)
            sp.wait_ge(s["mod_out"], 16)
            sp.dma_start(k.g2_row[:, :], k.g2_d.rearrange("(a n) -> a n", a=1).to_broadcast([P, D])).then_inc(s["row_in"], 16)
            sp.wait_ge(s["kept"], 2 * TL)
            sp.dma_start(k.h2_d.rearrange("(t p) d -> p t d", p=P), h2N[:, :, :]).then_inc(s["h2_out"], 16)
            sp.wait_ge(s["tab_out"], 16 * 2 * TL)
            with nc.allow_non_contiguous_dma(reason="a small table"):
                sp.dma_start(k.idx[:, 0:BLOCKS], tab_v).then_inc(s["idx_in"], 16)
            sp.wait_ge(s["idx_in"], 16)
            sp.wait_ge(s["h2_out"], 16)
            sp.wait_ge(s["row_in"], 16)

        @block.tensor
        def _(pe):
            pe.wait_ge(s["small"], 32)
            for t in range(TL):
                for b in range(DB):
                    mm = pe.matmul(ps[:, 4, t * NE:(t + 1) * NE], k.h2T[:, b, t * P:(t + 1) * P], rw[:, b, :],
                                   start=(b == 0), stop=(b == DB - 1))
            mm.then_inc(s["logits"], 1)
            n = 0
            for src in (k.h2T, k.x1T):
                for t in range(TL):
                    for g in range(2):
                        if n >= 4:
                            pe.wait_ge(s["kept"], n - 3)
                        for j in range(4):
                            mm = pe.transpose(ps[:, n % 4, j * P:(j + 1) * P], src[:, 4 * g + j, t * P:(t + 1) * P],
                                              k.ident[:, :])
                        mm.then_inc(s["turned"], 1)
                        n += 1
            pe.wait_ge(s["chosen"], 2)
            pe.wait_ge(s["consts"], 6)
            for t in range(TL + 1):
                for t2_ in range(min(t + 1, TL)):
                    mm = pe.matmul(ps[:, 5, t * NE:(t + 1) * NE], strict[:, :] if t2_ == t else k.ones[:, :],
                                   both[:, t2_, :], start=(t2_ == 0), stop=(t2_ == min(t, TL - 1)))
            mm.then_inc(s["rank_done"], 1)

        @block.scalar
        def _(act):
            act.wait_ge(s["logits"], 1)
            act.activation(sc[:, :, :], ps[:, 4, 0:TL * NE].rearrange("p (t e) -> p t e", t=TL), ACT.Exp, scale=-1.0)\
               .then_inc(s["e_done"], 1)
            n = 0
            for dst in (h2N, k.x1N):
                for t in range(TL):
                    for g in range(2):
                        act.wait_ge(s["turned"], n + 1)
                        act.activation(dst[:, t, 512 * g:512 * g + 512], ps[:, n % 4, :], ACT.Copy).then_inc(s["kept"], 1)
                        n += 1

        @block.gpsimd
        def _(pool):
            pool.iota(prio[:, :], pattern=[[-1, NE]], base=NE, channel_multiplier=0, allow_small_or_imprecise_dtypes=True)\
                .then_inc(s["consts"], 1)
            pool.iota(gprio[:, :], pattern=[[-1, NG_E]], base=NG_E, channel_multiplier=0,
                      allow_small_or_imprecise_dtypes=True).then_inc(s["consts"], 1)
            pool.iota(blk[:, :], pattern=[[1, BLOCKS]], base=0, channel_multiplier=0, allow_small_or_imprecise_dtypes=True)\
                .then_inc(s["consts"], 1)
            pool.iota(tok[:, :], pattern=[[P, TL]], base=0, channel_multiplier=1).then_inc(s["consts"], 1)
            pool.memset(zero_i[:, :], 0).then_inc(s["consts"], 1)
            pool.memset(k.idx[:, BLOCKS:BLOCKS + 2], 0).then_inc(s["consts"], 1)
            pool.wait_ge(s["consts"], 6)
            pool.wait_ge(s["slots"], 1)
            pool.wait_ge(s["zero_out"], 16)
            for j in range(2):
                for t in range(TL):
                    pool.indirect_dma_start(out=k.tab_d, out_offset=bass.IndirectOffsetOnAxis(ap=k.slot_t[2 * t + j][:, :], axis=0),
                                            in_=tok[:, t:t + 1], in_offset=None).then_inc(s["tab_out"], 16)
            pool.wait_ge(s["tab_out"], 16 * 2 * TL)

        @block.vector
        def _(dve):
            link = Chain(dve, s["dve"])

            def over(ap, n):
                return ap.unsqueeze(1).to_broadcast([P, TL, n])
            dve.wait_ge(s["small"], 32)
            dve.wait_ge(s["consts"], 6)
            dve.tensor_scalar(strict[:, :], k.onward[:, :], -1.0, 1.0, ALU.mult, ALU.add)
            link(dve.memset(ones16[:, :], 1.0))
            dve.wait_ge(s["e_done"], 1)
            link(dve.tensor_scalar(selm[:, :, :], sc[:, :, :], 1.0, None, ALU.add))
            link(dve.reciprocal(sc[:, :, :], selm[:, :, :]))
            link(dve.tensor_tensor(sel[:, :, :], sc[:, :, :], over(rb[:, :], NE), ALU.add))
            v = sel[:, :, :].rearrange("p t (g a) -> p (t g) a", a=EPG)
            hi_, lo_ = (a[:, :, :, :].rearrange("p t g a -> p (t g) a") for a in (hi, lo))
            link(dve.tensor_tensor(hi_, v[:, :, 0:2], v[:, :, 2:4], ALU.max))
            link(dve.tensor_tensor(lo_, v[:, :, 0:2], v[:, :, 2:4], ALU.min))
            gs_, t1_, t2_ = (a[:, :, :].rearrange("p t g -> p (t g)") for a in (gs, t1, t2))
            link(dve.tensor_tensor(gs_, hi_[:, :, 0], hi_[:, :, 1], ALU.max))
            link(dve.tensor_tensor(t1_, hi_[:, :, 0], hi_[:, :, 1], ALU.min))
            link(dve.tensor_tensor(t2_, lo_[:, :, 0], lo_[:, :, 1], ALU.max))
            link(dve.tensor_tensor(t1_, t1_, t2_, ALU.max))
            link(dve.tensor_tensor(gs_, gs_, t1_, ALU.add))

            def first_best(values, prior, n, onehot, scratch):
                link(dve.tensor_reduce(top[:, :], values[:, :, :], AX.X, ALU.max))
                link(dve.tensor_tensor(scratch[:, :, :], values[:, :, :], bc(top[:, :], n), ALU.is_equal))
                link(dve.tensor_tensor(scratch[:, :, :], scratch[:, :, :], over(prior[:, :], n), ALU.mult))
                link(dve.tensor_reduce(top[:, :], scratch[:, :, :], AX.X, ALU.max))
                link(dve.tensor_tensor(onehot[:, :, :], scratch[:, :, :], bc(top[:, :], n), ALU.is_equal))
            first_best(gs, gprio, NG_E, t1, t2)
            link(dve.tensor_copy(both[:, :, :].rearrange("p t (g a) -> p (t g) a", a=EPG), bc(t1_, EPG)))
            link(dve.tensor_scalar(work[:, :, :], both[:, :, :], OUTSIDE, -OUTSIDE, ALU.mult, ALU.add))
            link(dve.tensor_tensor(selm[:, :, :], sel[:, :, :], both[:, :, :], ALU.mult))
            link(dve.tensor_tensor(selm[:, :, :], selm[:, :, :], work[:, :, :], ALU.add))
            first_best(selm, prio, NE, oh[0], work)
            link(dve.tensor_scalar(work[:, :, :], oh[0][:, :, :], -2 * OUTSIDE, None, ALU.mult))
            link(dve.tensor_tensor(selm[:, :, :], selm[:, :, :], work[:, :, :], ALU.add))
            first_best(selm, prio, NE, oh[1], work)
            dve.tensor_tensor(both[:, :, :], oh[0][:, :, :], oh[1][:, :, :], ALU.add).then_inc(s["chosen"], 1)
            for j in range(2):
                link(dve.tensor_tensor(work[:, :, :], sc[:, :, :], oh[j][:, :, :], ALU.mult))
                link(dve.tensor_reduce(k.comb[:, j, :], work[:, :, :], AX.X, ALU.add))
            link(dve.tensor_tensor(ws[:, :], k.comb[:, 0, :], k.comb[:, 1, :], ALU.add))
            link(dve.reciprocal(top[:, :], ws[:, :]))
            for j in range(2):
                ins = dve.tensor_tensor(k.comb[:, j, :], k.comb[:, j, :], top[:, :], ALU.mult)
            ins.then_inc(s["chosen"], 1)
            dve.wait_ge(s["rank_done"], 1)
            link(dve.tensor_copy(rank[:, :, :].rearrange("p t e -> p (t e)"), ps[:, 5, 0:(TL + 1) * NE]))
            cnt = rank[:, TL, :]
            link(dve.tensor_scalar(nb[:, :], cnt, 0.0, None, ALU.is_gt))
            for m in range(1, TL):
                link(dve.tensor_scalar(acc[:, :], cnt, float(P * m), None, ALU.is_gt))
                link(dve.tensor_tensor(nb[:, :], nb[:, :], acc[:, :], ALU.add))
            link(dve.tensor_tensor_scan(end[:, :], ones16[:, :], nb[:, :], 0.0, ALU.mult, ALU.add))
            link(dve.tensor_tensor(acc[:, :], end[:, :], nb[:, :], ALU.subtract))
            link(dve.tensor_scalar(acc[:, :], acc[:, :], float(P), None, ALU.mult))
            link(dve.tensor_tensor(work[:, :, :], rank[:, 0:TL, :], over(acc[:, :], NE), ALU.add))
            for j in range(2):
                link(dve.tensor_tensor(selm[:, :, :], work[:, :, :], oh[j][:, :, :], ALU.mult))
                link(dve.tensor_reduce(slot_f[:, j, :], selm[:, :, :], AX.X, ALU.add))
                for t in range(TL):
                    link(dve.tensor_copy(k.slot_t[2 * t + j][:, :], slot_f[:, j, t:t + 1]))
            dve.tensor_copy(ws[:, 0:1], top[:, 0:1]).then_inc(s["slots"], 1)
            link(dve.tensor_tensor(cmp_[:, :, :], bc(blk[:, :], NE), end[:, :].unsqueeze(1).to_broadcast([P, BLOCKS, NE]),
                                   ALU.is_ge))
            link(dve.tensor_reduce(plan_f[:, 0:BLOCKS], cmp_[:, :, :], AX.X, ALU.add))
            link(dve.tensor_scalar(plan_f[:, 0:BLOCKS], plan_f[:, 0:BLOCKS], float(NE - 1), None, ALU.min))
            link(dve.tensor_scalar(cmp_[:, 0, 0:PAIRS], blk[:, 0:BLOCKS:2], end[:, NE - 1:NE], None, ALU.is_lt))
            link(dve.tensor_reduce(plan_f[:, BLOCKS:BLOCKS + 1], cmp_[:, 0, 0:PAIRS], AX.X, ALU.add))
            link(dve.tensor_copy(k.plan[:, :], plan_f[:, :]))


OUTSIDE = 1e4


def experts(nc, k):
    ctx = ExitStack()
    with ctx:
        def sb(name, shape, dt=F32):
            return ctx.enter_context(nc.sbuf_tensor(name, shape, dt))
        wg = [sb(f"wg{s}", [P, DB, DE]) for s in range(2)]
        wu = [sb(f"wu{s}", [P, DB, DE]) for s in range(2)]
        wd = [sb(f"wd{s}", [P, EB, D]) for s in range(2)]
        ids = [sb(f"ids{s}", [P, 1], I32) for s in range(2)]
        xg = [sb(f"xg{s}", [P, D]) for s in range(2)]
        xgT = [sb(f"xgT{s}", [P, DB, P]) for s in range(2)]
        th = [sb(f"th{s}", [P, DE]) for s in range(2)]
        hid = [sb(f"hid{s}", [P, DE]) for s in range(2)]
        hidT = [sb(f"hidT{s}", [P, EB, P]) for s in range(2)]
        yr = [sb(f"yr{s}", [P, D]) for s in range(2)]
        ps = k.ps
        names = "g_in u_in d_in id_done x_in x_turned x_kept g_ready u_ready th_done hid_half hid_u hid_done h_turned h_kept y_ready y_kept y_out".split()
        s = {n: [k.sem(f"e_{n}{j}") for j in range(2)] for n in names}
        block = ctx.enter_context(nc.Block())

        def pairs(eng):
            n = eng.value_load(k.plan[0:1, BLOCKS:BLOCKS + 1], min_val=FEWEST // 2, max_val=PAIRS)
            yield 0, n
            with eng.Fori(1, n) as i:
                yield i, n

        @block.sync
        def _(sp):
            for i, n in pairs(sp):
                for j in range(2):
                    e = sp.value_load(k.plan[0:1, bass.ds(2 * i + j, 1)], min_val=0, max_val=NE - 1)
                    for w, src, used, came in ((wg, "exp_w_gate", "g_ready", "g_in"), (wu, "exp_w_up", "u_ready", "u_in"),
                                               (wd, "exp_w_down", "y_ready", "d_in")):
                        wait(sp, s[used][j], i)
                        sp.dma_start(w[j][:, :, :], k.w[src][0][bass.ds(e, 1)].rearrange("a (b p) n -> p (a b) n", p=P))\
                            .then_inc(s[came][j], 16)

        @block.gpsimd
        def _(pool):
            def gather(i, j):
                pool.wait_ge(s["id_done"][j], i + 1)
                pool.nop(nofuse=True)
                pool.indirect_dma_start(out=xg[j][:, :], out_offset=None, in_=k.h2_d,
                                        in_offset=bass.IndirectOffsetOnAxis(ap=ids[j][:, :], axis=0))\
                    .then_inc(s["x_in"][j], 16)
            gather(0, 0)
            gather(0, 1)
            for i, n in pairs(pool):
                gather(i + 1, 0)
                gather(i + 1, 1)
            for j in range(2):
                pool.wait_ge(s["x_in"][j], 16 * n + 16)
            pool.nop(nofuse=True)

        @block.tensor
        def _(pe):
            def turn_x(i, j):
                pe.wait_ge(s["x_in"][j], 16 * i + 16)
                for h in range(2):
                    for c in range(4):
                        mm = pe.transpose(ps[:, 4 * j + h, c * P:(c + 1) * P], xg[j][:, (4 * h + c) * P:(4 * h + c + 1) * P],
                                          k.ident[:, :])
                mm.then_inc(s["x_turned"][j], 1)

            def product(w, j, bank, first, last):
                for b in range(first, last):
                    mm = pe.matmul(ps[:, 4 * j + bank, :], xgT[j][:, b, :], w[j][:, b, :], start=(b == 0), stop=(b == DB - 1))
                return mm

            def gate(i, j, between=None):
                wait(pe, s["y_kept"][j], i)
                pe.wait_ge(s["g_in"][j], 16 * i + 16)
                pe.wait_ge(s["x_kept"][j], i + 1)
                product(wg, j, 2, 0, DB // 2)
                if between:
                    between()
                product(wg, j, 2, DB // 2, DB).then_inc(s["g_ready"][j], 1)

            def up(i, j):
                pe.wait_ge(s["u_in"][j], 16 * i + 16)
                product(wu, j, 3, 0, DB).then_inc(s["u_ready"][j], 1)

            def turn_hidden(c1, j):
                pe.wait_ge(s["hid_done"][j], c1)
                for c in range(EB):
                    mm = pe.transpose(ps[:, 4 * j, c * P:(c + 1) * P], hid[j][:, c * P:(c + 1) * P], k.ident[:, :])
                mm.then_inc(s["h_turned"][j], 1)

            def down(c1, j):
                pe.wait_ge(s["d_in"][j], 16 * c1)
                pe.wait_ge(s["h_kept"][j], c1)
                for h in range(2):
                    for b in range(EB):
                        mm = pe.matmul(ps[:, 4 * j + 2 + h, :], hidT[j][:, b, :], wd[j][:, b, 512 * h:512 * h + 512],
                                       start=(b == 0), stop=(b == EB - 1))
                mm.then_inc(s["y_ready"][j], 1)
            for i, n in pairs(pe):
                started = not (isinstance(i, int) and i == 0)
                turn_x(i, 0)
                if started:
                    turn_hidden(i, 1)
                gate(i, 0)
                if started:
                    down(i, 1)
                turn_x(i, 1)
                up(i, 0)
                gate(i, 1, between=lambda: turn_hidden(i + 1, 0))
                down(i + 1, 0)
                up(i, 1)
            turn_hidden(n, 1)
            down(n, 1)

        @block.scalar
        def _(act):
            def keep_x(i, j):
                act.wait_ge(s["x_turned"][j], i + 1)
                for h in range(2):
                    ins = act.activation(xgT[j][:, 4 * h:4 * h + 4, :].rearrange("p b c -> p (b c)"), ps[:, 4 * j + h, :],
                                         ACT.Copy)
                ins.then_inc(s["x_kept"][j], 1)

            def squash(i, j):
                act.wait_ge(s["g_ready"][j], i + 1)
                act.activation(th[j][:, :], ps[:, 4 * j + 2, :], ACT.Tanh, scale=0.5).then_inc(s["th_done"][j], 1)

            def keep_hidden(c1, j):
                act.wait_ge(s["h_turned"][j], c1)
                act.activation(hidT[j][:, :, :].rearrange("p b c -> p (b c)"), ps[:, 4 * j, :], ACT.Copy)\
                   .then_inc(s["h_kept"][j], 1)

            def keep_y(c1, j):
                act.wait_ge(s["y_ready"][j], c1)
                for h in range(2):
                    ins = act.activation(yr[j][:, 512 * h:512 * h + 512], ps[:, 4 * j + 2 + h, :], ACT.Copy)
                ins.then_inc(s["y_kept"][j], 1)
                act.wait_ge(s["y_kept"][j], c1)
                act.dma_start(k.ys_d[bass.ds((2 * c1 - 2 + j) * P, P), :], yr[j][:, :]).then_inc(s["y_out"][j], 16)
            for i, n in pairs(act):
                started = not (isinstance(i, int) and i == 0)
                keep_x(i, 0)
                if started:
                    keep_hidden(i, 1)
                squash(i, 0)
                if started:
                    keep_y(i, 1)
                keep_x(i, 1)
                keep_hidden(i + 1, 0)
                squash(i, 1)
                for j in range(2):
                    wait(act, s["y_out"][j], 16 * i)
                keep_y(i + 1, 0)
            keep_hidden(n, 1)
            keep_y(n, 1)
            for j in range(2):
                act.wait_ge(s["y_out"][j], 16 * n)
            act.nop(nofuse=True)

        @block.vector
        def _(dve):
            def numbers(i, j):
                dve.tensor_copy(ids[j][:, :], k.idx[:, bass.ds(2 * i + j, 1)]).then_inc(s["id_done"][j], 1)

            def half(i, j):
                dve.wait_ge(s["th_done"][j], i + 1)
                dve.scalar_tensor_tensor(th[j][:, :], th[j][:, :], 1.0, ps[:, 4 * j + 2, :], ALU.add, ALU.mult)\
                   .then_inc(s["hid_half"][j], 1)

            def whole(i, j):
                dve.wait_ge(s["hid_half"][j], i + 1)
                dve.wait_ge(s["u_ready"][j], i + 1)
                dve.scalar_tensor_tensor(hid[j][:, :], th[j][:, :], 0.5, ps[:, 4 * j + 3, :], ALU.mult, ALU.mult)\
                   .then_inc(s["hid_done"][j], 1)
            numbers(0, 0)
            numbers(0, 1)
            for i, n in pairs(dve):
                dve.wait_ge(s["x_turned"][0], i + 1)
                numbers(i + 1, 0)
                half(i, 0)
                dve.wait_ge(s["x_turned"][1], i + 1)
                numbers(i + 1, 1)
                whole(i, 0)
                half(i, 1)
                whole(i, 1)


def finish(nc, k):
    ctx = ExitStack()
    with ctx:
        def sb(name, shape, dt=F32):
            return ctx.enter_context(nc.sbuf_tensor(name, shape, dt))
        y = [[sb(f"y{j}_{t}", [P, D]) for t in range(TL)] for j in range(2)]
        fg = sb("final_row", [P, D])
        ss, inv = sb("ss", [P, TL]), sb("inv", [P, TL])
        sq = sb("fin_sq", [P, D])
        y_in = [k.sem(f"f_y{n}") for n in range(2 * TL)]
        names = "row_in part mixed x2 sq_done ms rooted dve done out".split()
        s = {n: k.sem("f_" + n) for n in names}
        block = ctx.enter_context(nc.Block())

        @block.sync
        def _(sp):
            sp.dma_start(fg[:, :], k.w["final_g"].rearrange("(a n) -> a n", a=1).to_broadcast([P, D])).then_inc(s["row_in"], 16)
            for t in range(TL):
                sp.wait_ge(s["done"], t + 1)
                sp.dma_start(k.out[0, t * P:(t + 1) * P, :], y[0][t][:, :]).then_inc(s["out"], 16)
            sp.wait_ge(s["out"], 16 * TL)

        @block.gpsimd
        def _(pool):
            for t in range(TL):
                for j in range(2):
                    pool.indirect_dma_start(out=y[j][t][:, :], out_offset=None, in_=k.ys_d,
                                            in_offset=bass.IndirectOffsetOnAxis(ap=k.slot_t[2 * t + j][:, :], axis=0))\
                        .then_inc(y_in[2 * t + j], 16)

        @block.scalar
        def _(act):
            for t in range(TL + 1):
                if t < TL:
                    act.wait_ge(y_in[2 * t], 16)
                    act.activation(y[0][t][:, :], y[0][t][:, :], ACT.Copy, scale=k.comb[:, 0, t:t + 1]).then_inc(s["part"], 1)
                if t:
                    act.wait_ge(s["x2"], t)
                    if t > 1:
                        act.wait_ge(s["sq_done"], t - 1)
                    act.activation(sq[:, :], y[1][t - 1][:, :], ACT.Square, accum_out=ss[:, t - 1:t])\
                       .then_inc(s["sq_done"], 1)
            act.wait_ge(s["ms"], 1)
            act.activation(inv[:, :], inv[:, :], ACT.Sqrt).then_inc(s["rooted"], 1)

        @block.vector
        def _(dve):
            link = Chain(dve, s["dve"])
            dve.wait_ge(s["row_in"], 16)
            for t in range(TL):
                dve.wait_ge(s["part"], t + 1)
                dve.wait_ge(y_in[2 * t + 1], 16)
                a, b = y[0][t][:, :], y[1][t][:, :]
                link(dve.scalar_tensor_tensor(b, b, k.comb[:, 1, t:t + 1], a, ALU.mult, ALU.add))
                link(dve.tensor_tensor(b, b, k.g2_row[:, :], ALU.mult))
                dve.tensor_tensor(b, b, k.x1N[:, t, :], ALU.add).then_inc(s["x2"], 1)
            dve.wait_ge(s["sq_done"], TL)
            dve.tensor_scalar(inv[:, :], ss[:, :], 1.0 / D, EPS, ALU.mult, ALU.add).then_inc(s["ms"], 1)
            dve.wait_ge(s["rooted"], 1)
            link(dve.reciprocal(ss[:, :], inv[:, :]))
            for t in range(TL):
                dve.scalar_tensor_tensor(y[0][t][:, :], y[1][t][:, :], ss[:, t:t + 1], fg[:, :], ALU.mult, ALU.mult)\
                   .then_inc(s["done"], 1)


def merge_and_moe(nc, k):
    with ExitStack() as c1:
        def sb(name, shape, dt=F32):
            return c1.enter_context(nc.sbuf_tensor(name, shape, dt))
        k.x1N = sb("x1_rows", [P, TL, D])
        k.g2_row = sb("g2_row", [P, D])
        k.comb = sb("comb", [P, 2, TL])
        k.slot_t = [sb(f"slot{n}", [P, 1], I32) for n in range(2 * TL)]
        k.idx = sb("slot_tokens", [P, BLOCKS + 2], I32)
        k.plan = sb("plan", [P, BLOCKS + 1], I32)
        with ExitStack() as c2:
            k.x1T, k.h2T = (c2.enter_context(nc.sbuf_tensor(n, [P, DB, SEQ], F32)) for n in ("x1T", "h2T"))
            with ExitStack() as c3:
                def sb3(name, shape):
                    return c3.enter_context(nc.sbuf_tensor(name, shape, F32))
                k.bT, k.aT = sb3("bT", [P, 4, SEQ]), sb3("aT_in", [P, 4, SEQ])
                k.merge_w = [sb3(f"merge_w{j}", [P, 4, D]) for j in range(2)]
                k.wo = sb3("wo", [P, DB, D])
                k.gate = [sb3(f"gate_in{j}", [P, DB, SEQ]) for j in range(2)]
                k.merge_in, k.wo_in = (nc.alloc_semaphore(name=n) for n in ("merge_in", "wo_in"))
                phase(nc, k, rwkv_readout, give_back=False)
                phase(nc, k, merge)
            phase(nc, k, route)
        phase(nc, k, experts)
        phase(nc, k, finish, give_back=False)


def build(nc, ins, out):
    k = Core()
    k.w = ins
    ctx = ExitStack()
    with ctx:
        def dram(name, shape, dt=F32):
            return nc.dram_tensor(name, shape, dt, kind="Internal").ap()

        def sb(name, shape, dt=F32):
            return ctx.enter_context(nc.sbuf_tensor(name, shape, dt))
        k.out = out
        k.ps = ctx.enter_context(nc.psum_tensor("ps", [P, 8, 512], F32))
        k.xT_d = dram("xT_d", [D, SEQ])
        k.rw_d = dram("rw_d", [NRW, P, T])
        k.gt_d = dram("gt_d", [16, P, SEQ])
        k.aT_d = dram("aT_d", [4, P, SEQ])
        k.kk_d = dram("kk_d", [4, P, T])
        k.y_d = dram("y_d", [4, P, SEQ])
        k.bonus_d = dram("bonus_d", [4, P, SEQ])
        k.h2_d = dram("h2_d", [SEQ, D])
        k.ys_d = dram("ys_d", [SLOTS, D])
        k.tab_d = dram("tab_d", [SLOTS, 1], I32)
        k.g2_d = dram("g2_d", [D])
        k.ident, k.ones = sb("ident", [P, P]), sb("ones", [P, P])
        k.mod = sb("mod", [P, 2, 48])
        k.upto, k.onward = sb("upto", [P, P]), sb("onward", [P, P])
        k.neg_upto, k.neg_onward = sb("neg_upto", [P, P]), sb("neg_onward", [P, P])
        phase(nc, k, constants, give_back=False)
        phase(nc, k, masks, give_back=False)
        with ExitStack() as c4:
            def sb4(name, shape):
                return c4.enter_context(nc.sbuf_tensor(name, shape, F32))
            k.same_head = sb4("same_head", [P, P])
            k.cut = sb4("cut", [P, 2, 2, C])
            k.join = sb4("join", [P, 2, 6, P])
            k.reset = sb4("reset", [P, NC, C])
            with ExitStack() as c2:
                def sb2(name, shape):
                    return c2.enter_context(nc.sbuf_tensor(name, shape, F32))
                k.conv = sb2("conv", [P, 4, T])
                k.v_ml = sb2("v_ml", [P, TT, ML_H, DV + 1])
                k.o_ml = sb2("o_ml", [P, TL, 512])
                k.g_ml = sb2("g_ml", [P, TT, 16])
                with ExitStack() as c3:
                    k.hT = c3.enter_context(nc.sbuf_tensor("hT", [P, DB, T], F32))
                    phase(nc, k, modulate)
                    phase(nc, k, project)
                phase(nc, k, mlstm)
            phase(nc, k, rwkv)
        merge_and_moe(nc, k)


_INS = ["x", "c", "ctx", "c_ctx", "w_ada", "b_ada", "norm1_g", "norm2_g", "w_in", "ml_conv_k", "ml_conv_b",
        "ml_gate_b", "ml_norm_g", "rw_mu", "rw_w_up", "rw_w0", "rw_a_up", "rw_a0", "rw_g_up", "rw_k_k", "rw_k_a",
        "rw_r_k", "rw_ln_w", "rw_ln_b", "merge_pa", "merge_pb", "w_out", "router_w", "router_b", "exp_w_gate",
        "exp_w_up", "exp_w_down", "final_g"]


def kernel(**inputs):
    import numpy as _np
    import concourse.bacc as _bacc
    from concourse import mybir as _mybir
    from concourse.bass_utils import run_bass_kernel_spmd as _run

    nc = _bacc.Bacc("TRN2", target_bir_lowering=False, num_devices=1)
    arrays, aps = {}, {}
    for name in _INS:
        a = _np.ascontiguousarray(inputs[name])
        arrays[f"in_{name}"] = a
        aps[name] = nc.dram_tensor(f"in_{name}", a.shape, _mybir.dt.from_np(a.dtype), kind="ExternalInput").ap()
    out = nc.dram_tensor("out_latent", (1, SEQ, D), F32, kind="ExternalOutput").ap()
    build(nc, aps, out)
    r = _run(nc, [arrays], core_ids=[0])
    return r.results[0]["out_latent"]
```
